# Optimizing a Trainium2 kernel written in Bass

```python
import math
import jax, jax.numpy as jnp
from jax import lax
import numpy as np

D_MODEL = 1024
BATCH = 1
SEQ = 256
DEPTH = 2

N_MIXERS = 2
N_HEADS = 8
HEAD_DIM = D_MODEL // N_HEADS
ATTN_WIDTH = N_HEADS * HEAD_DIM
BLOCK = 256
TOPK_BLOCKS = 3
QUERY_CHUNK = 32
CONV_WIDTH = 3
D_FF = int(math.ceil((8 * D_MODEL / 3) / 256) * 256)
N_ATTN_LAYERS = (DEPTH + 1) // 2
N_CONV_LAYERS = DEPTH // 2
EPS = 1e-6


def rms_norm(x, gain):
    xf = x.astype(jnp.float32)
    y = xf * lax.rsqrt(jnp.mean(xf * xf, axis=-1, keepdims=True) + EPS)
    return (y * gain.astype(jnp.float32)).astype(x.dtype)

def modulate(x, gain, shift, scale):
    return rms_norm(x, gain) * (1 + scale[:, None, :]) + shift[:, None, :]

def moba_attention(h, w_qkv, w_o, q_gain, k_gain):
    B, S, _ = h.shape
    qkv = (h @ w_qkv).reshape(B, S, 3, N_HEADS, HEAD_DIM).transpose(2, 0, 3, 1, 4)
    q = rms_norm(qkv[0], q_gain) * (HEAD_DIM ** -0.5)
    k = rms_norm(qkv[1], k_gain)
    v = qkv[2]
    n_blocks = -(-S // BLOCK)
    pad = n_blocks * BLOCK - S
    kp = jnp.pad(k, ((0, 0), (0, 0), (0, pad), (0, 0)))
    vp = jnp.pad(v, ((0, 0), (0, 0), (0, pad), (0, 0)))
    k_blocks = kp.reshape(B, N_HEADS, n_blocks, BLOCK, HEAD_DIM)
    v_blocks = vp.reshape(B, N_HEADS, n_blocks, BLOCK, HEAD_DIM)
    k_mean = jnp.mean(k_blocks.astype(jnp.float32), axis=3).astype(k.dtype)
    n_sel = min(TOPK_BLOCKS, n_blocks)
    bi = jnp.arange(B)[:, None, None, None]
    hi = jnp.arange(N_HEADS)[None, :, None, None]
    blk_ids = jnp.arange(n_blocks)

    def chunk(ci):
        q0 = ci * QUERY_CHUNK
        nb = q0 // BLOCK
        qc = lax.dynamic_slice_in_dim(q, q0, QUERY_CHUNK, axis=2)
        k_own = lax.dynamic_slice_in_dim(kp, nb * BLOCK, BLOCK, axis=2)
        v_own = lax.dynamic_slice_in_dim(vp, nb * BLOCK, BLOCK, axis=2)
        route = jnp.einsum('bhqd,bhnd->bhqn', qc, k_mean).astype(jnp.float32)
        route = jnp.where(blk_ids < nb, route, -jnp.inf)
        _, idx = lax.top_k(route, n_sel)
        k_sel = k_blocks[bi, hi, idx]
        v_sel = v_blocks[bi, hi, idx]
        qpos = q0 + jnp.arange(QUERY_CHUNK)
        kpos = nb * BLOCK + jnp.arange(BLOCK)
        s_own = jnp.einsum('bhqd,bhkd->bhqk', qc, k_own).astype(jnp.float32)
        s_own = jnp.where(kpos[None, :] <= qpos[:, None], s_own, -jnp.inf)
        s_sel = jnp.einsum('bhqd,bhqjkd->bhqjk', qc, k_sel).astype(jnp.float32)
        slot_ok = jnp.arange(n_sel) < nb
        s_sel = jnp.where(slot_ok[:, None], s_sel, -jnp.inf)
        s_sel = s_sel.reshape(B, N_HEADS, QUERY_CHUNK, n_sel * BLOCK)
        p = jax.nn.softmax(jnp.concatenate([s_own, s_sel], axis=-1), axis=-1).astype(v.dtype)
        p_own = p[..., :BLOCK]
        p_sel = p[..., BLOCK:].reshape(B, N_HEADS, QUERY_CHUNK, n_sel, BLOCK)
        return (jnp.einsum('bhqk,bhkd->bhqd', p_own, v_own)
                + jnp.einsum('bhqjk,bhqjkd->bhqd', p_sel, v_sel))

    o = lax.map(chunk, jnp.arange(S // QUERY_CHUNK))
    o = o.transpose(1, 0, 3, 2, 4).reshape(B, S, ATTN_WIDTH)
    return o @ w_o

def short_conv(h, w_in, conv_w, w_out):
    S = h.shape[1]
    b_gate, c_gate, u = jnp.split(h @ w_in, 3, axis=-1)
    u = c_gate * u
    up = jnp.pad(u, ((0, 0), (CONV_WIDTH - 1, 0), (0, 0)))
    y = sum(conv_w[j] * up[:, j:j + S] for j in range(CONV_WIDTH))
    return (b_gate * y) @ w_out

def swiglu(h, w_gate_up, w_down):
    g, u = jnp.split(h @ w_gate_up, 2, axis=-1)
    return (jax.nn.silu(g) * u) @ w_down

def first_inputs(seed: int = 0) -> dict:
    key = jax.random.key(seed)
    ks = jax.random.split(key, 16)
    f32 = jnp.float32
    nrm = lambda k, shape, s: (jax.random.normal(k, shape, f32) * s)
    return {
        "x": nrm(ks[0], (BATCH, SEQ, D_MODEL), 1.0),
        "c": nrm(ks[1], (BATCH, D_MODEL), 1.0),
        "w_ada": nrm(ks[2], (DEPTH, D_MODEL, 6 * D_MODEL), 0.5 * D_MODEL ** -0.5),
        "b_ada": nrm(ks[3], (DEPTH, 6 * D_MODEL), 0.02),
        "norm_mix": 1.0 + nrm(ks[4], (DEPTH, D_MODEL), 0.02),
        "norm_ffn": 1.0 + nrm(ks[5], (DEPTH, D_MODEL), 0.02),
        "w_qkv": nrm(ks[6], (N_ATTN_LAYERS, D_MODEL, 3 * ATTN_WIDTH), D_MODEL ** -0.5),
        "w_o": nrm(ks[7], (N_ATTN_LAYERS, ATTN_WIDTH, D_MODEL), ATTN_WIDTH ** -0.5),
        "q_gain": 1.0 + nrm(ks[8], (N_ATTN_LAYERS, HEAD_DIM), 0.02),
        "k_gain": 1.0 + nrm(ks[9], (N_ATTN_LAYERS, HEAD_DIM), 0.02),
        "w_in": nrm(ks[10], (N_CONV_LAYERS, D_MODEL, 3 * D_MODEL), D_MODEL ** -0.5),
        "conv_w": nrm(ks[11], (N_CONV_LAYERS, CONV_WIDTH, D_MODEL), CONV_WIDTH ** -0.5),
        "w_out": nrm(ks[12], (N_CONV_LAYERS, D_MODEL, D_MODEL), D_MODEL ** -0.5),
        "w_gate_up": nrm(ks[13], (DEPTH, D_MODEL, 2 * D_FF), D_MODEL ** -0.5),
        "w_down": nrm(ks[14], (DEPTH, D_FF, D_MODEL), D_FF ** -0.5),
    }

def first_block(x, c, w_ada, b_ada, norm_mix, norm_ffn, w_qkv, w_o, q_gain, k_gain,
              w_in, conv_w, w_out, w_gate_up, w_down):
    sc = jax.nn.silu(c)
    for i in range(DEPTH):
        mod = sc @ w_ada[i] + b_ada[i]
        sh_m, sc_m, g_m, sh_f, sc_f, g_f = jnp.split(mod, 6, axis=-1)
        h = modulate(x, norm_mix[i], sh_m, sc_m)
        j = i // N_MIXERS
        if i % N_MIXERS == 0:
            y = moba_attention(h, w_qkv[j], w_o[j], q_gain[j], k_gain[j])
        else:
            y = short_conv(h, w_in[j], conv_w[j], w_out[j])
        x = x + g_m[:, None, :] * y
        h = modulate(x, norm_ffn[i], sh_f, sc_f)
        x = x + g_f[:, None, :] * swiglu(h, w_gate_up[i], w_down[i])
    return x


N_A_LAYERS = DEPTH // 2
N_B_LAYERS = DEPTH - N_A_LAYERS
MIX_W = D_MODEL
MEM_LEN = 256
MEM_HEADS = 4
MEM_HEAD_DIM = 64
MEM_W = MEM_HEADS * MEM_HEAD_DIM
SEQ_MIX_W = MIX_W - MEM_W
HGRN_EXPAND = 128
HGRN_HEADS = SEQ_MIX_W // HGRN_EXPAND
HGRN_DK = HGRN_EXPAND
HGRN_DV = SEQ_MIX_W // HGRN_HEADS
HGRN_CHUNK = 64
SB_HEAD_DIM = 64
SB_HEADS = SEQ_MIX_W // SB_HEAD_DIM
SB_BLOCK = 128
A_IN_W = 4 * SEQ_MIX_W + MEM_W
B_IN_W = SEQ_MIX_W + MEM_W
N_GROUPS = 4
EXPERTS_PER_GROUP = 4
N_EXPERTS = N_GROUPS * EXPERTS_PER_GROUP
TOP_K_IN_GROUP = 2
D_EXPERT = 256
DEEPNORM_ALPHA = (2 * DEPTH) ** 0.25
DEEPNORM_BETA = (8 * DEPTH) ** -0.25
LN_EPS = 1e-5
RMS_EPS = 1e-6


def layer_norm(x, g, b):
    xf = x.astype(jnp.float32)
    mu = jnp.mean(xf, axis=-1, keepdims=True)
    var = jnp.mean(jnp.square(xf - mu), axis=-1, keepdims=True)
    y = (xf - mu) * lax.rsqrt(var + LN_EPS) * g.astype(jnp.float32) + b.astype(jnp.float32)
    return y.astype(x.dtype)

def post_norm(x, y, g, b):
    return layer_norm(DEEPNORM_ALPHA * x + y.astype(x.dtype), g, b)

def gla_chunkwise(q, k, v, logf):
    B, S, H, dk = q.shape
    dv = v.shape[-1]
    nc = S // HGRN_CHUNK

    def to_chunks(t):
        return t.reshape(B, nc, HGRN_CHUNK, H, t.shape[-1]).transpose(1, 0, 3, 2, 4)

    qc, kc, vc = to_chunks(q), to_chunks(k), to_chunks(v)
    G = jnp.cumsum(to_chunks(logf), axis=3)
    incl = jnp.tril(jnp.ones((HGRN_CHUNK, HGRN_CHUNK), dtype=bool))

    def step(state, inp):
        q_, k_, v_, G_ = inp
        diff = G_[:, :, :, None, :] - G_[:, :, None, :, :]
        decay = jnp.exp(jnp.where(incl[:, :, None], diff, -jnp.inf))
        scores = jnp.einsum('bhtd,bhsd,bhtsd->bhts', q_, k_, decay)
        out = (jnp.einsum('bhts,bhse->bhte', scores, v_)
               + jnp.einsum('bhtd,bhde->bhte', q_ * jnp.exp(G_), state))
        g_last = G_[:, :, -1]
        state = (jnp.exp(g_last)[..., None] * state
                 + jnp.einsum('bhsd,bhse->bhde', k_ * jnp.exp(g_last[:, :, None] - G_), v_))
        return state, out

    s0 = jnp.zeros((B, H, dk, dv), jnp.float32)
    _, out = lax.scan(step, s0, (qc, kc, vc, G))
    return out.transpose(1, 0, 3, 2, 4).reshape(B, S, H, dv)

def hgrn2_mix(q, f_raw, i_in, g, lb, gnorm):
    B, S, _ = q.shape
    qh = (jax.nn.silu(q.astype(jnp.float32)) * HGRN_DK ** -0.5).reshape(B, S, HGRN_HEADS, HGRN_DK)
    lbf = lb.astype(jnp.float32)
    logf = jnp.logaddexp(jnp.log(lbf), jnp.log1p(-lbf) + jax.nn.log_sigmoid(f_raw.astype(jnp.float32)))
    logf = logf.reshape(B, S, HGRN_HEADS, HGRN_DK)
    kh = -jnp.expm1(logf)
    vh = i_in.astype(jnp.float32).reshape(B, S, HGRN_HEADS, HGRN_DV)
    o = gla_chunkwise(qh, kh, vh, logf)
    o = o * lax.rsqrt(jnp.mean(jnp.square(o), axis=-1, keepdims=True) + RMS_EPS)
    o = o * gnorm.astype(jnp.float32).reshape(HGRN_HEADS, HGRN_DV)
    o = o.reshape(B, S, SEQ_MIX_W) * jax.nn.silu(g.astype(jnp.float32))
    return o

def stick_breaking_attention(q, k, v):
    B, S, _ = q.shape
    qh = q.astype(jnp.float32).reshape(B, S, SB_HEADS, SB_HEAD_DIM).transpose(0, 2, 1, 3)
    scale = 1.0 / math.sqrt(SB_HEAD_DIM)
    outs = []
    for blk in range(S // SB_BLOCK):
        start, end = blk * SB_BLOCK, (blk + 1) * SB_BLOCK
        qb = qh[:, :, start:end]
        kb, vb = k[:, :, :end], v[:, :, :end]
        z = jnp.einsum('bhtd,bhsd->bhts', qb, kb) * scale
        t_pos = start + jnp.arange(SB_BLOCK)
        s_pos = jnp.arange(end)
        mask = s_pos[None, :] < t_pos[:, None]
        neg_log_1m_beta = jnp.where(mask, jax.nn.softplus(z), 0.0)
        rest = lax.cumsum(neg_log_1m_beta, axis=3, reverse=True) - neg_log_1m_beta
        log_a = jax.nn.log_sigmoid(z) - rest
        a = jnp.where(mask, jnp.exp(log_a), 0.0)
        outs.append(jnp.einsum('bhts,bhsd->bhtd', a, vb))
    o = jnp.concatenate(outs, axis=2)
    return o.transpose(0, 2, 1, 3).reshape(B, S, SEQ_MIX_W)

def memory_attention(qm, mem_k, mem_v):
    B, S, _ = qm.shape
    qh = qm.astype(jnp.float32).reshape(B, S, MEM_HEADS, MEM_HEAD_DIM)
    scores = jnp.einsum('bthd,bmhd->bhtm', qh, mem_k.astype(jnp.float32)) / math.sqrt(MEM_HEAD_DIM)
    p = jax.nn.softmax(scores, axis=-1)
    o = jnp.einsum('bhtm,bmhd->bthd', p, mem_v.astype(jnp.float32))
    return o.reshape(B, S, MEM_W)

def hier_moe(x, w_group, b_group, w_router, b_router, w_gate, w_up, w_down):
    B, S, D = x.shape
    xf = x.reshape(B * S, D)
    T = xf.shape[0]
    probs_g = jax.nn.softmax((xf @ w_group + b_group).astype(jnp.float32), axis=-1)
    p_top, g_idx = lax.top_k(probs_g, 1)
    logits_e = (xf @ w_router + b_router).astype(jnp.float32).reshape(T, N_GROUPS, EXPERTS_PER_GROUP)
    in_group = jnp.take_along_axis(logits_e, g_idx[:, :, None], axis=1)[:, 0]
    probs_in = jax.nn.softmax(in_group, axis=-1)
    w_top, e_local = lax.top_k(probs_in, TOP_K_IN_GROUP)
    w_top = w_top / jnp.sum(w_top, axis=-1, keepdims=True)
    ids = g_idx * EXPERTS_PER_GROUP + e_local
    gates = jnp.einsum('tk,tke->te', p_top * w_top, jax.nn.one_hot(ids, N_EXPERTS, dtype=jnp.float32))
    h = jax.nn.silu(jnp.einsum('td,edf->tef', xf, w_gate)) * jnp.einsum('td,edf->tef', xf, w_up)
    y = jnp.einsum('tef,efd->td', h * gates[:, :, None].astype(h.dtype), w_down)
    return y.reshape(B, S, D)

def second_inputs(seed: int = 0) -> dict:
    key = jax.random.key(seed)
    ks = iter(jax.random.split(key, 40))

    def nrm(shape, scale):
        return jax.random.normal(next(ks), shape, jnp.float32) * scale

    d_s = D_MODEL ** -0.5
    x = nrm((BATCH, SEQ, D_MODEL), 1.0)
    mem = nrm((BATCH, MEM_LEN, D_MODEL), 1.0)
    a_w_in = jnp.concatenate([
        nrm((N_A_LAYERS, D_MODEL, SEQ_MIX_W), d_s),
        nrm((N_A_LAYERS, D_MODEL, SEQ_MIX_W), d_s),
        nrm((N_A_LAYERS, D_MODEL, SEQ_MIX_W), d_s * DEEPNORM_BETA),
        nrm((N_A_LAYERS, D_MODEL, SEQ_MIX_W), d_s),
        nrm((N_A_LAYERS, D_MODEL, MEM_W), d_s),
    ], axis=-1)
    a_lower_bounds = nrm((N_A_LAYERS, SEQ_MIX_W), 0.1)
    a_gnorm = 1.0 + nrm((N_A_LAYERS, SEQ_MIX_W), 0.02)
    b_w_in = nrm((N_B_LAYERS, D_MODEL, B_IN_W), d_s)
    w_kv_shared = jnp.concatenate([nrm((D_MODEL, SEQ_MIX_W), d_s),
                                   nrm((D_MODEL, SEQ_MIX_W), d_s * DEEPNORM_BETA)], axis=-1)
    w_mem_kv = jnp.concatenate([nrm((DEPTH, D_MODEL, MEM_W), d_s),
                                nrm((DEPTH, D_MODEL, MEM_W), d_s * DEEPNORM_BETA)], axis=-1)
    w_o = nrm((DEPTH, MIX_W, D_MODEL), MIX_W ** -0.5 * DEEPNORM_BETA)
    ln_mix_g = 1.0 + nrm((DEPTH, D_MODEL), 0.02)
    ln_mix_b = nrm((DEPTH, D_MODEL), 0.02)
    ln_ffn_g = 1.0 + nrm((DEPTH, D_MODEL), 0.02)
    ln_ffn_b = nrm((DEPTH, D_MODEL), 0.02)
    w_group = nrm((DEPTH, D_MODEL, N_GROUPS), d_s)
    b_group = nrm((DEPTH, N_GROUPS), 0.01)
    w_router = nrm((DEPTH, D_MODEL, N_EXPERTS), d_s)
    b_router = nrm((DEPTH, N_EXPERTS), 0.01)
    w_gate = nrm((DEPTH, N_EXPERTS, D_MODEL, D_EXPERT), d_s)
    w_up = nrm((DEPTH, N_EXPERTS, D_MODEL, D_EXPERT), d_s)
    w_down = nrm((DEPTH, N_EXPERTS, D_EXPERT, D_MODEL), D_EXPERT ** -0.5 * DEEPNORM_BETA)
    return {"x": x, "mem": mem, "a_w_in": a_w_in, "a_lower_bounds": a_lower_bounds,
            "a_gnorm": a_gnorm, "b_w_in": b_w_in, "w_kv_shared": w_kv_shared,
            "w_mem_kv": w_mem_kv, "w_o": w_o, "ln_mix_g": ln_mix_g, "ln_mix_b": ln_mix_b,
            "ln_ffn_g": ln_ffn_g, "ln_ffn_b": ln_ffn_b, "w_group": w_group, "b_group": b_group,
            "w_router": w_router, "b_router": b_router, "w_gate": w_gate, "w_up": w_up,
            "w_down": w_down}

def second_block(x, mem, a_w_in, a_lower_bounds, a_gnorm, b_w_in, w_kv_shared, w_mem_kv, w_o,
              ln_mix_g, ln_mix_b, ln_ffn_g, ln_ffn_b, w_group, b_group, w_router, b_router,
              w_gate, w_up, w_down):
    B, S, _ = x.shape
    lb_all = jnp.cumsum(jax.nn.softmax(a_lower_bounds.astype(jnp.float32), axis=0), axis=0)
    lb_all = lb_all - lb_all[0]
    shared_k = None
    shared_v = None
    for layer in range(DEPTH):
        mem_kv = mem @ w_mem_kv[layer]
        mem_k = mem_kv[..., :MEM_W].reshape(B, MEM_LEN, MEM_HEADS, MEM_HEAD_DIM)
        mem_v = mem_kv[..., MEM_W:].reshape(B, MEM_LEN, MEM_HEADS, MEM_HEAD_DIM)
        if layer < N_A_LAYERS:
            h = x @ a_w_in[layer]
            q, f_raw, i_in, g, qm = jnp.split(
                h, [SEQ_MIX_W, 2 * SEQ_MIX_W, 3 * SEQ_MIX_W, 4 * SEQ_MIX_W], axis=-1)
            seq_out = hgrn2_mix(q, f_raw, i_in, g, lb_all[layer], a_gnorm[layer])
        else:
            if layer == N_A_LAYERS:
                kv = x @ w_kv_shared
                shared_k = kv[..., :SEQ_MIX_W].astype(jnp.float32).reshape(
                    B, S, SB_HEADS, SB_HEAD_DIM).transpose(0, 2, 1, 3)
                shared_v = kv[..., SEQ_MIX_W:].astype(jnp.float32).reshape(
                    B, S, SB_HEADS, SB_HEAD_DIM).transpose(0, 2, 1, 3)
            h = x @ b_w_in[layer - N_A_LAYERS]
            q, qm = jnp.split(h, [SEQ_MIX_W], axis=-1)
            seq_out = stick_breaking_attention(q, shared_k, shared_v)
        mem_out = memory_attention(qm, mem_k, mem_v)
        mixed = jnp.concatenate([seq_out.astype(x.dtype), mem_out.astype(x.dtype)], axis=-1)
        x = post_norm(x, mixed @ w_o[layer], ln_mix_g[layer], ln_mix_b[layer])
        moe_out = hier_moe(x, w_group[layer], b_group[layer], w_router[layer], b_router[layer],
                           w_gate[layer], w_up[layer], w_down[layer])
        x = post_norm(x, moe_out, ln_ffn_g[layer], ln_ffn_b[layer])
    return x


def setup_inputs(seed=0):
    out = dict(first_inputs(seed))
    for name, value in second_inputs(seed + 1).items():
        if name != "x":
            out[name + "_2"] = value
    return out


def reference(
    x, c, w_ada, b_ada, norm_mix, norm_ffn, w_qkv, w_o, q_gain, k_gain, w_in, conv_w, w_out,
    w_gate_up, w_down, mem_2, a_w_in_2, a_lower_bounds_2, a_gnorm_2, b_w_in_2, w_kv_shared_2,
    w_mem_kv_2, w_o_2, ln_mix_g_2, ln_mix_b_2, ln_ffn_g_2, ln_ffn_b_2, w_group_2, b_group_2,
    w_router_2, b_router_2, w_gate_2, w_up_2, w_down_2,
):
    x = first_block(
        x, c, w_ada, b_ada, norm_mix, norm_ffn, w_qkv, w_o, q_gain, k_gain, w_in, conv_w, w_out,
        w_gate_up, w_down,
    )
    return second_block(
        x, mem_2, a_w_in_2, a_lower_bounds_2, a_gnorm_2, b_w_in_2, w_kv_shared_2, w_mem_kv_2,
        w_o_2, ln_mix_g_2, ln_mix_b_2, ln_ffn_g_2, ln_ffn_b_2, w_group_2, b_group_2, w_router_2,
        b_router_2, w_gate_2, w_up_2, w_down_2,
    )


_drawn_inputs = setup_inputs


def setup_inputs(seed=0):
    import zlib

    import numpy as np

    out = dict(_drawn_inputs(seed))
    spreads = {}
    factors = {'norm_mix': 3.464,
     'norm_ffn': 4.515,
     'q_gain': 8.0,
     'k_gain': 8.0,
     'mem_2': 3.461,
     'a_gnorm_2': 8.0,
     'w_mem_kv_2': 2.999,
     'b_group_2': 8.0,
     'b_router_2': 8.0}
    for name, (base, spread) in spreads.items():
        noise = np.random.default_rng([zlib.crc32(name.encode()), seed]).standard_normal(out[name].shape)
        drawn = base * np.exp(spread * noise) if base else spread * noise
        out[name] = __import__('jax').numpy.asarray(drawn.astype(out[name].dtype))
    for name, factor in factors.items():
        out[name] = (out[name] * factor).astype(out[name].dtype)
    return out
```

```python
from contextlib import ExitStack, contextmanager

import concourse.bass as bass
from concourse import mybir

F32 = mybir.dt.float32
F32R = mybir.dt.float32r
U8 = mybir.dt.uint8
ALU = mybir.AluOpType
ACT = mybir.ActivationFunctionType
AX = mybir.AxisListType

P = 128
S = 256
TT = S // P
D = 1024
KT = D // P
NC = 512
UK = 4
RAW = 6
SPL = 3
DEPTH = 2
HEADS = 8
FF = 2816
FW = 256
NFF = FF // FW
NEXP = 16
MIX = 768
HG = MIX // P
SBH = MIX // 64
EPS = 1e-6
LN_EPS = 1e-5
ALPHA = (2 * DEPTH) ** 0.25


class Count:

    def __init__(self, sem):
        self.sem, self.n, self.per, self.it = sem, 0, 0, None

    def value(self, ahead=0):
        return self.n + ahead if self.it is None else self.it * self.per + (self.n + ahead)

    def up(self, by=1):
        self.n += by
        return self.value()


@contextmanager
def looped(eng, times, counts):
    base = {c: c.n for c in counts}
    with eng.Fori(0, times, 1) as it:
        for c, per in counts.items():
            c.per, c.it = per, it
        yield it
    for c, per in counts.items():
        assert c.n == base[c] + per, (c.sem, c.n, base[c], per)
        c.n, c.per, c.it = base[c] + per * times, 0, None


def narrow_units():
    out = {}
    for name, ws in (("a_in", (512, 512, 512, 512, 256, 512, 512)), ("kv", (512, 256, 512, 256))):
        for i, w in enumerate(ws):
            if w < NC:
                out[PLAN[name] + 2 * i] = out[PLAN[name] + 2 * i + 1] = w
    return out


def stream_plan():
    at, plan = 0, {}
    for name, units in (("qkv", 12), ("wo0", 4), ("ffn0", 3 * NFF), ("win", 12), ("wout", 4), ("ffn1", 3 * NFF),
                        ("mem", 4), ("a_in", 14), ("wo1", 4), ("moe0", 3 * NEXP), ("kv", 8), ("b_in", 4),
                        ("wo2", 4), ("moe1", 3 * NEXP)):
        plan[name] = at
        at += units
    plan["end"] = at
    return plan


PLAN = stream_plan()

C_C, C_NMIX, C_NFFN, C_CONV, C_QG, C_KG, C_GN, C_BADA = 0, 8, 24, 40, 64, 65, 66, 72
NCOL = 168


def build(nc, A, out):
    ctx = ExitStack()
    with ctx:
        def sb(name, shape, dt=F32):
            return ctx.enter_context(nc.sbuf_tensor(name, shape, dt))

        def sem(name):
            return ctx.enter_context(nc.semaphore(name))

        raw = [sb(f"raw{i}", [P, UK, NC]) for i in range(RAW)]
        wh = [sb(f"w_high{i}", [P, UK, NC], F32R) for i in range(SPL)]
        wl = [sb(f"w_low{i}", [P, UK, NC], F32R) for i in range(SPL)]
        xs = sb("x_rows", [P, TT, D])
        hh = sb("h_high", [P, KT, S], F32R)
        hl = sb("h_low", [P, KT, S], F32R)
        FT = sb("features", [P, 20, S])
        tv = sb("rows", [P, TT, D])
        W = sb("scratch", [P, 41 * 256])
        Z = sb("small", [P, 8 * 256])
        ah = sb("act_high", [P, 2, S], F32R)
        al = sb("act_low", [P, 2, S], F32R)
        ident = sb("ident", [P, P])
        ones = sb("ones", [P, P])
        tri = sb("tri", [P, P])
        mcausal = sb("mask_causal", [P, 3 * P])
        mlev = sb("mask_levels", [P, 8, P], U8)
        cols = sb("cols", [P, NCOL])
        scol = sb("silu_c", [P, 8])
        modA = sb("mod_scale", [P, 16])
        modB = sb("mod_shift", [P, 16])
        st = sb("stats", [P, 64])
        gate = sb("gates", [P, TT, NEXP])

        cring = W[:, 0:16 * 256].rearrange("p (s k n) -> p s k n", s=2, k=UK)
        accw = W[:, 16 * 256:32 * 256].rearrange("p (c n) -> p c n", n=NC)
        gb = W[:, 32 * 256:40 * 256].rearrange("p (g n) -> p g n", g=2)
        pfx = W[:, 0:6 * 256].rearrange("p (h t) -> p h t", h=HG)
        sfx = W[:, 6 * 256:12 * 256].rearrange("p (h t) -> p h t", h=HG)
        qd = W[:, 12 * 256:18 * 256].rearrange("p (h t) -> p h t", h=HG)
        kd = W[:, 18 * 256:24 * 256].rearrange("p (h t) -> p h t", h=HG)
        scT = W[:, 24 * 256:33 * 256].rearrange("p (h t) -> p h t", h=HG)
        mk = W[:, 33 * 256:37 * 256].rearrange("p (l b m) -> p l b m", l=2, b=2)
        mv = W[:, 37 * 256:41 * 256].rearrange("p (l t n) -> p l t n", l=2, t=2)
        lnv = W[:, 0:8 * 256].rearrange("p (g n) -> p g n", g=2)
        mstrict = W[:, 8 * 256:8 * 256 + 384]
        rw = W[:, 10 * 256:10 * 256 + 160].rearrange("p (k n) -> p k n", k=KT)
        rbias = W[:, 11 * 256:11 * 256 + 20]
        rt = W[:, 12 * 256:20 * 256]

        ps = ctx.enter_context(nc.psum_tensor("ps", [P, 8, 512], F32))

        raw_loaded = [sem(f"raw_loaded{i}") for i in range(RAW)]
        small_loaded = sem("small_loaded")
        x_loaded = sem("x_loaded")
        ada_loaded = [sem(f"ada_loaded{i}") for i in range(2)]
        row_loaded = sem("row_loaded")
        mem_loaded = sem("mem_loaded")
        h_split = sem("h_split")
        l_split = sem("l_split")
        unit_used = sem("unit_used")
        act_step = sem("act_step")
        dve_step = sem("dve_step")
        ada_used = sem("ada_used")
        ada_acc = sem("ada_acc")
        sc_ready = sem("sc_ready")
        mod_sums = sem("mod_sums")
        mod_taken = sem("mod_taken")
        rstd_ready = sem("rstd_ready")
        stat_ready = sem("stat_ready")
        xn_ready = sem("xn_ready")
        xt_ready = sem("xt_ready")
        v_ready = sem("v_ready")
        hh_ready = sem("hh_ready")
        h_ready = sem("h_ready")
        lin_evac = sem("lin_evac")
        lin_taken = sem("lin_taken")
        sq_sum = sem("sq_sum")
        rs_ready = sem("rs_ready")
        normed = sem("normed")
        x_ready = sem("x_ready")
        s_ready = sem("s_ready")
        sm_ready = sem("sm_ready")
        nmax_ready = sem("nmax_ready")
        e_ready = sem("e_ready")
        p_ready = sem("p_ready")
        pt_ready = sem("pt_ready")
        pt_evac = sem("pt_evac")
        o_ready = sem("o_ready")
        oh_ready = sem("oh_ready")
        ol_ready = sem("ol_ready")
        z_ready = sem("z_ready")
        l_ready = sem("l_ready")
        sp_ready = sem("sp_ready")
        rest_ready = sem("rest_ready")
        la_ready = sem("la_ready")
        a_ready = sem("a_ready")
        sil_ready = sem("sil_ready")
        act_ready = sem("act_ready")
        at_ready = sem("at_ready")
        ah_ready = sem("ah_ready")
        a_split = sem("a_split")
        qk_in = sem("qk_in")
        dk_ready = sem("dk_ready")
        lev_scores = sem("lev_scores")
        lev_taken = sem("lev_taken")
        exp_ready = sem("exp_ready")
        router_ready = sem("router_ready")
        router_sums = sem("router_sums")
        am_ready = sem("am_ready")
        out_done = sem("out_done")

        block = ctx.enter_context(nc.Block())

        used_until = PLAN["end"]

        def moba_job(h):
            q, k, v = FT[:, h, :], FT[:, 8 + h, :], tv[:, :, h * P:(h + 1) * P]
            return dict(
                spans=((0, P), (P, 3 * P)), causal=True, blk=h, row=0, rows=P,
                scores=((0, P, q[:, 0:P], k[:, 0:P]), (P, 3 * P, q[:, P:S], k[:, 0:S])),
                turns=((0, 0), (P, P), (2 * P, 2 * P)),
                outs=((0, S, v[:, 0, :], 0), (P, S, v[:, 1, :], 2 * P)))

        def mem_job(l, h):
            r = slice(64 * (h % 2), 64 * (h % 2) + 64)
            q, k = FT[r, 18 + h // 2, :], mk[r, l, h // 2, :]
            v = mv[:, l, :, 64 * h:64 * h + 64]
            return dict(
                spans=((0, S), (S, 2 * S)), causal=False, blk=HG + h // 2, row=64 * (h % 2), rows=64,
                scores=((0, S, q[:, 0:P], k), (S, 2 * S, q[:, P:S], k)),
                turns=((0, 0), (P, 2 * P), (2 * P, P), (3 * P, 3 * P)),
                outs=((0, S, v[:, 0, :], 0), (0, S, v[:, 1, :], 2 * P)))

        MOBA = [moba_job(h) for h in range(HEADS)]
        MEM = [[mem_job(l, h) for h in range(4)] for l in range(2)]

        @block.sync
        def _(sp):
            xr = A["x"].rearrange("b (t p) d -> p (b t) d", p=P)
            for dst, src in ((cols[:, :], A["cols"]), (ident[:, :], A["k_ident"]), (ones[:, :], A["k_ones"]),
                             (tri[:, :], A["k_tri"]), (mcausal[:, :], A["k_causal"]),
                             (Z[:, 0:8 * P], A["k_levels"])):
                sp.dma_start(dst, src).then_inc(small_loaded, 16)
            sp.dma_start(xs[:, :, :], xr).then_inc(x_loaded, 16)

            hsp, lsp = Count(h_split), Count(l_split)
            n = [0]

            def load(src_a, src_b, dst_a, dst_b, j=0):
                u = n[0] + j
                slot = u % RAW
                if u >= RAW or hsp.it is not None:
                    sp.wait_ge(h_split, hsp.up())
                    sp.wait_ge(l_split, lsp.up())
                sp.dma_start(dst_a(raw[slot]), src_a).then_inc(raw_loaded[slot], 16)
                sp.dma_start(dst_b(raw[slot]), src_b).then_inc(raw_loaded[slot], 16)

            def columns(w, c0, width):
                v = w.rearrange("(k p) n -> p k n", p=P)
                for k in (0, UK):
                    load(v[:, k:k + 2, c0:c0 + width], v[:, k + 2:k + 4, c0:c0 + width],
                         lambda r: r[:, 0:2, 0:width], lambda r: r[:, 2:4, 0:width])
                    n[0] += 1

            def gate_up(wg, wu, c0, j):
                g, u = (w.rearrange("(k p) n -> p k n", p=P) for w in (wg, wu))
                for q, k in enumerate((0, UK)):
                    load(g[:, k:k + UK, c0], u[:, k:k + UK, c0],
                         lambda r: r[:, :, 0:FW], lambda r: r[:, :, FW:2 * FW], j + q)

            def down(wd, c0, j):
                d = wd[c0, :].rearrange("(k p) (h n) -> p k h n", p=P, h=2)
                load(d[:, 0, :, :], d[:, 1, :, :], lambda r: r[:, 0:2, :], lambda r: r[:, 2:4, :], j)

            def ffn(chunks, gu, dn):
                gu(0, 0)
                n[0] += 2
                loops, rest = divmod(chunks - 1, 2)
                with looped(sp, loops, {hsp: 6, lsp: 6}) as it:
                    for r in range(2):
                        gu(it * 2 + (r + 1), 3 * r)
                        dn(it * 2 + r, 3 * r + 2)
                n[0] += 6 * loops
                for c in range(2 * loops + 1, chunks):
                    gu(c, 0)
                    dn(c - 1, 2)
                    n[0] += 3
                dn(chunks - 1, 0)
                n[0] += 1

            def dense_ffn(layer):
                w, wd = A["w_gate_up"][layer], A["w_down"][layer]
                ffn(NFF, lambda c, j: gate_up(w[:, 0:FF], w[:, FF:2 * FF], bass.ds(c * FW, FW), j),
                    lambda c, j: down(wd, bass.ds(c * FW, FW), j))

            def moe(layer):
                wg, wu = (A[name][layer].rearrange("e d f -> (e d) f") for name in ("w_gate_2", "w_up_2"))
                wd = A["w_down_2"][layer].rearrange("e f d -> (e f) d")

                def gu(e, j):
                    g, u = (w[bass.ds(e * D, D), :].rearrange("(k p) n -> p k n", p=P) for w in (wg, wu))
                    for q, k in enumerate((0, UK)):
                        load(g[:, k:k + UK, :], u[:, k:k + UK, :],
                             lambda r: r[:, :, 0:FW], lambda r: r[:, :, FW:2 * FW], j + q)
                ffn(NEXP, gu, lambda e, j: down(wd, bass.ds(e * FW, FW), j))

            for c in range(6):
                columns(A["w_qkv"][0], c * NC, NC)
            for c in range(2):
                columns(A["w_o"][0], c * NC, NC)
            dense_ffn(0)
            for c in (2, 3, 4, 5, 0, 1):
                columns(A["w_in"][0], c * NC, NC)
            for c in range(2):
                columns(A["w_out"][0], c * NC, NC)
            dense_ffn(1)
            for l in range(DEPTH):
                columns(A["w_mem_kv_2"][l], 0, NC)
            for c0, w in ((0, 512), (512, 512), (1024, 512), (1536, 512), (2048, 256), (2304, 512), (2816, 512)):
                columns(A["a_w_in_2"][0], c0, w)
            for c in range(2):
                columns(A["w_o_2"][0], c * NC, NC)
            moe(0)
            for c0, w in ((0, 512), (512, 256), (768, 512), (1280, 256)):
                columns(A["w_kv_shared_2"], c0, w)
            for c in range(2):
                columns(A["b_w_in_2"][0], c * NC, NC)
            for c in range(2):
                columns(A["w_o_2"][1], c * NC, NC)
            moe(1)
            xrd = Count(x_ready)
            sp.wait_ge(x_ready, xrd.up(8))
            sp.dma_start(out.rearrange("b (t p) d -> p (b t) d", p=P), xs[:, :, :]).then_inc(out_done, 16)
            sp.wait_ge(out_done, 16)

        @block.gpsimd
        def _(pool):
            used = Count(ada_used)

            def ada(layer):
                v = A["w_ada"][layer].rearrange("(k p) n -> p k n", p=P)

                def chunk(c, first):
                    for q in range(2):
                        if not first:
                            pool.wait_ge(ada_used, used.up())
                        pool.dma_start(cring[:, q, :, :], v[:, q * UK:(q + 1) * UK, bass.ds(c * NC, NC)]) \
                            .then_inc(ada_loaded[q], 16)
                if layer == 0:
                    chunk(0, True)
                    with looped(pool, 11, {used: 2}) as it:
                        chunk(it + 1, False)
                else:
                    with looped(pool, 12, {used: 2}) as it:
                        chunk(it, False)

            def gate_rows(layer):
                for g, c0 in enumerate((2 * D, 5 * D)):
                    pool.dma_start(gb[:, g, :], A["b_ada"][layer:layer + 1, c0:c0 + D].to_broadcast([P, D])) \
                        .then_inc(row_loaded, 16)

            xrd = Count(x_ready)
            gate_rows(0)
            ada(0)
            ada(1)
            pool.wait_ge(x_ready, xrd.up(2))
            gate_rows(1)
            pool.wait_ge(x_ready, xrd.up(2))
            olr = Count(ol_ready)

            def ln_rows(kind, layer):
                pool.dma_start(lnv[:, 0, :], A[f"ln_{kind}_g_2"][layer:layer + 1, :].to_broadcast([P, D])) \
                    .then_inc(row_loaded, 16)
                pool.dma_start(lnv[:, 1, :], A[f"ln_{kind}_b_2"][layer:layer + 1, :].to_broadcast([P, D])) \
                    .then_inc(row_loaded, 16)

            def router_rows(layer):
                pool.dma_start(rw[:, :, 0:4], A["w_group_2"][layer].rearrange("(k p) n -> p k n", p=P)) \
                    .then_inc(row_loaded, 16)
                pool.dma_start(rw[:, :, 4:20], A["w_router_2"][layer].rearrange("(k p) n -> p k n", p=P)) \
                    .then_inc(row_loaded, 16)
                pool.dma_start(rbias[:, 0:4], A["b_group_2"][layer:layer + 1, :].to_broadcast([P, 4])) \
                    .then_inc(row_loaded, 16)
                pool.dma_start(rbias[:, 4:20], A["b_router_2"][layer:layer + 1, :].to_broadcast([P, 16])) \
                    .then_inc(row_loaded, 16)

            pool.dma_start(tv[:, :, :], A["mem_2"].rearrange("b (t p) d -> p (b t) d", p=P)).then_inc(mem_loaded, 16)
            pool.wait_ge(ol_ready, olr.up(len(MOBA) + 1 + len(MEM[0])))
            ln_rows("mix", 0)
            router_rows(0)
            pool.dma_start(mstrict, A["k_strict"]).then_inc(row_loaded, 16)
            pool.wait_ge(x_ready, xrd.up(1))
            ln_rows("ffn", 0)
            pool.wait_ge(x_ready, xrd.up(1))
            ln_rows("mix", 1)
            router_rows(1)
            pool.wait_ge(x_ready, xrd.up(1))
            ln_rows("ffn", 1)

        @block.scalar
        def _(act):
            step = Count(act_step)
            hsp, used = Count(h_split), Count(unit_used)
            n = [0]
            LIMIT = PLAN["end"]
            widths = narrow_units()

            def split(j=0, waited=False):
                u = n[0] + j
                if u >= LIMIT:
                    return
                w = widths.get(u, NC)
                loaded = 32 * (u // RAW + 1)
                act.wait_ge(raw_loaded[u % RAW], loaded if hsp.it is None else hsp.it * 32 + loaded)
                if u >= SPL and not waited:
                    act.wait_ge(unit_used, used.up())
                act.activation(wh[u % SPL][:, :, 0:w], raw[u % RAW][:, :, 0:w], ACT.Copy).then_inc(h_split, 1)
                hsp.up()

            def ahead(upto):
                while n[0] < upto + SPL:
                    split()
                    n[0] += 1

            xt, v, hhr = Count(xt_ready), Count(v_ready), Count(hh_ready)
            rstd, stat, xrd = Count(rstd_ready), Count(stat_ready), Count(x_ready)
            evac = Count(lin_evac)
            eps_col = {EPS: st[:, 60:61], LN_EPS: st[:, 61:62]}

            def rstd_of(src, width, eps):
                act.activation(st[:, 2:4], src, ACT.Ln, bias=eps_col[eps], scale=1.0 / width).then_inc(act_step, 1)
                act.wait_ge(act_step, step.up())
                act.activation(st[:, 4:6], st[:, 2:4], ACT.Exp, scale=-0.5).then_inc(rstd_ready, 1)
                act.wait_ge(rstd_ready, rstd.up())

            def rms_stats():
                for t in range(TT):
                    act.activation(tv[:, t, :], xs[:, t, :], ACT.Square, accum_out=st[:, t:t + 1]).then_inc(act_step, 1)
                    act.wait_ge(act_step, step.up())
                rstd_of(st[:, 0:2], D, EPS)

            def ln_stats():
                act.wait_ge(stat_ready, stat.up())
                rstd_of(st[:, 57:60:2], 1, LN_EPS)

            def bank_k(g):
                return ps[:, 4 + g, :].rearrange("p (k t) -> p k t", k=2)

            def transposed(modulated):
                for g in range(4):
                    act.wait_ge(v_ready if modulated else xt_ready, (v if modulated else xt).up())
                    act.activation(hh[:, 2 * g:2 * g + 2, :], bank_k(g), ACT.Copy).then_inc(hh_ready, 1)
                    hhr.up()
                if modulated:
                    xt.n += 4

            act.wait_ge(small_loaded, 96)
            scr = Count(sc_ready)
            act.activation(scol[:, :], cols[:, C_C:C_C + 8], ACT.Exp, scale=-1.0).then_inc(sc_ready, 1)
            scr.up()
            act.wait_ge(x_loaded, 16)
            act.wait_ge(dve_step, 2)
            rms_stats()
            ahead(0)
            transposed(True)

            lin = [0]

            def pair(b=0, e=2):
                return ps[:, 2 * (lin[0] % 2) + b:2 * (lin[0] % 2) + e, :]

            def chunk_ready(ph, c):
                ahead(PLAN[ph] + 2 * c + 1)
                act.wait_ge(unit_used, PLAN[ph] + 2 * c + 2)

            sqs, rsr, nrm = Count(sq_sum), Count(rs_ready), Count(normed)
            sq, rs = Z[:, 0:1024], Z[:, 1024:2048]

            def qk_rs():
                act.wait_ge(sq_sum, sqs.up())
                if rsr.n:
                    act.wait_ge(normed, nrm.up())
                act.activation(rs, ps[:, 4:6, :].rearrange("p a b -> p (a b)"), ACT.Ln, bias=eps_col[EPS], scale=1.0 / P).then_inc(act_step, 1)
                act.wait_ge(act_step, step.up())
                act.activation(rs, rs, ACT.Exp, scale=-0.5).then_inc(rs_ready, 1)
                act.wait_ge(rs_ready, rsr.up())

            for c in range(6):
                chunk_ready("qkv", c)
                if c < 4:
                    act.activation(FT[:, 4 * c:4 * c + 4, :].rearrange("p k t -> p (k t)"),
                                                  pair().rearrange("p a b -> p (a b)"), ACT.Copy).then_inc(act_step, 1)
                    act.wait_ge(act_step, step.up())
                    if c:
                        qk_rs()
                    act.activation(sq, pair().rearrange("p a b -> p (a b)"), ACT.Square).then_inc(lin_evac, 1)
                    act.wait_ge(lin_evac, evac.up())
                else:
                    if c == 4:
                        qk_rs()
                    act.activation(tv[:, :, (c - 4) * NC:(c - 3) * NC], pair(), ACT.Copy).then_inc(lin_evac, 1)
                    act.wait_ge(lin_evac, evac.up())
                lin[0] += 1
            ahead(PLAN["wo0"])

            nmx, er = Count(nmax_ready), Count(e_ready)
            ptr, pte = Count(pt_ready), Count(pt_evac)
            orr, ohr = Count(o_ready), Count(oh_ready)

            def head_out(m):
                act.wait_ge(o_ready, orr.up())
                r = slice(m["row"], m["row"] + m["rows"])
                act.activation(hh[r, m["blk"], :], ps[r, 7, 0:S], ACT.Copy).then_inc(oh_ready, 1)
                act.wait_ge(oh_ready, ohr.up())

            def heads(jobs):
                def exps(j):
                    act.wait_ge(nmax_ready, nmx.up())
                    b = j % 2
                    for t, (c0, c1) in enumerate(jobs[j]["spans"]):
                        z = Z[:, b * 512 + c0:b * 512 + c1]
                        act.activation(
                            z, z, ACT.Exp, bias=st[:, 8 + 4 * b + t:9 + 4 * b + t],
                            accum_out=st[:, 16 + 4 * b + t:17 + 4 * b + t]).then_inc(e_ready if t else act_step, 1)
                        act.wait_ge(e_ready if t else act_step, (er if t else step).up())

                def turned(j):
                    act.wait_ge(pt_ready, ptr.up())
                    w = jobs[j]["spans"][1][1]
                    act.activation(Z[:, 1024 + (j % 2) * 512:1024 + (j % 2) * 512 + w],
                                                 ps[:, 6, 0:w], ACT.Copy).then_inc(pt_evac, 1)
                    act.wait_ge(pt_evac, pte.up())

                for i in range(len(jobs) + 2):
                    if i < len(jobs):
                        exps(i)
                    if 0 <= i - 1 < len(jobs):
                        turned(i - 1)
                    if i >= 2:
                        head_out(jobs[i - 2])

            heads(MOBA)

            def wo(ph):
                ahead(PLAN[ph] + 1)
                ahead(PLAN[ph] + 4)

            def norm_first():
                act.wait_ge(x_ready, xrd.up())
                rms_stats()
                transposed(True)

            wo("wo0")
            norm_first()

            silr, atr, ahr = Count(sil_ready), Count(at_ready), Count(ah_ready)

            def ffn(ph, chunks):
                def silu():
                    act.wait_ge(unit_used, used.up())
                    act.activation(Z[:, 0:512].rearrange("p (t n) -> p t n", t=2), ps[:, 0:2, 0:FW], ACT.Silu).then_inc(sil_ready, 1)
                    silr.up()

                def high():
                    act.wait_ge(at_ready, atr.up())
                    act.activation(ah[:, :, :], ps[:, 2, :].rearrange("p (k t) -> p k t", k=2), ACT.Copy).then_inc(ah_ready, 1)
                    ahr.up()

                def chunk(j):
                    high()
                    split(j)
                    silu()
                    split(j + 1, True)
                    split(j + 2)

                ahead(PLAN[ph])
                assert n[0] == PLAN[ph] + SPL
                split()
                silu()
                split(1, True)
                n[0] += 2
                loops = (chunks - 1) // 2
                with looped(act, loops, {hsp: 6, used: 6, silr: 2, atr: 2, ahr: 2}):
                    chunk(0)
                    chunk(3)
                n[0] += 6 * loops
                for _ in range(chunks - 1 - 2 * loops):
                    chunk(0)
                    n[0] += 3
                high()

            ffn("ffn0", NFF)
            ahead(PLAN["win"])
            act.wait_ge(x_ready, xrd.up())
            rms_stats()
            transposed(True)

            ptk = Count(lin_taken)
            for c in range(6):
                chunk_ready("win", c)
                if c < 2:
                    i = act.activation(FT[:, 4 * c:4 * c + 4, :].rearrange("p k t -> p (k t)"),
                                       pair().rearrange("p a b -> p (a b)"), ACT.Copy)
                else:
                    i = act.activation(Z[:, 0:1024] if c % 2 == 0 else Z[:, 1024:2048],
                                       pair().rearrange("p a b -> p (a b)"), ACT.Copy)
                i.then_inc(lin_evac, 1)
                act.wait_ge(lin_evac, evac.up())
                lin[0] += 1
                if c in (2, 3, 4, 5):
                    act.wait_ge(lin_taken, ptk.up())
            ahead(PLAN["wout"])
            for g in range(2):
                act.activation(hh[:, 4 * g:4 * g + 4, :], Z[:, 1024 * g:1024 * g + 1024].rearrange("p (k t) -> p k t", k=4), ACT.Copy).then_inc(hh_ready, 1)
                hhr.up()
            wo("wout")
            norm_first()
            ffn("ffn1", NFF)
            ahead(PLAN["mem"])
            act.wait_ge(x_ready, xrd.up())

            transposed(False)
            for l in range(DEPTH):
                chunk_ready("mem", l)
                act.activation(mk[:, l, :, :].rearrange("p b m -> p (b m)"), pair(0, 1).rearrange("p a b -> p (a b)"), ACT.Copy).then_inc(act_step, 1)
                act.wait_ge(act_step, step.up())
                act.activation(mv[:, l, :, :].rearrange("p b m -> p (b m)"), pair(1, 2).rearrange("p a b -> p (a b)"), ACT.Copy).then_inc(lin_evac, 1)
                act.wait_ge(lin_evac, evac.up())
                lin[0] += 1
            ahead(PLAN["a_in"])
            transposed(False)

            def features(b0, nb, func, last=True, skip=0):
                src = pair().rearrange("p a (b t) -> p (a b) t", t=S)[:, skip:skip + nb, :]
                act.activation(FT[:, b0:b0 + nb, :], src, func).then_inc(lin_evac if last else act_step, 1)
                act.wait_ge(lin_evac if last else act_step, (evac if last else step).up())

            def rows(c0, w):
                act.activation(tv[:, :, c0:c0 + w], pair()[:, :, 0:w], ACT.Copy).then_inc(lin_evac, 1)
                act.wait_ge(lin_evac, evac.up())

            for c in range(7):
                chunk_ready("a_in", c)
                if c == 0:
                    features(0, 4, ACT.Silu)
                elif c == 1:
                    features(4, 2, ACT.Silu, last=False)
                    features(6, 2, ACT.Copy, skip=2)
                elif c == 2:
                    features(8, 4, ACT.Copy)
                elif c == 3:
                    rows(0, 512)
                elif c == 4:
                    rows(512, 256)
                elif c == 5:
                    features(12, 4, ACT.Silu)
                else:
                    features(16, 2, ACT.Silu, last=False)
                    features(18, 2, ACT.Copy, skip=2)
                lin[0] += 1
            ahead(PLAN["wo1"])
            heads(MEM[0])

            exr, dkr, dsg = Count(exp_ready), Count(qk_in), Count(dk_ready)
            levs = Count(lev_scores)
            act.wait_ge(qk_in, dkr.up())
            act.activation(kd, kd, ACT.Exp).then_inc(act_step, 1)
            act.wait_ge(act_step, step.up())
            act.activation(kd, kd, ACT.Ln, bias=1.0).then_inc(exp_ready, 1)
            act.wait_ge(exp_ready, exr.up())
            act.wait_ge(qk_in, dkr.up())
            act.activation(FT[:, 6:12, :], sfx, ACT.Exp, scale=-1.0).then_inc(exp_ready, 1)
            act.wait_ge(exp_ready, exr.up())
            for l in range(1, 9):
                act.wait_ge(lev_scores, levs.up())
                act.wait_ge(qk_in, dkr.up())
                act.activation(qd, pfx, ACT.Exp).then_inc(act_step, 1)
                act.wait_ge(act_step, step.up())
                act.activation(kd, sfx, ACT.Exp).then_inc(exp_ready, 1)
                act.wait_ge(exp_ready, exr.up())
            act.wait_ge(o_ready, orr.up())
            o3 = ps[:, 4:7, :].rearrange("p a (b t) -> p (a b) t", t=S)
            act.activation(pfx, o3, ACT.Copy).then_inc(act_step, 1)
            act.wait_ge(act_step, step.up())
            act.activation(qd, o3, ACT.Square).then_inc(exp_ready, 1)
            act.wait_ge(exp_ready, exr.up())
            act.wait_ge(sq_sum, sqs.up())
            act.activation(kd, o3, ACT.Ln, bias=eps_col[EPS], scale=1.0 / P).then_inc(act_step, 1)
            act.wait_ge(act_step, step.up())
            act.activation(kd, kd, ACT.Exp, scale=-0.5).then_inc(rs_ready, 1)
            act.wait_ge(rs_ready, rsr.up())
            act.wait_ge(v_ready, v.up())
            act.activation(hh[:, 0:6, :], sfx, ACT.Copy).then_inc(hh_ready, 1)
            hhr.up()
            wo("wo1")
            ln_stats()
            act.wait_ge(x_ready, xrd.up())
            transposed(False)
            def router():
                act.wait_ge(router_ready, sp_in.up())
                act.activation(rt[:, 64:104], rt[:, 64:104], ACT.Exp).then_inc(exp_ready, 1)
                act.wait_ge(exp_ready, exr.up())

            sp_in = Count(router_ready)
            router()
            ffn("moe0", NEXP)
            ahead(PLAN["kv"])
            ln_stats()
            act.wait_ge(x_ready, xrd.up())
            transposed(False)

            for c in range(4):
                chunk_ready("kv", c)
                if c == 0:
                    features(6, 4, ACT.Copy)
                elif c == 1:
                    features(10, 2, ACT.Copy)
                elif c == 2:
                    rows(0, 512)
                else:
                    rows(512, 256)
                lin[0] += 1
            for c in range(2):
                chunk_ready("b_in", c)
                if c == 0:
                    features(0, 4, ACT.Copy)
                else:
                    features(4, 2, ACT.Copy, last=False)
                    features(18, 2, ACT.Copy, skip=2)
                lin[0] += 1
            ahead(PLAN["wo2"])
            heads(MEM[1])
            zr, lr, lar, ar = Count(z_ready), Count(l_ready), Count(la_ready), Count(a_ready)

            def sb_buf(kind, b):
                return Z[:, (2 * kind + b) * 512:(2 * kind + b) * 512 + 384]

            for i in range(SBH + 2):
                if i >= 2:
                    head_out(dict(row=64 * (i % 2), rows=64, blk=(i - 2) // 2))
                if i < SBH:
                    act.wait_ge(z_ready, zr.up())
                    nb = sb_buf(1, i % 2)
                    act.activation(nb, nb, ACT.Exp).then_inc(act_step, 1)
                    act.wait_ge(act_step, step.up())
                    act.activation(nb, nb, ACT.Ln, bias=1.0).then_inc(l_ready, 1)
                    act.wait_ge(l_ready, lr.up())
                if 0 <= i - 1 < SBH:
                    act.wait_ge(la_ready, lar.up())
                    nb = sb_buf(1, (i - 1) % 2)
                    act.activation(nb, nb, ACT.Exp).then_inc(a_ready, 1)
                    act.wait_ge(a_ready, ar.up())
            wo("wo2")
            ln_stats()
            act.wait_ge(x_ready, xrd.up())
            transposed(False)
            router()
            ffn("moe1", NEXP)
            ln_stats()

        @block.vector
        def _(dve):
            step = Count(dve_step)
            hsp, lsp = Count(h_split), Count(l_split)
            n = [0]
            LIMIT = PLAN["end"]
            widths = narrow_units()

            def split(j=0):
                u = n[0] + j
                if u >= LIMIT:
                    return
                w = widths.get(u, NC)
                dve.wait_ge(h_split, hsp.up())
                dve.tensor_tensor(wl[u % SPL][:, :, 0:w], raw[u % RAW][:, :, 0:w],
                                             wh[u % SPL][:, :, 0:w].bitcast(F32), ALU.subtract).then_inc(l_split, 1)
                lsp.up()

            def ahead(upto):
                while n[0] < upto + SPL:
                    split()
                    n[0] += 1

            rstd, stat, xrd = Count(rstd_ready), Count(stat_ready), Count(x_ready)
            xn, xt, v, hhr, hr = Count(xn_ready), Count(xt_ready), Count(v_ready), Count(hh_ready), Count(h_ready)
            accd, usedd = Count(ada_acc), Count(ada_used)
            rows_in = [0]

            dve.memset(st[:, 60:61], EPS).then_inc(dve_step, 1)
            dve.wait_ge(dve_step, step.up())
            dve.memset(st[:, 61:62], LN_EPS).then_inc(dve_step, 1)
            dve.wait_ge(dve_step, step.up())
            dve.wait_ge(small_loaded, 96)
            dve.tensor_copy(mlev[:, :, :], Z[:, 0:8 * P].rearrange("p (l n) -> p l n", n=P)).then_inc(dve_step, 1)
            dve.wait_ge(dve_step, step.up())
            dve.tensor_scalar(st[:, 62:63], cols[:, C_QG:C_QG + 1], P ** -0.5, None, ALU.mult).then_inc(dve_step, 1)
            dve.wait_ge(dve_step, step.up())
            dve.wait_ge(sc_ready, 1)
            dve.tensor_scalar(scol[:, :], scol[:, :], 1.0, None, ALU.add).then_inc(dve_step, 1)
            dve.wait_ge(dve_step, step.up())
            dve.reciprocal(scol[:, :], scol[:, :]).then_inc(dve_step, 1)
            dve.wait_ge(dve_step, step.up())
            dve.tensor_tensor(scol[:, :], scol[:, :], cols[:, C_C:C_C + 8], ALU.mult).then_inc(dve_step, 1)
            dve.wait_ge(dve_step, step.up())

            def ada(layer, c, acc, it=None):
                g = 12 * layer + c
                for q in range(2):
                    dve.wait_ge(ada_loaded[q], 16 * (g + 1) if it is None else it * 32 + 16 * (g + 1))
                    for k in range(UK):
                        w, s = cring[:, q, k, :], scol[:, UK * q + k:UK * q + k + 1]
                        if q == k == 0:
                            i = dve.tensor_scalar(acc, w, s, None, ALU.mult)
                        else:
                            i = dve.scalar_tensor_tensor(acc, w, s, acc, ALU.mult, ALU.add)
                        i.then_inc(ada_used if k == UK - 1 else ada_acc, 1)
                        dve.wait_ge(ada_used if k == UK - 1 else ada_acc, (usedd if k == UK - 1 else accd).up())

            ft_acc = FT[:, :, :].rearrange("p (c a) t -> p c (a t)", a=2)

            def acc_of(layer, c):
                if layer == 0:
                    return ft_acc[:, c, :] if c < 4 else accw[:, c - 4, :]
                return ft_acc[:, c, :] if c < 10 else accw[:, c - 10, :]

            msum, mtk = Count(mod_sums), Count(mod_taken)

            def mod_cols(layer, which):
                dve.wait_ge(mod_sums, msum.up())
                b = cols[:, C_BADA + 48 * layer + 24 * which:C_BADA + 48 * layer + 24 * which + 16]
                gain = cols[:, (C_NFFN if which else C_NMIX) + 8 * layer:(C_NFFN if which else C_NMIX) + 8 * layer + 8]
                o = slice(8 * which, 8 * which + 8)
                dve.tensor_tensor(modB[:, o], ps[:, 7, 0:8], b[:, 0:8], ALU.add).then_inc(dve_step, 1)
                dve.wait_ge(dve_step, step.up())
                dve.tensor_tensor(modA[:, o], ps[:, 7, 8:16], b[:, 8:16], ALU.add).then_inc(dve_step, 1)
                dve.wait_ge(dve_step, step.up())
                dve.scalar_tensor_tensor(modA[:, o], modA[:, o], 1.0, gain, ALU.add, ALU.mult).then_inc(mod_taken, 1)
                dve.wait_ge(mod_taken, mtk.up())

            def mod_gate(g):
                dve.wait_ge(mod_sums, msum.up())
                dve.tensor_tensor(gb[:, g, :], ps[:, 4:6, :].rearrange("p a b -> p (a b)"), gb[:, g, :], ALU.add).then_inc(mod_taken, 1)
                dve.wait_ge(mod_taken, mtk.up())

            def rms_apply():
                dve.wait_ge(rstd_ready, rstd.up())
                dve.tensor_scalar(tv[:, 0, :], xs[:, 0, :], st[:, 4:5], None, ALU.mult).then_inc(dve_step, 1)
                dve.wait_ge(dve_step, step.up())
                dve.tensor_scalar(tv[:, 1, :], xs[:, 1, :], st[:, 5:6], None, ALU.mult).then_inc(xn_ready, 1)
                dve.wait_ge(xn_ready, xn.up())

            def bank_k(g):
                return ps[:, 4 + g, :].rearrange("p (k t) -> p k t", k=2)

            def low(g):
                dve.wait_ge(hh_ready, hhr.up())
                dve.tensor_tensor(hl[:, 2 * g:2 * g + 2, :], bank_k(g),
                                            hh[:, 2 * g:2 * g + 2, :].bitcast(F32), ALU.subtract).then_inc(h_ready, 1)
                hr.up()

            def transposed_mod(which):
                for g in range(5):
                    if g < 4:
                        dve.wait_ge(xt_ready, xt.up())
                        for q in range(2):
                            k = 8 * which + 2 * g + q
                            b = ps[:, 4 + g, q * S:(q + 1) * S]
                            dve.tensor_scalar(
                                b, b, modA[:, k:k + 1], modB[:, k:k + 1], ALU.mult, ALU.add).then_inc(v_ready if q else dve_step, 1)
                            dve.wait_ge(v_ready if q else dve_step, (v if q else step).up())
                    if g:
                        low(g - 1)

            def transposed_plain():
                for g in range(4):
                    low(g)
                xt.n += 4

            for c in range(4):
                ada(0, c, acc_of(0, c))
            ahead(0)
            mod_cols(0, 0)
            rms_apply()
            transposed_mod(0)

            rsr, nrm = Count(rs_ready), Count(normed)

            def qk_norm(c):
                dve.wait_ge(rs_ready, rsr.up())
                f = FT[:, 4 * c:4 * c + 4, :].rearrange("p k t -> p (k t)")
                gain = st[:, 62:63] if c < 2 else cols[:, C_KG:C_KG + 1]
                dve.scalar_tensor_tensor(f, f, gain, Z[:, 1024:2048], ALU.mult, ALU.mult).then_inc(normed, 1)
                dve.wait_ge(normed, nrm.up())

            for c in range(6):
                ahead(PLAN["qkv"] + 2 * c + 1)
                if 1 <= c <= 4:
                    qk_norm(c - 1)
                ada(0, 4 + c, acc_of(0, 4 + c))
            ahead(PLAN["wo0"])
            for c in (10, 11):
                ada(0, c, acc_of(0, c))

            sr, smr, nmx = Count(s_ready), Count(sm_ready), Count(nmax_ready)
            er, pr, ohr, olr = Count(e_ready), Count(p_ready), Count(oh_ready), Count(ol_ready)

            def head_low(m):
                dve.wait_ge(oh_ready, ohr.up())
                r = slice(m["row"], m["row"] + m["rows"])
                dve.tensor_tensor(hl[r, m["blk"], :], ps[r, 7, 0:S], hh[r, m["blk"], :].bitcast(F32),
                                                ALU.subtract).then_inc(ol_ready, 1)
                dve.wait_ge(ol_ready, olr.up())

            def heads(jobs):
                def scores(j):
                    dve.wait_ge(s_ready, sr.up())
                    b, m = j % 2, jobs[j]
                    w = m["spans"][1][1]
                    z, s = Z[:, b * 512:b * 512 + w], ps[:, 4 + b, 0:w]
                    if m["causal"]:
                        i = dve.tensor_tensor(z, s, mcausal[:, :], ALU.add)
                    else:
                        i = dve.tensor_scalar(z, s, 64 ** -0.5, None, ALU.mult)
                    i.then_inc(sm_ready, 1)
                    dve.wait_ge(sm_ready, smr.up())
                    for t, (c0, c1) in enumerate(m["spans"]):
                        dve.tensor_reduce(
                            st[:, 8 + 4 * b + t:9 + 4 * b + t], Z[:, b * 512 + c0:b * 512 + c1], AX.X, ALU.max,
                            negate=True).then_inc(nmax_ready if t else dve_step, 1)
                        dve.wait_ge(nmax_ready if t else dve_step, (nmx if t else step).up())

                def probs(j):
                    dve.wait_ge(e_ready, er.up())
                    b = j % 2
                    dve.reciprocal(st[:, 24 + 4 * b:26 + 4 * b], st[:, 16 + 4 * b:18 + 4 * b]).then_inc(dve_step, 1)
                    dve.wait_ge(dve_step, step.up())
                    for t, (c0, c1) in enumerate(jobs[j]["spans"]):
                        z = Z[:, b * 512 + c0:b * 512 + c1]
                        dve.tensor_scalar(z, z, st[:, 24 + 4 * b + t:25 + 4 * b + t], None, ALU.mult).then_inc(p_ready if t else dve_step, 1)
                        dve.wait_ge(p_ready if t else dve_step, (pr if t else step).up())

                for i in range(len(jobs) + 2):
                    if i < len(jobs):
                        scores(i)
                    if 0 <= i - 1 < len(jobs):
                        probs(i - 1)
                    if i >= 2:
                        head_low(jobs[i - 2])

            heads(MOBA)
            dve.wait_ge(row_loaded, 32)
            mod_cols(0, 1)
            mod_gate(0)
            mod_gate(1)

            def wo(ph):
                ahead(PLAN[ph] + 1)
                ahead(PLAN[ph] + 4)

            def add_gated(g, after):
                dve.wait_ge(unit_used, PLAN[after])
                for t in range(TT):
                    y = ps[:, 4 + t:8:2, :]
                    dve.tensor_tensor(tv[:, t, :].rearrange("p (a n) -> p a n", a=2), y,
                                         gb[:, g, :].rearrange("p (a n) -> p a n", a=2), ALU.mult).then_inc(dve_step, 1)
                    dve.wait_ge(dve_step, step.up())
                    dve.tensor_tensor(xs[:, t, :], xs[:, t, :], tv[:, t, :], ALU.add).then_inc(x_ready if t else dve_step, 1)
                    dve.wait_ge(x_ready if t else dve_step, (xrd if t else step).up())

            wo("wo0")
            add_gated(0, "ffn0")
            rms_apply()
            transposed_mod(1)

            silr, acr, ahr, asp = Count(sil_ready), Count(act_ready), Count(ah_ready), Count(a_split)

            def ffn(ph, chunks, weight, extra=None):
                def product(c, r=0):
                    dve.wait_ge(sil_ready, silr.up())
                    for t in range(TT):
                        sil = Z[:, t * FW:(t + 1) * FW]
                        up = ps[:, t, FW:2 * FW]
                        dve.scalar_tensor_tensor(
                            Z[:, 512 + t * FW:512 + (t + 1) * FW], sil, weight(t, c), up, ALU.mult, ALU.mult).then_inc(act_ready, 1)
                        acr.up()

                def low_part():
                    dve.wait_ge(ah_ready, ahr.up())
                    dve.tensor_tensor(al[:, :, :], ps[:, 2, :].rearrange("p (k t) -> p k t", k=2),
                                                 ah[:, :, :].bitcast(F32), ALU.subtract).then_inc(a_split, 1)
                    asp.up()

                def chunk(c, j, it=None):
                    low_part()
                    split(j)
                    split(j + 1)
                    product(c)
                    split(j + 2)

                ahead(PLAN[ph])
                split()
                product(0)
                split(1)
                n[0] += 2
                loops = (chunks - 1) // 2
                per = {hsp: 6, lsp: 6, silr: 2, acr: 4, ahr: 2, asp: 2}
                if extra:
                    per.update({accd: 12, usedd: 4})
                with looped(dve, loops, per) as it:
                    for r in range(2):
                        chunk(it * 2 + (r + 1), 3 * r)
                        if extra:
                            extra(r, it)
                n[0] += 6 * loops
                for q in range(chunks - 1 - 2 * loops):
                    chunk(2 * loops + 1 + q, 0)
                    n[0] += 3
                low_part()

            def ada_in_loop(r, it):
                ada(1, r, ft_acc[:, bass.ds(it * 2 + r, 1), :].rearrange("p a n -> p (a n)"), it)

            ffn("ffn0", NFF, lambda t, c: 1.0, ada_in_loop)
            for c in (10, 11):
                ada(1, c, acc_of(1, c))
            ahead(PLAN["win"])
            add_gated(1, "win")
            mod_cols(1, 0)
            mod_cols(1, 1)
            dve.wait_ge(row_loaded, 64)
            mod_gate(0)
            mod_gate(1)
            rms_apply()
            transposed_mod(0)

            evac, ptk = Count(lin_evac), Count(lin_taken)
            evac.n = 6
            cu = FT[:, 0:8, :]
            cy = FT[:, 8:16, :]
            for c in range(6):
                ahead(PLAN["win"] + 2 * c + 1)
                dve.wait_ge(lin_evac, evac.up())
                if c in (2, 3):
                    f = cu[:, 4 * (c - 2):4 * (c - 1), :].rearrange("p k t -> p (k t)")
                    dve.tensor_tensor(f, f, Z[:, 1024 * (c % 2):1024 * (c % 2) + 1024], ALU.mult).then_inc(lin_taken, 1)
                    dve.wait_ge(lin_taken, ptk.up())
                    for k in range(4 * (c - 2), 4 * (c - 1)):
                        w = lambda j: cols[:, C_CONV + 8 * j + k:C_CONV + 8 * j + k + 1]
                        dve.tensor_scalar(cy[:, k, :], cu[:, k, :], w(2), None, ALU.mult).then_inc(dve_step, 1)
                        dve.wait_ge(dve_step, step.up())
                        dve.scalar_tensor_tensor(cy[:, k, 1:S], cu[:, k, 0:S - 1], w(1), cy[:, k, 1:S], ALU.mult, ALU.add).then_inc(dve_step, 1)
                        dve.wait_ge(dve_step, step.up())
                        dve.scalar_tensor_tensor(cy[:, k, 2:S], cu[:, k, 0:S - 2], w(0), cy[:, k, 2:S], ALU.mult, ALU.add).then_inc(dve_step, 1)
                        dve.wait_ge(dve_step, step.up())
                if c >= 4:
                    z = Z[:, 1024 * (c % 2):1024 * (c % 2) + 1024]
                    dve.tensor_tensor(z, z, cy[:, 4 * (c - 4):4 * (c - 3), :].rearrange("p k t -> p (k t)"), ALU.mult).then_inc(lin_taken, 1)
                    dve.wait_ge(lin_taken, ptk.up())
            ahead(PLAN["wout"])
            for g in range(2):
                dve.wait_ge(hh_ready, hhr.up())
                dve.tensor_tensor(hl[:, 4 * g:4 * g + 4, :], Z[:, 1024 * g:1024 * g + 1024].rearrange("p (k t) -> p k t", k=4),
                                            hh[:, 4 * g:4 * g + 4, :].bitcast(F32), ALU.subtract).then_inc(h_ready, 1)
                hr.up()
            wo("wout")
            add_gated(0, "ffn1")
            rms_apply()
            transposed_mod(1)
            ffn("ffn1", NFF, lambda t, c: 1.0)
            ahead(PLAN["mem"])
            add_gated(1, "mem")

            transposed_plain()
            for l in range(DEPTH):
                ahead(PLAN["mem"] + 2 * l + 1)
            ahead(PLAN["a_in"])
            transposed_plain()
            for c in range(7):
                ahead(PLAN["a_in"] + 2 * c + 1)
            ahead(PLAN["wo1"])
            heads(MEM[0])

            exr, dkr, dkd = Count(exp_ready), Count(qk_in), Count(dk_ready)
            levs, levt = Count(lev_scores), Count(lev_taken)
            q, f, kk, g = FT[:, 0:6, :], FT[:, 6:12, :], FT[:, 6:12, :], FT[:, 12:18, :]
            scale = P ** -0.5
            dve.memset(scT, 0.0).then_inc(dve_step, 1)
            dve.wait_ge(dve_step, step.up())
            dve.tensor_scalar(qd, q, scale, None, ALU.mult).then_inc(dve_step, 1)
            dve.wait_ge(dve_step, step.up())
            dve.scalar_tensor_tensor(kd, f, -1.0, f, ALU.mult, ALU.min).then_inc(qk_in, 1)
            dve.wait_ge(qk_in, dkr.up())
            dve.wait_ge(exp_ready, exr.up())
            dve.scalar_tensor_tensor(pfx, f, 0.0, kd, ALU.min, ALU.subtract).then_inc(dve_step, 1)
            dve.wait_ge(dve_step, step.up())
            dve.scalar_tensor_tensor(sfx, f, 0.0, kd, ALU.max, ALU.add).then_inc(qk_in, 1)
            dve.wait_ge(qk_in, dkr.up())
            dve.wait_ge(exp_ready, exr.up())
            dve.tensor_copy(kd, kk).then_inc(dk_ready, 1)
            dve.wait_ge(dk_ready, dkd.up())
            dve.memset(sfx, 0.0).then_inc(qk_in, 1)
            dve.wait_ge(qk_in, dkr.up())
            diag = scT.rearrange("p h (c t) -> p h c t", c=3)[:, :, 0:3:2, :]
            for l in range(9):
                if l:
                    dve.wait_ge(exp_ready, exr.up())
                    dve.scalar_tensor_tensor(qd, qd, scale, q, ALU.mult, ALU.mult).then_inc(dve_step, 1)
                    dve.wait_ge(dve_step, step.up())
                    dve.tensor_tensor(kd, kd, kk, ALU.mult).then_inc(dk_ready, 1)
                    dve.wait_ge(dk_ready, dkd.up())
                    if l < 8:
                        m = 2 ** (l - 1)
                        pv = pfx.rearrange("p h (b c m) -> p (h b) c m", c=2, m=m)
                        sv = sfx.rearrange("p h (b c m) -> p (h b) c m", c=2, m=m)
                        nb = HG * S // (2 * m)
                        dve.tensor_tensor(sv[:, :, 0, :], sv[:, :, 0, :],
                                             pv[:, :, 1, m - 1:m].to_broadcast([P, nb, m]), ALU.add).then_inc(dve_step, 1)
                        dve.wait_ge(dve_step, step.up())
                        dve.tensor_tensor(pv[:, :, 1, :], pv[:, :, 1, :],
                                             pv[:, :, 0, m - 1:m].to_broadcast([P, nb, m]), ALU.add).then_inc(qk_in, 1)
                        dve.wait_ge(qk_in, dkr.up())
                dve.wait_ge(lev_scores, levs.up())
                if l < 8:
                    for h in range(HG):
                        i = dve.copy_predicated(scT[:, h, :].rearrange("p (c t) -> p c t", c=3)[:, 0:3:2, :],
                                                mlev[:, l:l + 1, :].to_broadcast([P, 2, P]),
                                                ps[:, 4 + h // 2, 256 * (h % 2):256 * (h % 2) + 256].rearrange("p (c t) -> p c t", c=2))
                        i.then_inc(lev_taken if h == HG - 1 else dve_step, 1)
                        dve.wait_ge(lev_taken if h == HG - 1 else dve_step, (levt if h == HG - 1 else step).up())
                else:
                    dve.tensor_copy(scT.rearrange("p h (c t) -> p h c t", c=3)[:, :, 1, :],
                                                   ps[:, 4:6, :].rearrange("p a b -> p (a b)")[:, 0:HG * P].rearrange("p (h t) -> p h t", h=HG)).then_inc(lev_taken, 1)
                    dve.wait_ge(lev_taken, levt.up())
            dve.wait_ge(rs_ready, rsr.up())
            exr.n += 1
            for h in range(HG):
                dve.scalar_tensor_tensor(pfx[:, h, :], pfx[:, h, :], cols[:, C_GN + h:C_GN + h + 1], kd[:, h, :],
                                            ALU.mult, ALU.mult).then_inc(dve_step, 1)
                dve.wait_ge(dve_step, step.up())
            dve.tensor_tensor(sfx, pfx, g, ALU.mult).then_inc(v_ready, 1)
            dve.wait_ge(v_ready, v.up())
            dve.wait_ge(hh_ready, hhr.up())
            dve.tensor_tensor(hl[:, 0:6, :], sfx, hh[:, 0:6, :].bitcast(F32), ALU.subtract).then_inc(ol_ready, 1)
            dve.wait_ge(ol_ready, olr.up())

            def post_norm(after, rows_need):
                dve.wait_ge(unit_used, PLAN[after])
                for t in range(TT):
                    x2 = xs[:, t, :].rearrange("p (a n) -> p a n", a=2)
                    dve.scalar_tensor_tensor(x2, x2, ALPHA, ps[:, 4 + t:8:2, :], ALU.mult, ALU.add).then_inc(dve_step, 1)
                    dve.wait_ge(dve_step, step.up())
                    for a in range(2):
                        dve.bn_stats(st[:, 32 + 12 * t + 6 * a:38 + 12 * t + 6 * a], xs[:, t, a * 512:(a + 1) * 512]).then_inc(dve_step, 1)
                        dve.wait_ge(dve_step, step.up())
                    dve.bn_aggr(st[:, 56 + 2 * t:58 + 2 * t], st[:, 32 + 12 * t:44 + 12 * t]).then_inc(stat_ready if t else dve_step, 1)
                    dve.wait_ge(stat_ready if t else dve_step, (stat if t else step).up())
                dve.wait_ge(rstd_ready, rstd.up())
                dve.wait_ge(row_loaded, rows_need)
                for t in range(TT):
                    x = xs[:, t, :]
                    dve.tensor_scalar(x, x, st[:, 56 + 2 * t:57 + 2 * t], st[:, 4 + t:5 + t], ALU.subtract, ALU.mult).then_inc(dve_step, 1)
                    dve.wait_ge(dve_step, step.up())
                    dve.tensor_tensor(x, x, lnv[:, 0, :], ALU.mult).then_inc(dve_step, 1)
                    dve.wait_ge(dve_step, step.up())
                    dve.tensor_tensor(x, x, lnv[:, 1, :], ALU.add).then_inc(x_ready if t else dve_step, 1)
                    dve.wait_ge(x_ready if t else dve_step, (xrd if t else step).up())

            rin, rsum = Count(router_ready), Count(router_sums)

            def router():
                dve.wait_ge(router_sums, rsum.up())
                N = 2 * 5
                lg = rt[:, 0:40]
                g3 = lambda a: a.rearrange("p (g e) -> p g e", e=4)
                for t in range(TT):
                    dve.tensor_tensor(lg[:, 20 * t:20 * t + 20], ps[:, 7, 20 * t:20 * t + 20], rbias, ALU.add).then_inc(dve_step, 1)
                    dve.wait_ge(dve_step, step.up())
                mx, ex = rt[:, 48:58], rt[:, 64:104]
                dve.tensor_reduce(mx, g3(lg), AX.X, ALU.max).then_inc(dve_step, 1)
                dve.wait_ge(dve_step, step.up())
                dve.tensor_tensor(g3(ex), g3(lg), mx.unsqueeze(2).to_broadcast([P, N, 4]), ALU.subtract).then_inc(router_ready, 1)
                dve.wait_ge(router_ready, rin.up())
                rank, cmp_ = rt[:, 112:152], rt[:, 160:200]
                dve.memset(rank, 0.0).then_inc(dve_step, 1)
                dve.wait_ge(dve_step, step.up())
                for j in range(4):
                    other = g3(lg)[:, :, j:j + 1].to_broadcast([P, N, 4])
                    dve.tensor_tensor(g3(cmp_), other, g3(lg), ALU.is_gt).then_inc(dve_step, 1)
                    dve.wait_ge(dve_step, step.up())
                    dve.tensor_tensor(rank, rank, cmp_, ALU.add).then_inc(dve_step, 1)
                    dve.wait_ge(dve_step, step.up())
                    if j < 3:
                        dve.tensor_tensor(g3(cmp_)[:, :, j + 1:4], other[:, :, 0:3 - j], g3(lg)[:, :, j + 1:4], ALU.is_equal).then_inc(dve_step, 1)
                        dve.wait_ge(dve_step, step.up())
                        dve.tensor_tensor(g3(rank)[:, :, j + 1:4], g3(rank)[:, :, j + 1:4], g3(cmp_)[:, :, j + 1:4], ALU.add).then_inc(dve_step, 1)
                        dve.wait_ge(dve_step, step.up())
                best, sums = rt[:, 208:248], rt[:, 256:266]
                dve.wait_ge(exp_ready, exr.up())
                dve.tensor_reduce(sums, g3(ex), AX.X, ALU.add).then_inc(dve_step, 1)
                dve.wait_ge(dve_step, step.up())
                dve.tensor_scalar(best, rank, 2.0, None, ALU.is_lt).then_inc(dve_step, 1)
                dve.wait_ge(dve_step, step.up())
                dve.tensor_tensor(best, best, ex, ALU.mult).then_inc(dve_step, 1)
                dve.wait_ge(dve_step, step.up())
                dve.tensor_reduce(mx, g3(best), AX.X, ALU.add).then_inc(dve_step, 1)
                dve.wait_ge(dve_step, step.up())
                dve.reciprocal(mx, mx).then_inc(dve_step, 1)
                dve.wait_ge(dve_step, step.up())
                dve.reciprocal(sums, sums).then_inc(dve_step, 1)
                dve.wait_ge(dve_step, step.up())
                dve.tensor_scalar(rank, rank, 1.0, None, ALU.is_lt).then_inc(dve_step, 1)
                dve.wait_ge(dve_step, step.up())
                for t in range(TT):
                    w = rt[:, 272 + 4 * t:276 + 4 * t]
                    dve.tensor_scalar(w, rank[:, 20 * t:20 * t + 4], sums[:, 5 * t:5 * t + 1], None, ALU.mult).then_inc(dve_step, 1)
                    dve.wait_ge(dve_step, step.up())
                    dve.tensor_tensor(w, w, mx[:, 5 * t + 1:5 * t + 5], ALU.mult).then_inc(dve_step, 1)
                    dve.wait_ge(dve_step, step.up())
                    dve.tensor_tensor(g3(gate[:, t, :]), g3(best[:, 20 * t + 4:20 * t + 20]),
                                         w.unsqueeze(2).to_broadcast([P, 4, 4]), ALU.mult).then_inc(dve_step, 1)
                    dve.wait_ge(dve_step, step.up())

            def expert_gate(t, e):
                if isinstance(e, int):
                    return gate[:, t, e:e + 1]
                return gate[:, t, bass.ds(e, 1)]

            wo("wo1")
            post_norm("moe0", 176)
            transposed_plain()
            router()
            ffn("moe0", NEXP, expert_gate)
            ahead(PLAN["kv"])
            post_norm("kv", 208)
            transposed_plain()
            for c in range(4):
                ahead(PLAN["kv"] + 2 * c + 1)
            for c in range(2):
                ahead(PLAN["b_in"] + 2 * c + 1)
            ahead(PLAN["wo2"])
            heads(MEM[1])
            zr, lr, spr = Count(z_ready), Count(l_ready), Count(sp_ready)
            rr, lar, ar, amr = Count(rest_ready), Count(la_ready), Count(a_ready), Count(am_ready)

            def sb_buf(kind, b):
                return Z[:, (2 * kind + b) * 512:(2 * kind + b) * 512 + 384]

            for i in range(SBH + 2):
                if i >= 2:
                    head_low(dict(row=64 * (i % 2), rows=64, blk=(i - 2) // 2))
                if i < SBH:
                    b = i % 2
                    zb, nb = sb_buf(0, b), sb_buf(1, b)
                    dve.wait_ge(s_ready, sr.up())
                    dve.tensor_scalar(zb, ps[:, 4 + b, 0:384], 64 ** -0.5, None, ALU.mult).then_inc(sm_ready, 1)
                    dve.wait_ge(sm_ready, smr.up())
                    dve.scalar_tensor_tensor(nb, zb, -1.0, zb, ALU.mult, ALU.min).then_inc(z_ready, 1)
                    dve.wait_ge(z_ready, zr.up())
                    dve.wait_ge(l_ready, lr.up())
                    dve.scalar_tensor_tensor(nb, zb, 0.0, nb, ALU.max, ALU.add).then_inc(dve_step, 1)
                    dve.wait_ge(dve_step, step.up())
                    dve.tensor_tensor(nb, nb, mstrict, ALU.mult).then_inc(sp_ready, 1)
                    dve.wait_ge(sp_ready, spr.up())
                if 0 <= i - 1 < SBH:
                    b = (i - 1) % 2
                    zb, nb = sb_buf(0, b), sb_buf(1, b)
                    dve.wait_ge(rest_ready, rr.up())
                    dve.scalar_tensor_tensor(nb, ps[:, 6, 0:384], -1.0, zb, ALU.mult, ALU.add).then_inc(dve_step, 1)
                    dve.wait_ge(dve_step, step.up())
                    dve.tensor_scalar(nb, nb, 0.0, None, ALU.min).then_inc(la_ready, 1)
                    dve.wait_ge(la_ready, lar.up())
                    dve.wait_ge(a_ready, ar.up())
                    dve.tensor_tensor(nb, nb, mstrict, ALU.mult).then_inc(am_ready, 1)
                    dve.wait_ge(am_ready, amr.up())
            wo("wo2")
            post_norm("moe1", 304)
            transposed_plain()
            router()
            ffn("moe1", NEXP, expert_gate)
            post_norm("end", 336)

        @block.tensor
        def _(pe):
            lsp, used = Count(l_split), Count(unit_used)
            n = [0]

            def mm3(o, h1, l1, h2, l2, start, stop):
                pe.matmul(o, h1, h2, start=start, stop=False, skip_group_check=True)
                pe.matmul(o, h1, l2, start=False, stop=False, skip_group_check=True)
                return pe.matmul(o, l1, h2, start=False, stop=stop, skip_group_check=True)

            def unit_rows(u, bank, k0, w, first, last):
                pe.wait_ge(l_split, lsp.up())
                for t in range(TT):
                    for k in range(UK):
                        tok = slice(t * P, (t + 1) * P)
                        i = mm3(bank(t)[:, 0:w], hh[:, k0 + k, tok], hl[:, k0 + k, tok],
                                wh[u % SPL][:, k, 0:w], wl[u % SPL][:, k, 0:w],
                                first and k == 0, last and k == UK - 1)
                i.then_inc(unit_used, 1)
                used.up()

            def unit_features(u, b0, nb, k0, first, last, signal=True, c0=0):
                for b in range(nb):
                    o = ps[:, b0 + b // 2, (b % 2) * S:(b % 2 + 1) * S]
                    for k in range(UK):
                        cs = slice(c0 + b * P, c0 + (b + 1) * P)
                        i = mm3(o, wh[u % SPL][:, k, cs], wl[u % SPL][:, k, cs], hh[:, k0 + k, :], hl[:, k0 + k, :],
                                first and k == 0 and b % 2 == 0, last and k == UK - 1)
                return i

            evac = Count(lin_evac)
            lin = [0]

            def chunk(kind, w=NC):
                if lin[0] >= 2:
                    pe.wait_ge(lin_evac, evac.up())
                pair = 2 * (lin[0] % 2)
                for q in range(2):
                    if kind == "rows":
                        unit_rows(n[0], lambda t: ps[:, pair + t, :], UK * q, w, q == 0, q == 1)
                    else:
                        pe.wait_ge(l_split, lsp.up())
                        unit_features(n[0], pair, w // P, UK * q, q == 0, q == 1).then_inc(unit_used, 1)
                        used.up()
                    n[0] += 1
                lin[0] += 1

            hr, xrd = Count(h_ready), Count(x_ready)
            olr = Count(ol_ready)

            def out_rows():
                for c in range(2):
                    for q in range(2):
                        unit_rows(n[0], lambda t: ps[:, 4 + 2 * c + t, :], UK * q, NC, q == 0, q == 1)
                        n[0] += 1

            xn, xt = Count(xn_ready), Count(xt_ready)

            def transposes(src):
                for g in range(4):
                    for k in range(2):
                        for t in range(TT):
                            c = (2 * g + k) * P
                            i = pe.transpose(ps[:, 4 + g, k * S + t * P:k * S + (t + 1) * P], src[:, t, c:c + P], ident[:, :])
                    i.then_inc(xt_ready, 1)
                    xt.up()

            usedd, msum, mtk = Count(ada_used), Count(mod_sums), Count(mod_taken)
            ft_acc = FT[:, :, :].rearrange("p (c a) t -> p c (a t)", a=2)

            def acc_of(layer, c):
                if layer == 0:
                    return ft_acc[:, c, :] if c < 4 else accw[:, c - 4, :]
                return ft_acc[:, c, :] if c < 10 else accw[:, c - 10, :]

            def mod_cols(layer, which):
                for c in range(4):
                    for q in range(4):
                        i = pe.matmul(ps[:, 7, 4 * c + q:4 * c + q + 1], acc_of(layer, 6 * which + c)[:, q * P:(q + 1) * P],
                                      ones[:, 0:1], start=True, stop=True)
                i.then_inc(mod_sums, 1)
                msum.up()

            def mod_gate(layer, g):
                for c in range(2):
                    i = pe.matmul(ps[:, 4 + c, :], ones[:, :], acc_of(layer, 6 * g + 4 + c), start=True, stop=True)
                i.then_inc(mod_sums, 1)
                msum.up()

            pe.wait_ge(small_loaded, 96)
            pe.wait_ge(ada_used, usedd.up(8))
            mod_cols(0, 0)
            pe.wait_ge(mod_taken, mtk.up())
            pe.wait_ge(xn_ready, xn.up())
            transposes(tv)
            pe.wait_ge(h_ready, hr.up(4))

            sqs, rsr = Count(sq_sum), Count(rs_ready)

            def square_sums():
                for a in range(2):
                    i = pe.matmul(ps[:, 4 + a, :], ones[:, :], Z[:, a * 512:(a + 1) * 512], start=True, stop=True)
                i.then_inc(sq_sum, 1)
                sqs.up()

            for c in range(6):
                chunk("features" if c < 4 else "rows")
                if 1 <= c <= 4:
                    pe.wait_ge(lin_evac, c)
                    if c >= 2:
                        pe.wait_ge(rs_ready, rsr.up())
                    square_sums()
            pe.wait_ge(lin_evac, 6)

            sr, smr, pr = Count(s_ready), Count(sm_ready), Count(p_ready)
            ptr, pte, orr = Count(pt_ready), Count(pt_evac), Count(o_ready)

            def heads(jobs):
                def scores(j):
                    if j >= 2:
                        pe.wait_ge(sm_ready, smr.up())
                    for c0, c1, a, b in jobs[j]["scores"]:
                        i = pe.matmul(ps[:, 4 + j % 2, c0:c1], a, b, start=True, stop=True)
                    i.then_inc(s_ready, 1)
                    sr.up()

                def turn(j):
                    pe.wait_ge(p_ready, pr.up())
                    if j:
                        pe.wait_ge(pt_evac, pte.value(1))
                    for a, b in jobs[j]["turns"]:
                        i = pe.transpose(ps[:, 6, b:b + P], Z[:, (j % 2) * 512 + a:(j % 2) * 512 + a + P], ident[:, :])
                    i.then_inc(pt_ready, 1)
                    ptr.up()

                def outs(j):
                    pe.wait_ge(pt_evac, pte.up())
                    if j:
                        pe.wait_ge(ol_ready, olr.up())
                    m = jobs[j]
                    for q, (t0, t1, val, c0) in enumerate(m["outs"]):
                        p0 = 1024 + (j % 2) * 512 + c0
                        i = pe.matmul(ps[m["row"]:m["row"] + m["rows"], 7, t0:t1], val, Z[:, p0:p0 + t1 - t0],
                                      start=q == 0, stop=q == len(m["outs"]) - 1, skip_group_check=True)
                    i.then_inc(o_ready, 1)
                    orr.up()

                for i in range(len(jobs) + 2):
                    if i < len(jobs):
                        scores(i)
                    if 0 <= i - 1 < len(jobs):
                        turn(i - 1)
                    if i >= 2:
                        outs(i - 2)
                smr.n += 2
                pe.wait_ge(ol_ready, olr.up())

            nrm = Count(normed)
            pe.wait_ge(normed, nrm.up(4))
            heads(MOBA)
            pe.wait_ge(ada_used, usedd.up(16))
            mod_cols(0, 1)
            mod_gate(0, 0)
            pe.wait_ge(mod_taken, mtk.up(2))
            mod_gate(0, 1)
            pe.wait_ge(mod_taken, mtk.up())
            out_rows()
            pe.wait_ge(xn_ready, xn.up())
            transposes(tv)
            pe.wait_ge(h_ready, hr.up(4))

            acr, atr, asp = Count(act_ready), Count(at_ready), Count(a_split)

            def ffn(ph, chunks):
                def gate_up(j):
                    for q in range(2):
                        pe.wait_ge(l_split, lsp.up())
                        u = n[0] + j + q
                        for t in range(TT):
                            for k in range(UK):
                                tok = slice(t * P, (t + 1) * P)
                                i = mm3(ps[:, t, :], hh[:, UK * q + k, tok], hl[:, UK * q + k, tok],
                                        wh[u % SPL][:, k, :], wl[u % SPL][:, k, :], q == 0 and k == 0, q == 1 and k == UK - 1)
                        i.then_inc(unit_used, 1)
                        used.up()

                def turn():
                    pe.wait_ge(act_ready, acr.up(2))
                    for k in range(2):
                        for t in range(TT):
                            i = pe.transpose(ps[:, 2, k * S + t * P:k * S + (t + 1) * P],
                                             Z[:, 512 + t * FW + k * P:512 + t * FW + (k + 1) * P], ident[:, :])
                    i.then_inc(at_ready, 1)
                    atr.up()

                def down(j, first, last):
                    pe.wait_ge(a_split, asp.up())
                    pe.wait_ge(l_split, lsp.up())
                    u = n[0] + j
                    for t in range(TT):
                        for k in range(2):
                            tok = slice(t * P, (t + 1) * P)
                            for h in range(2):
                                i = mm3(ps[:, 4 + 2 * h + t, :], ah[:, k, tok], al[:, k, tok],
                                        wh[u % SPL][:, 2 * k + h, :], wl[u % SPL][:, 2 * k + h, :],
                                        first and k == 0, last and k == 1)
                    i.then_inc(unit_used, 1)
                    used.up()

                gate_up(0)
                n[0] += 2
                turn()
                gate_up(0)
                down(2, True, False)
                n[0] += 3
                turn()
                gate_up(0)
                down(2, False, False)
                n[0] += 3
                loops, rest = divmod(chunks - 3, 2)
                with looped(pe, loops, {lsp: 6, used: 6, acr: 4, atr: 2, asp: 2}):
                    for r in range(2):
                        turn()
                        gate_up(3 * r)
                        down(3 * r + 2, False, False)
                n[0] += 6 * loops
                for _ in range(rest):
                    turn()
                    gate_up(0)
                    down(2, False, False)
                    n[0] += 3
                turn()
                down(0, False, True)
                n[0] += 1


            ffn("ffn0", NFF)
            pe.wait_ge(ada_used, usedd.up(24))
            pe.wait_ge(x_ready, 2)
            mod_cols(1, 0)
            pe.wait_ge(mod_taken, mtk.up())
            mod_cols(1, 1)
            mod_gate(1, 0)
            pe.wait_ge(mod_taken, mtk.up(2))
            mod_gate(1, 1)
            pe.wait_ge(mod_taken, mtk.up())
            pe.wait_ge(xn_ready, xn.up())
            transposes(tv)
            pe.wait_ge(h_ready, hr.up(4))
            for c in range(6):
                chunk("features")
            pe.wait_ge(h_ready, hr.up(2))
            out_rows()
            pe.wait_ge(xn_ready, xn.up())
            transposes(tv)
            pe.wait_ge(h_ready, hr.up(4))
            ffn("ffn1", NFF)

            pe.wait_ge(x_ready, 4)
            pe.wait_ge(mem_loaded, 16)
            transposes(tv)
            pe.wait_ge(h_ready, hr.up(4))
            for l in range(DEPTH):
                if True:
                    pe.wait_ge(lin_evac, evac.up())
                pair = 2 * (lin[0] % 2)
                for q in range(2):
                    pe.wait_ge(l_split, lsp.up())
                    unit_features(n[0], pair, 2, UK * q, q == 0, q == 1)
                    for t in range(TT):
                        for k in range(UK):
                            tok = slice(t * P, (t + 1) * P)
                            u = n[0]
                            i = mm3(ps[:, pair + 1, t * S:(t + 1) * S], hh[:, UK * q + k, tok], hl[:, UK * q + k, tok],
                                    wh[u % SPL][:, k, 256:512], wl[u % SPL][:, k, 256:512],
                                    q == 0 and k == 0 and t == 0, q == 1 and k == UK - 1)
                    i.then_inc(unit_used, 1)
                    used.up()
                    n[0] += 1
                lin[0] += 1
            transposes(xs)
            pe.wait_ge(h_ready, hr.up(4))
            for kind, w in (("features", 512), ("features", 512), ("features", 512), ("rows", 512), ("rows", 256),
                            ("features", 512), ("features", 512)):
                chunk(kind, w)
            pe.wait_ge(lin_evac, lin[0])
            heads(MEM[0])

            dkd, exr = Count(dk_ready), Count(exp_ready)
            levs, levt = Count(lev_scores), Count(lev_taken)
            for l in range(9):
                pe.wait_ge(dk_ready, dkd.up())
                if l:
                    pe.wait_ge(lev_taken, levt.up())
                for h in range(HG):
                    if l < 8:
                        for t in range(TT):
                            tok = slice(t * P, (t + 1) * P)
                            c = (h % 2) * S + t * P
                            i = pe.matmul(ps[:, 4 + h // 2, c:c + P], kd[:, h, tok], qd[:, h, tok], start=True, stop=True)
                    else:
                        i = pe.matmul(ps[:, 4 + h // 4, (h % 4) * P:(h % 4 + 1) * P], kd[:, h, 0:P], qd[:, h, P:S],
                                      start=True, stop=True)
                i.then_inc(lev_scores, 1)
                levs.up()
            pe.wait_ge(lev_taken, levt.up())
            for h in range(HG):
                o = ps[:, 4 + h // 2, (h % 2) * S:(h % 2 + 1) * S]
                pe.matmul(o, tv[:, 0, h * P:(h + 1) * P], scT[:, h, 0:S], start=True, stop=False, skip_group_check=True)
                i = pe.matmul(o[:, P:S], tv[:, 1, h * P:(h + 1) * P], scT[:, h, S:S + P], start=False, stop=True,
                              skip_group_check=True)
            i.then_inc(o_ready, 1)
            orr.up()
            exr.n = 10
            pe.wait_ge(exp_ready, exr.up())
            for a in range(3):
                i = pe.matmul(ps[:, 4 + a, :], ones[:, :], qd[:, 2 * a:2 * a + 2, :].rearrange("p a t -> p (a t)"), start=True, stop=True)
            i.then_inc(sq_sum, 1)
            sqs.up()
            pe.wait_ge(ol_ready, olr.up())
            out_rows()

            def after_norm(count):
                pe.wait_ge(x_ready, count)
                transposes(xs)
                pe.wait_ge(h_ready, hr.up(4))

            def router(rows_need):
                pe.wait_ge(row_loaded, rows_need)
                for t in range(TT):
                    tok = slice(t * P, (t + 1) * P)
                    for k in range(KT):
                        for half in (hh, hl):
                            i = pe.matmul(ps[:, 7, 20 * t:20 * t + 20], half[:, k, tok].bitcast(F32), rw[:, k, :],
                                          start=k == 0 and half is hh, stop=k == KT - 1 and half is hl,
                                          skip_group_check=True)
                i.then_inc(router_sums, 1)
                rsum.up()

            rsum = Count(router_sums)
            after_norm(5)
            router(176)
            ffn("moe0", NEXP)
            after_norm(6)
            for kind, w in (("features", 512), ("features", 256), ("rows", 512), ("rows", 256)):
                chunk(kind, w)
            for c in range(2):
                chunk("features")
            pe.wait_ge(lin_evac, lin[0])
            heads(MEM[1])

            rr, spr, amr = Count(rest_ready), Count(sp_ready), Count(am_ready)
            lar = Count(la_ready)
            for i in range(SBH + 2):
                if i >= 2:
                    h, b = i - 2, i % 2
                    nb = Z[:, (2 + b) * 512:(2 + b) * 512 + 384]
                    pe.wait_ge(am_ready, amr.up())
                    if i >= 3:
                        pe.wait_ge(ol_ready, olr.up())
                    o = ps[64 * (h % 2):64 * (h % 2) + 64, 7, 0:S]
                    pe.matmul(o, tv[:, 0, 64 * h:64 * h + 64], nb[:, 0:S], start=True, stop=False, skip_group_check=True)
                    pe.matmul(o[:, P:S], tv[:, 1, 64 * h:64 * h + 64], nb[:, S:S + P], start=False, stop=True,
                                         skip_group_check=True).then_inc(o_ready, 1)
                    orr.up()
                if i < SBH:
                    h, b = i, i % 2
                    r = slice(64 * (h % 2), 64 * (h % 2) + 64)
                    q, k = FT[r, h // 2, :], FT[r, 6 + h // 2, :]
                    if i >= 2:
                        pe.wait_ge(sm_ready, smr.up())
                    pe.matmul(ps[:, 4 + b, 0:S], k[:, 0:P], q[:, :], start=True, stop=True)
                    pe.matmul(ps[:, 4 + b, S:S + P], k[:, P:S], q[:, P:S], start=True, stop=True).then_inc(s_ready, 1)
                    sr.up()
                if 0 <= i - 1 < SBH:
                    b = (i - 1) % 2
                    nb = Z[:, (2 + b) * 512:(2 + b) * 512 + 384]
                    pe.wait_ge(sp_ready, spr.up())
                    if i >= 2:
                        pe.wait_ge(la_ready, lar.up())
                    pe.matmul(ps[:, 6, 0:S], tri[:, :], nb[:, 0:S], start=True, stop=False, skip_group_check=True)
                    pe.matmul(ps[:, 6, P:S], ones[:, :], nb[:, S:S + P], start=False, stop=True, skip_group_check=True)
                    pe.matmul(ps[:, 6, S:S + P], tri[:, :], nb[:, S:S + P], start=True, stop=True, skip_group_check=True).then_inc(rest_ready, 1)
                    rr.up()
            pe.wait_ge(ol_ready, olr.up())
            out_rows()
            after_norm(7)
            router(304)
            ffn("moe1", NEXP)


_INS = ["x", "w_ada", "b_ada", "w_qkv", "w_o", "w_in", "w_out", "w_gate_up", "w_down", "mem_2", "a_w_in_2", "b_w_in_2",
        "w_kv_shared_2", "w_mem_kv_2", "w_o_2", "ln_mix_g_2", "ln_mix_b_2", "ln_ffn_g_2", "ln_ffn_b_2", "w_group_2",
        "b_group_2", "w_router_2", "b_router_2", "w_gate_2", "w_up_2", "w_down_2"]


def kernel(**inputs):
    import numpy as _np
    import concourse.bacc as _bacc
    from concourse import mybir as _mybir
    from concourse.bass_utils import run_bass_kernel_spmd as _run

    give = {name: _np.ascontiguousarray(inputs[name]) for name in _INS}
    give["cols"] = _np.ascontiguousarray(_np.concatenate(
        [_np.asarray(inputs[name]).reshape(-1, 128) for name in
         ("c", "norm_mix", "norm_ffn", "conv_w", "q_gain", "k_gain", "a_gnorm_2", "b_ada")]).T)
    i = _np.arange(128)
    give["k_ident"] = _np.eye(128, dtype=_np.float32)
    give["k_ones"] = _np.ones((128, 128), _np.float32)
    give["k_tri"] = (i[:, None] >= i[None, :]).astype(_np.float32)
    causal = _np.where(i[:, None] >= i[None, :], 0.0, -1e30).astype(_np.float32)
    give["k_causal"] = _np.concatenate([causal, _np.zeros_like(causal), causal], axis=1)
    strict = (i[:, None] < i[None, :]).astype(_np.float32)
    give["k_strict"] = _np.concatenate([strict, _np.ones_like(strict), strict], axis=1)
    levels = [i[:, None] == i[None, :]]
    for m in (1, 2, 4, 8, 16, 32, 64):
        same = (i[:, None] // (2 * m)) == (i[None, :] // (2 * m))
        levels.append(same & ((i[:, None] // m) % 2 == 0) & ((i[None, :] // m) % 2 == 1))
    give["k_levels"] = _np.stack(levels, axis=1).reshape(128, 8 * 128).astype(_np.float32)

    nc = _bacc.Bacc("TRN2", target_bir_lowering=False, num_devices=1)
    arrays = {f"in_{name}": a for name, a in give.items()}
    A = {name: nc.dram_tensor(f"in_{name}", a.shape, _mybir.dt.from_np(a.dtype), kind="ExternalInput").ap()
         for name, a in give.items()}
    out = nc.dram_tensor("out_0", (1, S, D), _mybir.dt.float32, kind="ExternalOutput").ap()
    build(nc, A, out)
    r = _run(nc, [arrays], core_ids=[0])
    return r.results[0]["out_0"]
```

```python
from contextlib import ExitStack, contextmanager

import concourse.bass as bass
from concourse import mybir

F32 = mybir.dt.float32
F32R = mybir.dt.float32r
U8 = mybir.dt.uint8
ALU = mybir.AluOpType
ACT = mybir.ActivationFunctionType
AX = mybir.AxisListType

P = 128
S = 256
TT = S // P
D = 1024
KT = D // P
NC = 512
UK = 4
RAW = 6
SPL = 3
DEPTH = 2
HEADS = 8
FF = 2816
FW = 256
NFF = FF // FW
NEXP = 16
MIX = 768
HG = MIX // P
SBH = MIX // 64
EPS = 1e-6
LN_EPS = 1e-5
ALPHA = (2 * DEPTH) ** 0.25


class Count:

    def __init__(self, sem):
        self.sem, self.n, self.per, self.it = sem, 0, 0, None

    def value(self, ahead=0):
        return self.n + ahead if self.it is None else self.it * self.per + (self.n + ahead)

    def up(self, by=1):
        self.n += by
        return self.value()


@contextmanager
def looped(eng, times, counts):
    base = {c: c.n for c in counts}
    with eng.Fori(0, times, 1) as it:
        for c, per in counts.items():
            c.per, c.it = per, it
        yield it
    for c, per in counts.items():
        assert c.n == base[c] + per, (c.sem, c.n, base[c], per)
        c.n, c.per, c.it = base[c] + per * times, 0, None


def narrow_units():
    out = {}
    for name, ws in (("a_in", (512, 512, 512, 512, 256, 512, 512)), ("kv", (512, 256, 512, 256))):
        for i, w in enumerate(ws):
            if w < NC:
                out[PLAN[name] + 2 * i] = out[PLAN[name] + 2 * i + 1] = w
    return out


def stream_plan():
    at, plan = 0, {}
    for name, units in (("qkv", 12), ("wo0", 4), ("ffn0", 3 * NFF), ("win", 12), ("wout", 4), ("ffn1", 3 * NFF),
                        ("mem", 4), ("a_in", 14), ("wo1", 4), ("moe0", 3 * NEXP), ("kv", 8), ("b_in", 4),
                        ("wo2", 4), ("moe1", 3 * NEXP)):
        plan[name] = at
        at += units
    plan["end"] = at
    return plan


PLAN = stream_plan()

C_C, C_NMIX, C_NFFN, C_CONV, C_QG, C_KG, C_GN, C_BADA = 0, 8, 24, 40, 64, 65, 66, 72
NCOL = 168


def build(nc, A, out):
    ctx = ExitStack()
    with ctx:
        def sb(name, shape, dt=F32):
            return ctx.enter_context(nc.sbuf_tensor(name, shape, dt))

        def sem(name):
            return ctx.enter_context(nc.semaphore(name))

        raw = [sb(f"raw{i}", [P, UK, NC]) for i in range(RAW)]
        wh = [sb(f"w_high{i}", [P, UK, NC], F32R) for i in range(SPL)]
        wl = [sb(f"w_low{i}", [P, UK, NC], F32R) for i in range(SPL)]
        xs = sb("x_rows", [P, TT, D])
        hh = sb("h_high", [P, KT, S], F32R)
        hl = sb("h_low", [P, KT, S], F32R)
        FT = sb("features", [P, 20, S])
        tv = sb("rows", [P, TT, D])
        W = sb("scratch", [P, 41 * 256])
        Z = sb("small", [P, 8 * 256])
        ah = sb("act_high", [P, 2, S], F32R)
        al = sb("act_low", [P, 2, S], F32R)
        ident = sb("ident", [P, P])
        ones = sb("ones", [P, P])
        ntri = sb("minus_tri", [P, P])
        mcausal = sb("mask_causal", [P, P])
        mlev = sb("mask_levels", [P, 8, P], U8)
        cols = sb("cols", [P, NCOL])
        scol = sb("silu_c", [P, 8])
        modA = sb("mod_scale", [P, 16])
        modB = sb("mod_shift", [P, 16])
        st = sb("stats", [P, 64])
        gate = sb("gates", [P, TT, NEXP])

        cring = W[:, 0:16 * 256].rearrange("p (s k n) -> p s k n", s=2, k=UK)
        accw = W[:, 16 * 256:32 * 256].rearrange("p (c n) -> p c n", n=NC)
        gb = W[:, 32 * 256:40 * 256].rearrange("p (g n) -> p g n", g=2)
        pfx = W[:, 0:6 * 256].rearrange("p (h t) -> p h t", h=HG)
        sfx = W[:, 6 * 256:12 * 256].rearrange("p (h t) -> p h t", h=HG)
        qd = W[:, 12 * 256:18 * 256].rearrange("p (h t) -> p h t", h=HG)
        kd = W[:, 18 * 256:24 * 256].rearrange("p (h t) -> p h t", h=HG)
        scD = W[:, 24 * 256:30 * 256].rearrange("p (h t) -> p h t", h=HG)
        scX = W[:, 30 * 256:33 * 256].rearrange("p (h t) -> p h t", h=HG)
        nstrict = W[:, 24 * 256:24 * 256 + 384]
        nones = W[:, 26 * 256:26 * 256 + P]
        mk = W[:, 33 * 256:37 * 256].rearrange("p (l b m) -> p l b m", l=2, b=2)
        mv = W[:, 37 * 256:41 * 256].rearrange("p (l t n) -> p l t n", l=2, t=2)
        lnv = W[:, 0:8 * 256].rearrange("p (g n) -> p g n", g=2)
        mstrict = W[:, 8 * 256:8 * 256 + 384]
        rw = W[:, 10 * 256:10 * 256 + 160].rearrange("p (k n) -> p k n", k=KT)
        rbias = W[:, 11 * 256:11 * 256 + 20]
        rt = W[:, 12 * 256:20 * 256]

        ps = ctx.enter_context(nc.psum_tensor("ps", [P, 8, 512], F32))

        raw_loaded = [sem(f"raw_loaded{i}") for i in range(RAW)]
        small_loaded = sem("small_loaded")
        x_loaded = sem("x_loaded")
        ada_loaded = [sem(f"ada_loaded{i}") for i in range(2)]
        row_loaded = sem("row_loaded")
        mem_loaded = sem("mem_loaded")
        h_split = sem("h_split")
        l_split = sem("l_split")
        unit_used = sem("unit_used")
        act_step = sem("act_step")
        dve_step = sem("dve_step")
        ada_used = sem("ada_used")
        ada_acc = sem("ada_acc")
        sc_ready = sem("sc_ready")
        mod_sums = sem("mod_sums")
        mod_taken = sem("mod_taken")
        rstd_ready = sem("rstd_ready")
        stat_ready = sem("stat_ready")
        xn_ready = sem("xn_ready")
        xt_ready = sem("xt_ready")
        v_ready = sem("v_ready")
        hh_ready = sem("hh_ready")
        h_ready = sem("h_ready")
        lin_evac = sem("lin_evac")
        lin_taken = sem("lin_taken")
        sq_sum = sem("sq_sum")
        rs_ready = sem("rs_ready")
        normed = sem("normed")
        x_ready = sem("x_ready")
        s_ready = sem("s_ready")
        nmax_ready = sem("nmax_ready")
        e_ready = sem("e_ready")
        p_ready = sem("p_ready")
        pt_ready = sem("pt_ready")
        pt_evac = sem("pt_evac")
        o_ready = sem("o_ready")
        oh_ready = sem("oh_ready")
        ol_ready = sem("ol_ready")
        l_ready = sem("l_ready")
        sp_ready = sem("sp_ready")
        rest_ready = sem("rest_ready")
        la_ready = sem("la_ready")
        a_ready = sem("a_ready")
        sil_ready = sem("sil_ready")
        act_ready = sem("act_ready")
        at_ready = sem("at_ready")
        ah_ready = sem("ah_ready")
        a_split = sem("a_split")
        qk_in = sem("qk_in")
        dk_ready = sem("dk_ready")
        lev_scores = sem("lev_scores")
        lev_taken = sem("lev_taken")
        exp_ready = sem("exp_ready")
        router_ready = sem("router_ready")
        router_sums = sem("router_sums")
        kd_ready = sem("kd_ready")
        sums_ready = sem("sums_ready")
        pool_step = sem("pool_step")
        out_done = sem("out_done")

        block = ctx.enter_context(nc.Block())

        used_until = PLAN["end"]

        def moba_wave(w):
            heads = []
            for h in (2 * w, 2 * w + 1):
                q, k, v = FT[:, h, :], FT[:, 8 + h, :], tv[:, :, h * P:(h + 1) * P]
                heads.append(dict(
                    scores=((0, P, q[:, 0:P], k[:, 0:P]), (P, 3 * P, q[:, P:S], k[:, 0:S])),
                    masked=(0, 2 * P), outs=((0, S, v[:, 0, :], 0), (P, S, v[:, 1, :], 2 * P))))
            return dict(heads=heads, w=3 * P, spans=((0, P), (P, 3 * P)), turns=((0, 0), (P, P), (2 * P, 2 * P)),
                        blk=2 * w, nb=2, rows=P)

        def mem_wave(l, w):
            heads = []
            for a in range(2):
                r = slice(64 * a, 64 * a + 64)
                q, k = FT[r, 18 + w, :], mk[r, l, w, :]
                v = mv[:, l, :, 128 * w + 64 * a:128 * w + 64 * a + 64]
                heads.append(dict(
                    scores=((0, S, q[:, 0:P], k), (S, 2 * S, q[:, P:S], k)), masked=(),
                    outs=((0, S, v[:, 0, :], 0), (0, S, v[:, 1, :], 2 * P))))
            return dict(heads=heads, w=4 * P, spans=((0, S), (S, 2 * S)),
                        turns=((0, 0), (P, 2 * P), (2 * P, P), (3 * P, 3 * P)), blk=HG + w, nb=1, rows=64)

        MOBA = [moba_wave(w) for w in range(HEADS // 2)]
        MEM = [[mem_wave(l, w) for w in range(2)] for l in range(2)]

        def prob(w):
            return Z[:, (w % 2) * 1024:(w % 2 + 1) * 1024].rearrange("p (a c) -> p a c", a=2)

        def turned(w):
            o = 16 * 256 + (w % 2) * 1024
            return W[:, o:o + 1024].rearrange("p (a c) -> p a c", a=2)

        def out_of(w, m):
            return ps[:, 6 + w % 2, 0:S * m["nb"]].rearrange("p (b t) -> p b t", t=S)

        def sb_buf(w):
            return Z[:, (w % 2) * 1024:(w % 2) * 1024 + 768].rearrange("p (a c) -> p a c", a=2)

        def halves(x, m):
            return x.rearrange("p h (b c m) -> p (h b) c m", c=2, m=m)

        def level_exps(m, kind):
            return Z[:, 768 * kind:768 * kind + 768].rearrange("p (b m) -> p b m", m=m)

        @block.sync
        def _(sp):
            xr = A["x"].rearrange("b (t p) d -> p (b t) d", p=P)
            for dst, src in ((cols[:, :], A["cols"]), (ident[:, :], A["k_ident"]), (ones[:, :], A["k_ones"]),
                             (ntri[:, :], A["k_ntri"]), (mcausal[:, :], A["k_causal"]),
                             (Z[:, 0:8 * P], A["k_levels"])):
                sp.dma_start(dst, src).then_inc(small_loaded, 16)
            sp.dma_start(xs[:, :, :], xr).then_inc(x_loaded, 16)

            hsp, lsp = Count(h_split), Count(l_split)
            n = [0]

            def load(src_a, src_b, dst_a, dst_b, j=0):
                u = n[0] + j
                slot = u % RAW
                if u >= RAW or hsp.it is not None:
                    sp.wait_ge(h_split, hsp.up())
                    sp.wait_ge(l_split, lsp.up())
                sp.dma_start(dst_a(raw[slot]), src_a).then_inc(raw_loaded[slot], 16)
                sp.dma_start(dst_b(raw[slot]), src_b).then_inc(raw_loaded[slot], 16)

            def columns(w, c0, width):
                v = w.rearrange("(k p) n -> p k n", p=P)
                for k in (0, UK):
                    load(v[:, k:k + 2, c0:c0 + width], v[:, k + 2:k + 4, c0:c0 + width],
                         lambda r: r[:, 0:2, 0:width], lambda r: r[:, 2:4, 0:width])
                    n[0] += 1

            def gate_up(wg, wu, c0, j):
                g, u = (w.rearrange("(k p) n -> p k n", p=P) for w in (wg, wu))
                for q, k in enumerate((0, UK)):
                    load(g[:, k:k + UK, c0], u[:, k:k + UK, c0],
                         lambda r: r[:, :, 0:FW], lambda r: r[:, :, FW:2 * FW], j + q)

            def down(wd, c0, j):
                d = wd[c0, :].rearrange("(k p) (h n) -> p k h n", p=P, h=2)
                load(d[:, 0, :, :], d[:, 1, :, :], lambda r: r[:, 0:2, :], lambda r: r[:, 2:4, :], j)

            def ffn(chunks, gu, dn):
                gu(0, 0)
                n[0] += 2
                loops, rest = divmod(chunks - 1, 2)
                with looped(sp, loops, {hsp: 6, lsp: 6}) as it:
                    for r in range(2):
                        gu(it * 2 + (r + 1), 3 * r)
                        dn(it * 2 + r, 3 * r + 2)
                n[0] += 6 * loops
                for c in range(2 * loops + 1, chunks):
                    gu(c, 0)
                    dn(c - 1, 2)
                    n[0] += 3
                dn(chunks - 1, 0)
                n[0] += 1

            def dense_ffn(layer):
                w, wd = A["w_gate_up"][layer], A["w_down"][layer]
                ffn(NFF, lambda c, j: gate_up(w[:, 0:FF], w[:, FF:2 * FF], bass.ds(c * FW, FW), j),
                    lambda c, j: down(wd, bass.ds(c * FW, FW), j))

            def moe(layer):
                wg, wu = (A[name][layer].rearrange("e d f -> (e d) f") for name in ("w_gate_2", "w_up_2"))
                wd = A["w_down_2"][layer].rearrange("e f d -> (e f) d")

                def gu(e, j):
                    g, u = (w[bass.ds(e * D, D), :].rearrange("(k p) n -> p k n", p=P) for w in (wg, wu))
                    for q, k in enumerate((0, UK)):
                        load(g[:, k:k + UK, :], u[:, k:k + UK, :],
                             lambda r: r[:, :, 0:FW], lambda r: r[:, :, FW:2 * FW], j + q)
                ffn(NEXP, gu, lambda e, j: down(wd, bass.ds(e * FW, FW), j))

            for c in range(6):
                columns(A["w_qkv"][0], c * NC, NC)
            for c in range(2):
                columns(A["w_o"][0], c * NC, NC)
            dense_ffn(0)
            for c in (2, 3, 4, 5, 0, 1):
                columns(A["w_in"][0], c * NC, NC)
            for c in range(2):
                columns(A["w_out"][0], c * NC, NC)
            dense_ffn(1)
            for l in range(DEPTH):
                columns(A["w_mem_kv_2"][l], 0, NC)
            for c0, w in ((0, 512), (512, 512), (1024, 512), (1536, 512), (2048, 256), (2304, 512), (2816, 512)):
                columns(A["a_w_in_2"][0], c0, w)
            for c in range(2):
                columns(A["w_o_2"][0], c * NC, NC)
            moe(0)
            for c0, w in ((0, 512), (512, 256), (768, 512), (1280, 256)):
                columns(A["w_kv_shared_2"], c0, w)
            for c in range(2):
                columns(A["b_w_in_2"][0], c * NC, NC)
            for c in range(2):
                columns(A["w_o_2"][1], c * NC, NC)
            moe(1)
            xrd = Count(x_ready)
            sp.wait_ge(x_ready, xrd.up(8))
            sp.dma_start(out.rearrange("b (t p) d -> p (b t) d", p=P), xs[:, :, :]).then_inc(out_done, 16)
            sp.wait_ge(out_done, 16)

        @block.gpsimd
        def _(pool):
            used = Count(ada_used)

            def ada(layer):
                v = A["w_ada"][layer].rearrange("(k p) n -> p k n", p=P)

                def chunk(c, first):
                    for q in range(2):
                        if not first:
                            pool.wait_ge(ada_used, used.up())
                        pool.dma_start(cring[:, q, :, :], v[:, q * UK:(q + 1) * UK, bass.ds(c * NC, NC)]) \
                            .then_inc(ada_loaded[q], 16)
                if layer == 0:
                    chunk(0, True)
                    with looped(pool, 11, {used: 2}) as it:
                        chunk(it + 1, False)
                else:
                    with looped(pool, 12, {used: 2}) as it:
                        chunk(it, False)

            def gate_rows(layer):
                for g, c0 in enumerate((2 * D, 5 * D)):
                    pool.dma_start(gb[:, g, :], A["b_ada"][layer:layer + 1, c0:c0 + D].to_broadcast([P, D])) \
                        .then_inc(row_loaded, 16)

            xrd = Count(x_ready)
            gate_rows(0)
            ada(0)
            ada(1)
            pool.wait_ge(x_ready, xrd.up(2))
            gate_rows(1)
            pool.wait_ge(x_ready, xrd.up(2))
            olr = Count(ol_ready)

            def ln_rows(kind, layer):
                pool.dma_start(lnv[:, 0, :], A[f"ln_{kind}_g_2"][layer:layer + 1, :].to_broadcast([P, D])) \
                    .then_inc(row_loaded, 16)
                pool.dma_start(lnv[:, 1, :], A[f"ln_{kind}_b_2"][layer:layer + 1, :].to_broadcast([P, D])) \
                    .then_inc(row_loaded, 16)

            def router_rows(layer):
                pool.dma_start(rw[:, :, 0:4], A["w_group_2"][layer].rearrange("(k p) n -> p k n", p=P)) \
                    .then_inc(row_loaded, 16)
                pool.dma_start(rw[:, :, 4:20], A["w_router_2"][layer].rearrange("(k p) n -> p k n", p=P)) \
                    .then_inc(row_loaded, 16)
                pool.dma_start(rbias[:, 0:4], A["b_group_2"][layer:layer + 1, :].to_broadcast([P, 4])) \
                    .then_inc(row_loaded, 16)
                pool.dma_start(rbias[:, 4:20], A["b_router_2"][layer:layer + 1, :].to_broadcast([P, 16])) \
                    .then_inc(row_loaded, 16)

            pool.dma_start(tv[:, :, :], A["mem_2"].rearrange("b (t p) d -> p (b t) d", p=P)).then_inc(mem_loaded, 16)
            exr, levs = Count(exp_ready), Count(lev_scores)
            kdr, upd, pst = Count(kd_ready), Count(sums_ready), Count(pool_step)
            kk = FT[:, 6:12, :]
            dkr = Count(qk_in)
            dkr.n = 2
            exr.n = 2
            for l in range(1, 9):
                m = 2 ** (l - 1)
                pool.wait_ge(exp_ready, exr.up())
                pool.wait_ge(lev_scores, levs.up())
                pool.tensor_tensor(halves(kd, m)[:, :, 0, :], level_exps(m, 1), halves(kk, m)[:, :, 0, :], ALU.mult).then_inc(kd_ready, 1)
                kdr.up()
                if l < 8:
                    pv, sv, nb = halves(pfx, m), halves(sfx, m), HG * S // (2 * m)
                    pool.tensor_tensor(sv[:, :, 0, :], sv[:, :, 0, :],
                                                      pv[:, :, 1, m - 1:m].to_broadcast([P, nb, m]), ALU.add).then_inc(pool_step, 1)
                    pool.wait_ge(pool_step, pst.up())
                    pool.tensor_tensor(pv[:, :, 1, :], pv[:, :, 1, :],
                                                      pv[:, :, 0, m - 1:m].to_broadcast([P, nb, m]), ALU.add).then_inc(sums_ready, 1)
                    pool.wait_ge(sums_ready, upd.up())
            pool.wait_ge(ol_ready, olr.up(len(MOBA) + len(MEM[0]) + 1))
            ln_rows("mix", 0)
            router_rows(0)
            for dst, src in ((mstrict, "k_strict"), (nstrict, "k_nstrict"), (nones, "k_nones")):
                pool.dma_start(dst, A[src]).then_inc(row_loaded, 16)
            pool.wait_ge(x_ready, xrd.up(1))
            ln_rows("ffn", 0)
            pool.wait_ge(x_ready, xrd.up(1))
            ln_rows("mix", 1)
            router_rows(1)
            pool.wait_ge(x_ready, xrd.up(1))
            ln_rows("ffn", 1)

        @block.scalar
        def _(act):
            step = Count(act_step)
            hsp, used = Count(h_split), Count(unit_used)
            n = [0]
            LIMIT = PLAN["end"]
            widths = narrow_units()

            def split(j=0, waited=False):
                u = n[0] + j
                if u >= LIMIT:
                    return
                w = widths.get(u, NC)
                loaded = 32 * (u // RAW + 1)
                act.wait_ge(raw_loaded[u % RAW], loaded if hsp.it is None else hsp.it * 32 + loaded)
                if u >= SPL and not waited:
                    act.wait_ge(unit_used, used.up())
                act.activation(wh[u % SPL][:, :, 0:w], raw[u % RAW][:, :, 0:w], ACT.Copy).then_inc(h_split, 1)
                hsp.up()

            def ahead(upto):
                while n[0] < upto + SPL:
                    split()
                    n[0] += 1

            xt, v, hhr = Count(xt_ready), Count(v_ready), Count(hh_ready)
            rstd, stat, xrd = Count(rstd_ready), Count(stat_ready), Count(x_ready)
            evac = Count(lin_evac)
            eps_col = {EPS: st[:, 60:61], LN_EPS: st[:, 61:62]}

            def rstd_of(src, width, eps):
                act.activation(st[:, 2:4], src, ACT.Ln, bias=eps_col[eps], scale=1.0 / width).then_inc(act_step, 1)
                act.wait_ge(act_step, step.up())
                act.activation(st[:, 4:6], st[:, 2:4], ACT.Exp, scale=-0.5).then_inc(rstd_ready, 1)
                act.wait_ge(rstd_ready, rstd.up())

            def rms_stats():
                for t in range(TT):
                    act.activation(tv[:, t, :], xs[:, t, :], ACT.Square, accum_out=st[:, t:t + 1]).then_inc(act_step, 1)
                    act.wait_ge(act_step, step.up())
                rstd_of(st[:, 0:2], D, EPS)

            def ln_stats():
                act.wait_ge(stat_ready, stat.up())
                rstd_of(st[:, 57:60:2], 1, LN_EPS)

            def bank_k(g):
                return ps[:, 4 + g, :].rearrange("p (k t) -> p k t", k=2)

            def transposed(modulated):
                for g in range(4):
                    act.wait_ge(v_ready if modulated else xt_ready, (v if modulated else xt).up())
                    act.activation(hh[:, 2 * g:2 * g + 2, :], bank_k(g), ACT.Copy).then_inc(hh_ready, 1)
                    hhr.up()
                if modulated:
                    xt.n += 4

            act.wait_ge(small_loaded, 96)
            scr = Count(sc_ready)
            act.activation(scol[:, :], cols[:, C_C:C_C + 8], ACT.Exp, scale=-1.0).then_inc(sc_ready, 1)
            scr.up()
            act.wait_ge(x_loaded, 16)
            act.wait_ge(dve_step, 2)
            rms_stats()
            ahead(0)
            transposed(True)

            lin = [0]

            def pair(b=0, e=2):
                return ps[:, 2 * (lin[0] % 2) + b:2 * (lin[0] % 2) + e, :]

            def chunk_ready(ph, c):
                ahead(PLAN[ph] + 2 * c + 1)
                act.wait_ge(unit_used, PLAN[ph] + 2 * c + 2)

            sqs, rsr, nrm = Count(sq_sum), Count(rs_ready), Count(normed)
            sq, rs = Z[:, 0:1024], Z[:, 1024:2048]

            def qk_rs():
                act.wait_ge(sq_sum, sqs.up())
                if rsr.n:
                    act.wait_ge(normed, nrm.up())
                act.activation(rs, ps[:, 4:6, :].rearrange("p a b -> p (a b)"), ACT.Ln, bias=eps_col[EPS], scale=1.0 / P).then_inc(act_step, 1)
                act.wait_ge(act_step, step.up())
                act.activation(rs, rs, ACT.Exp, scale=-0.5).then_inc(rs_ready, 1)
                act.wait_ge(rs_ready, rsr.up())

            for c in range(6):
                chunk_ready("qkv", c)
                if c < 4:
                    act.activation(FT[:, 4 * c:4 * c + 4, :].rearrange("p k t -> p (k t)"),
                                                  pair().rearrange("p a b -> p (a b)"), ACT.Copy).then_inc(act_step, 1)
                    act.wait_ge(act_step, step.up())
                    if c:
                        qk_rs()
                    act.activation(sq, pair().rearrange("p a b -> p (a b)"), ACT.Square).then_inc(lin_evac, 1)
                    act.wait_ge(lin_evac, evac.up())
                else:
                    if c == 4:
                        qk_rs()
                    act.activation(tv[:, :, (c - 4) * NC:(c - 3) * NC], pair(), ACT.Copy).then_inc(lin_evac, 1)
                    act.wait_ge(lin_evac, evac.up())
                lin[0] += 1
            ahead(PLAN["wo0"])

            nmx, er = Count(nmax_ready), Count(e_ready)
            ptr, pte = Count(pt_ready), Count(pt_evac)
            orr, ohr = Count(o_ready), Count(oh_ready)

            def head_out(src, dst):
                act.wait_ge(o_ready, orr.up())
                act.activation(dst, src, ACT.Copy).then_inc(oh_ready, 1)
                act.wait_ge(oh_ready, ohr.up())

            def heads(waves):
                def exps(w):
                    act.wait_ge(nmax_ready, nmx.up())
                    for a in range(2):
                        for t, (c0, c1) in enumerate(waves[w]["spans"]):
                            c = 4 * (w % 2) + 2 * a + t
                            i = act.activation(prob(w)[:, a, c0:c1], ps[:, 2 * (w % 2) + a, c0:c1], ACT.Exp,
                                               bias=st[:, 8 + c:9 + c], accum_out=st[:, 16 + c:17 + c])
                            if a == t == 1:
                                i.then_inc(e_ready, 1)
                                act.wait_ge(e_ready, er.up())
                            else:
                                i.then_inc(act_step, 1)
                                act.wait_ge(act_step, step.up())

                def turn_out(w):
                    act.wait_ge(pt_ready, ptr.up())
                    c = waves[w]["w"]
                    act.activation(turned(w)[:, :, 0:c], ps[:, 4:6, 0:c], ACT.Copy).then_inc(pt_evac, 1)
                    act.wait_ge(pt_evac, pte.up())

                for i in range(len(waves) + 2):
                    if i < len(waves):
                        exps(i)
                    if 0 <= i - 1 < len(waves):
                        turn_out(i - 1)
                    if i >= 2:
                        m = waves[i - 2]
                        head_out(out_of(i - 2, m), hh[:, m["blk"]:m["blk"] + m["nb"], :])

            heads(MOBA)

            def wo(ph):
                ahead(PLAN[ph] + 1)
                ahead(PLAN[ph] + 4)

            def norm_first():
                act.wait_ge(x_ready, xrd.up())
                rms_stats()
                transposed(True)

            wo("wo0")
            norm_first()

            silr, atr, ahr = Count(sil_ready), Count(at_ready), Count(ah_ready)

            def ffn(ph, chunks):
                def silu():
                    act.wait_ge(unit_used, used.up())
                    act.activation(Z[:, 0:512].rearrange("p (t n) -> p t n", t=2), ps[:, 0:2, 0:FW], ACT.Silu).then_inc(sil_ready, 1)
                    silr.up()

                def high():
                    act.wait_ge(at_ready, atr.up())
                    act.activation(ah[:, :, :], ps[:, 2, :].rearrange("p (k t) -> p k t", k=2), ACT.Copy).then_inc(ah_ready, 1)
                    ahr.up()

                def chunk(j):
                    high()
                    split(j)
                    silu()
                    split(j + 1, True)
                    split(j + 2)

                ahead(PLAN[ph])
                assert n[0] == PLAN[ph] + SPL
                split()
                silu()
                split(1, True)
                n[0] += 2
                loops = (chunks - 1) // 2
                with looped(act, loops, {hsp: 6, used: 6, silr: 2, atr: 2, ahr: 2}):
                    chunk(0)
                    chunk(3)
                n[0] += 6 * loops
                for _ in range(chunks - 1 - 2 * loops):
                    chunk(0)
                    n[0] += 3
                high()

            ffn("ffn0", NFF)
            ahead(PLAN["win"])
            act.wait_ge(x_ready, xrd.up())
            rms_stats()
            transposed(True)

            ptk = Count(lin_taken)
            for c in range(6):
                chunk_ready("win", c)
                if c < 2:
                    i = act.activation(FT[:, 4 * c:4 * c + 4, :].rearrange("p k t -> p (k t)"),
                                       pair().rearrange("p a b -> p (a b)"), ACT.Copy)
                else:
                    i = act.activation(Z[:, 0:1024] if c % 2 == 0 else Z[:, 1024:2048],
                                       pair().rearrange("p a b -> p (a b)"), ACT.Copy)
                i.then_inc(lin_evac, 1)
                act.wait_ge(lin_evac, evac.up())
                lin[0] += 1
                if c in (2, 3, 4, 5):
                    act.wait_ge(lin_taken, ptk.up())
            ahead(PLAN["wout"])
            for g in range(2):
                act.activation(hh[:, 4 * g:4 * g + 4, :], Z[:, 1024 * g:1024 * g + 1024].rearrange("p (k t) -> p k t", k=4), ACT.Copy).then_inc(hh_ready, 1)
                hhr.up()
            wo("wout")
            norm_first()
            ffn("ffn1", NFF)
            ahead(PLAN["mem"])
            act.wait_ge(x_ready, xrd.up())

            transposed(False)
            for l in range(DEPTH):
                chunk_ready("mem", l)
                act.activation(mk[:, l, :, :].rearrange("p b m -> p (b m)"), pair(0, 1).rearrange("p a b -> p (a b)"), ACT.Copy).then_inc(act_step, 1)
                act.wait_ge(act_step, step.up())
                act.activation(mv[:, l, :, :].rearrange("p b m -> p (b m)"), pair(1, 2).rearrange("p a b -> p (a b)"), ACT.Copy).then_inc(lin_evac, 1)
                act.wait_ge(lin_evac, evac.up())
                lin[0] += 1
            ahead(PLAN["a_in"])
            transposed(False)

            def features(b0, nb, func, last=True, skip=0, scale=1.0):
                src = pair().rearrange("p a (b t) -> p (a b) t", t=S)[:, skip:skip + nb, :]
                act.activation(FT[:, b0:b0 + nb, :], src, func, scale=scale).then_inc(lin_evac if last else act_step, 1)
                act.wait_ge(lin_evac if last else act_step, (evac if last else step).up())

            def rows(c0, w):
                act.activation(tv[:, :, c0:c0 + w], pair()[:, :, 0:w], ACT.Copy).then_inc(lin_evac, 1)
                act.wait_ge(lin_evac, evac.up())

            for c in range(7):
                chunk_ready("a_in", c)
                if c == 0:
                    features(0, 4, ACT.Silu)
                elif c == 1:
                    features(4, 2, ACT.Silu, last=False)
                    features(6, 2, ACT.Copy, skip=2)
                elif c == 2:
                    features(8, 4, ACT.Copy)
                elif c == 3:
                    rows(0, 512)
                elif c == 4:
                    rows(512, 256)
                elif c == 5:
                    features(12, 4, ACT.Silu)
                else:
                    features(16, 2, ACT.Silu, last=False)
                    features(18, 2, ACT.Copy, skip=2, scale=64 ** -0.5)
                lin[0] += 1
            ahead(PLAN["wo1"])
            heads(MEM[0])

            exr, dkr, upd = Count(exp_ready), Count(qk_in), Count(sums_ready)
            dqr, kdr = Count(dk_ready), Count(kd_ready)
            act.wait_ge(qk_in, dkr.up())
            act.activation(kd, kd, ACT.Exp).then_inc(act_step, 1)
            act.wait_ge(act_step, step.up())
            act.activation(kd, kd, ACT.Ln, bias=1.0).then_inc(exp_ready, 1)
            act.wait_ge(exp_ready, exr.up())
            act.wait_ge(qk_in, dkr.up())
            act.activation(FT[:, 6:12, :], sfx, ACT.Exp, scale=-1.0).then_inc(exp_ready, 1)
            act.wait_ge(exp_ready, exr.up())
            act.wait_ge(qk_in, dkr.up())
            dqr.n = 1
            for l in range(1, 9):
                m = 2 ** (l - 1)
                if l > 1:
                    act.wait_ge(sums_ready, upd.up())
                    act.wait_ge(dk_ready, dqr.up())
                    act.wait_ge(kd_ready, kdr.up())
                act.activation(level_exps(m, 0), halves(pfx, m)[:, :, 1, :], ACT.Exp).then_inc(act_step, 1)
                act.wait_ge(act_step, step.up())
                act.activation(level_exps(m, 1), halves(sfx, m)[:, :, 0, :], ACT.Exp).then_inc(exp_ready, 1)
                act.wait_ge(exp_ready, exr.up())
            act.wait_ge(o_ready, orr.up())
            o3 = ps[:, 4:7, :].rearrange("p a (b t) -> p (a b) t", t=S)
            act.activation(pfx, o3, ACT.Copy).then_inc(act_step, 1)
            act.wait_ge(act_step, step.up())
            act.activation(qd, o3, ACT.Square).then_inc(exp_ready, 1)
            act.wait_ge(exp_ready, exr.up())
            act.wait_ge(sq_sum, sqs.up())
            act.activation(kd, o3, ACT.Ln, bias=eps_col[EPS], scale=1.0 / P).then_inc(act_step, 1)
            act.wait_ge(act_step, step.up())
            act.activation(kd, kd, ACT.Exp, scale=-0.5).then_inc(rs_ready, 1)
            act.wait_ge(rs_ready, rsr.up())
            act.wait_ge(v_ready, v.up())
            act.activation(hh[:, 0:6, :], sfx, ACT.Copy).then_inc(hh_ready, 1)
            hhr.up()
            wo("wo1")
            ln_stats()
            act.wait_ge(x_ready, xrd.up())
            transposed(False)
            def router():
                act.wait_ge(router_ready, sp_in.up())
                act.activation(rt[:, 64:104], rt[:, 64:104], ACT.Exp).then_inc(exp_ready, 1)
                act.wait_ge(exp_ready, exr.up())

            sp_in = Count(router_ready)
            router()
            ffn("moe0", NEXP)
            ahead(PLAN["kv"])
            ln_stats()
            act.wait_ge(x_ready, xrd.up())
            transposed(False)

            for c in range(4):
                chunk_ready("kv", c)
                if c == 0:
                    features(6, 4, ACT.Copy)
                elif c == 1:
                    features(10, 2, ACT.Copy)
                elif c == 2:
                    rows(0, 512)
                else:
                    rows(512, 256)
                lin[0] += 1
            for c in range(2):
                chunk_ready("b_in", c)
                if c == 0:
                    features(0, 4, ACT.Copy, scale=64 ** -0.5)
                else:
                    features(4, 2, ACT.Copy, last=False, scale=64 ** -0.5)
                    features(18, 2, ACT.Copy, skip=2, scale=64 ** -0.5)
                lin[0] += 1
            ahead(PLAN["wo2"])
            heads(MEM[1])
            zr, lr, lar, ar = Count(s_ready), Count(l_ready), Count(la_ready), Count(a_ready)
            zr.n = len(MOBA) + len(MEM[0]) + len(MEM[1])
            for i in range(SBH // 2 + 2):
                if i >= 2:
                    head_out(ps[:, 4 + i % 2, 0:S], hh[:, i - 2, :])
                if i < SBH // 2:
                    act.wait_ge(s_ready, zr.up())
                    nb, z = sb_buf(i), ps[:, 2 * (i % 2):2 * (i % 2) + 2, 0:384]
                    act.activation(nb, z, ACT.Abs).then_inc(act_step, 1)
                    act.wait_ge(act_step, step.up())
                    act.activation(nb, nb, ACT.Exp, scale=-1.0).then_inc(act_step, 1)
                    act.wait_ge(act_step, step.up())
                    act.activation(nb, nb, ACT.Ln, bias=1.0).then_inc(l_ready, 1)
                    act.wait_ge(l_ready, lr.up())
                if 0 <= i - 1 < SBH // 2:
                    act.wait_ge(la_ready, lar.up())
                    act.activation(sb_buf(i - 1), sb_buf(i - 1), ACT.Exp).then_inc(a_ready, 1)
                    act.wait_ge(a_ready, ar.up())
            wo("wo2")
            ln_stats()
            act.wait_ge(x_ready, xrd.up())
            transposed(False)
            router()
            ffn("moe1", NEXP)
            ln_stats()

        @block.vector
        def _(dve):
            step = Count(dve_step)
            hsp, lsp = Count(h_split), Count(l_split)
            n = [0]
            LIMIT = PLAN["end"]
            widths = narrow_units()

            def split(j=0):
                u = n[0] + j
                if u >= LIMIT:
                    return
                w = widths.get(u, NC)
                dve.wait_ge(h_split, hsp.up())
                dve.tensor_tensor(wl[u % SPL][:, :, 0:w], raw[u % RAW][:, :, 0:w],
                                             wh[u % SPL][:, :, 0:w].bitcast(F32), ALU.subtract).then_inc(l_split, 1)
                lsp.up()

            def ahead(upto):
                while n[0] < upto + SPL:
                    split()
                    n[0] += 1

            rstd, stat, xrd = Count(rstd_ready), Count(stat_ready), Count(x_ready)
            xn, xt, v, hhr, hr = Count(xn_ready), Count(xt_ready), Count(v_ready), Count(hh_ready), Count(h_ready)
            accd, usedd = Count(ada_acc), Count(ada_used)
            rows_in = [0]

            dve.memset(st[:, 60:61], EPS).then_inc(dve_step, 1)
            dve.wait_ge(dve_step, step.up())
            dve.memset(st[:, 61:62], LN_EPS).then_inc(dve_step, 1)
            dve.wait_ge(dve_step, step.up())
            dve.wait_ge(small_loaded, 96)
            dve.tensor_copy(mlev[:, :, :], Z[:, 0:8 * P].rearrange("p (l n) -> p l n", n=P)).then_inc(dve_step, 1)
            dve.wait_ge(dve_step, step.up())
            dve.tensor_scalar(st[:, 62:63], cols[:, C_QG:C_QG + 1], P ** -0.5, None, ALU.mult).then_inc(dve_step, 1)
            dve.wait_ge(dve_step, step.up())
            dve.wait_ge(sc_ready, 1)
            dve.tensor_scalar(scol[:, :], scol[:, :], 1.0, None, ALU.add).then_inc(dve_step, 1)
            dve.wait_ge(dve_step, step.up())
            dve.reciprocal(scol[:, :], scol[:, :]).then_inc(dve_step, 1)
            dve.wait_ge(dve_step, step.up())
            dve.tensor_tensor(scol[:, :], scol[:, :], cols[:, C_C:C_C + 8], ALU.mult).then_inc(dve_step, 1)
            dve.wait_ge(dve_step, step.up())

            def ada(layer, c, acc, it=None):
                g = 12 * layer + c
                for q in range(2):
                    dve.wait_ge(ada_loaded[q], 16 * (g + 1) if it is None else it * 32 + 16 * (g + 1))
                    for k in range(UK):
                        w, s = cring[:, q, k, :], scol[:, UK * q + k:UK * q + k + 1]
                        if q == k == 0:
                            i = dve.tensor_scalar(acc, w, s, None, ALU.mult)
                        else:
                            i = dve.scalar_tensor_tensor(acc, w, s, acc, ALU.mult, ALU.add)
                        i.then_inc(ada_used if k == UK - 1 else ada_acc, 1)
                        dve.wait_ge(ada_used if k == UK - 1 else ada_acc, (usedd if k == UK - 1 else accd).up())

            ft_acc = FT[:, :, :].rearrange("p (c a) t -> p c (a t)", a=2)

            def acc_of(layer, c):
                if layer == 0:
                    return ft_acc[:, c, :] if c < 4 else accw[:, c - 4, :]
                return ft_acc[:, c, :] if c < 10 else accw[:, c - 10, :]

            msum, mtk = Count(mod_sums), Count(mod_taken)

            def mod_cols(layer, which):
                dve.wait_ge(mod_sums, msum.up())
                b = cols[:, C_BADA + 48 * layer + 24 * which:C_BADA + 48 * layer + 24 * which + 16]
                gain = cols[:, (C_NFFN if which else C_NMIX) + 8 * layer:(C_NFFN if which else C_NMIX) + 8 * layer + 8]
                o = slice(8 * which, 8 * which + 8)
                dve.tensor_tensor(modB[:, o], ps[:, 7, 0:8], b[:, 0:8], ALU.add).then_inc(dve_step, 1)
                dve.wait_ge(dve_step, step.up())
                dve.tensor_tensor(modA[:, o], ps[:, 7, 8:16], b[:, 8:16], ALU.add).then_inc(dve_step, 1)
                dve.wait_ge(dve_step, step.up())
                dve.scalar_tensor_tensor(modA[:, o], modA[:, o], 1.0, gain, ALU.add, ALU.mult).then_inc(mod_taken, 1)
                dve.wait_ge(mod_taken, mtk.up())

            def mod_gate(g):
                dve.wait_ge(mod_sums, msum.up())
                dve.tensor_tensor(gb[:, g, :], ps[:, 4:6, :].rearrange("p a b -> p (a b)"), gb[:, g, :], ALU.add).then_inc(mod_taken, 1)
                dve.wait_ge(mod_taken, mtk.up())

            def rms_apply():
                dve.wait_ge(rstd_ready, rstd.up())
                dve.tensor_scalar(tv[:, 0, :], xs[:, 0, :], st[:, 4:5], None, ALU.mult).then_inc(dve_step, 1)
                dve.wait_ge(dve_step, step.up())
                dve.tensor_scalar(tv[:, 1, :], xs[:, 1, :], st[:, 5:6], None, ALU.mult).then_inc(xn_ready, 1)
                dve.wait_ge(xn_ready, xn.up())

            def bank_k(g):
                return ps[:, 4 + g, :].rearrange("p (k t) -> p k t", k=2)

            def low(g):
                dve.wait_ge(hh_ready, hhr.up())
                dve.tensor_tensor(hl[:, 2 * g:2 * g + 2, :], bank_k(g),
                                            hh[:, 2 * g:2 * g + 2, :].bitcast(F32), ALU.subtract).then_inc(h_ready, 1)
                hr.up()

            def transposed_mod(which):
                for g in range(5):
                    if g < 4:
                        dve.wait_ge(xt_ready, xt.up())
                        for q in range(2):
                            k = 8 * which + 2 * g + q
                            b = ps[:, 4 + g, q * S:(q + 1) * S]
                            dve.tensor_scalar(
                                b, b, modA[:, k:k + 1], modB[:, k:k + 1], ALU.mult, ALU.add).then_inc(v_ready if q else dve_step, 1)
                            dve.wait_ge(v_ready if q else dve_step, (v if q else step).up())
                    if g:
                        low(g - 1)

            def transposed_plain():
                for g in range(4):
                    low(g)
                xt.n += 4

            for c in range(4):
                ada(0, c, acc_of(0, c))
            ahead(0)
            mod_cols(0, 0)
            rms_apply()
            transposed_mod(0)

            rsr, nrm = Count(rs_ready), Count(normed)

            def qk_norm(c):
                dve.wait_ge(rs_ready, rsr.up())
                f = FT[:, 4 * c:4 * c + 4, :].rearrange("p k t -> p (k t)")
                gain = st[:, 62:63] if c < 2 else cols[:, C_KG:C_KG + 1]
                dve.scalar_tensor_tensor(f, f, gain, Z[:, 1024:2048], ALU.mult, ALU.mult).then_inc(normed, 1)
                dve.wait_ge(normed, nrm.up())

            for c in range(6):
                ahead(PLAN["qkv"] + 2 * c + 1)
                if 1 <= c <= 4:
                    qk_norm(c - 1)
                ada(0, 4 + c, acc_of(0, 4 + c))
            ahead(PLAN["wo0"])
            for c in (10, 11):
                ada(0, c, acc_of(0, c))

            dve.wait_ge(row_loaded, 32)
            mod_cols(0, 1)
            mod_gate(0)
            mod_gate(1)

            sr, nmx = Count(s_ready), Count(nmax_ready)
            er, pr, ohr, olr = Count(e_ready), Count(p_ready), Count(oh_ready), Count(ol_ready)

            def head_low(src, h, dst):
                dve.wait_ge(oh_ready, ohr.up())
                dve.tensor_tensor(dst, src, h.bitcast(F32), ALU.subtract).then_inc(ol_ready, 1)
                dve.wait_ge(ol_ready, olr.up())

            def heads(waves):
                def maxima(w):
                    dve.wait_ge(s_ready, sr.up())
                    b, m = w % 2, waves[w]
                    s = ps[:, 2 * b:2 * b + 2, :]
                    for t, (c0, c1) in enumerate(m["spans"]):
                        dve.tensor_reduce(
                            st[:, 8 + 4 * b + t:12 + 4 * b:2], s[:, :, c0:c1], AX.X, ALU.max, negate=True).then_inc(nmax_ready if t else dve_step, 1)
                        dve.wait_ge(nmax_ready if t else dve_step, (nmx if t else step).up())

                def probs(w):
                    dve.wait_ge(e_ready, er.up())
                    b, m = w % 2, waves[w]
                    dve.reciprocal(st[:, 24 + 4 * b:28 + 4 * b], st[:, 16 + 4 * b:20 + 4 * b]).then_inc(dve_step, 1)
                    dve.wait_ge(dve_step, step.up())
                    for t, (c0, c1) in enumerate(m["spans"]):
                        z = prob(w)[:, :, c0:c1]
                        r = st[:, 24 + 4 * b + t:28 + 4 * b:2].unsqueeze(2).to_broadcast([P, 2, c1 - c0])
                        dve.tensor_tensor(z, z, r, ALU.mult).then_inc(p_ready if t else dve_step, 1)
                        dve.wait_ge(p_ready if t else dve_step, (pr if t else step).up())

                for i in range(len(waves) + 2):
                    if i < len(waves):
                        maxima(i)
                    if 0 <= i - 1 < len(waves):
                        probs(i - 1)
                    if i >= 2:
                        m = waves[i - 2]
                        b = slice(m["blk"], m["blk"] + m["nb"])
                        head_low(out_of(i - 2, m), hh[:, b, :], hl[:, b, :])

            heads(MOBA)

            def wo(ph):
                ahead(PLAN[ph] + 1)
                ahead(PLAN[ph] + 4)

            def add_gated(g, after):
                dve.wait_ge(unit_used, PLAN[after])
                for t in range(TT):
                    y = ps[:, 4 + t:8:2, :]
                    dve.tensor_tensor(tv[:, t, :].rearrange("p (a n) -> p a n", a=2), y,
                                         gb[:, g, :].rearrange("p (a n) -> p a n", a=2), ALU.mult).then_inc(dve_step, 1)
                    dve.wait_ge(dve_step, step.up())
                    dve.tensor_tensor(xs[:, t, :], xs[:, t, :], tv[:, t, :], ALU.add).then_inc(x_ready if t else dve_step, 1)
                    dve.wait_ge(x_ready if t else dve_step, (xrd if t else step).up())

            wo("wo0")
            add_gated(0, "ffn0")
            rms_apply()
            transposed_mod(1)

            silr, acr, ahr, asp = Count(sil_ready), Count(act_ready), Count(ah_ready), Count(a_split)

            def ffn(ph, chunks, weight, extra=None):
                def product(c, r=0):
                    dve.wait_ge(sil_ready, silr.up())
                    for t in range(TT):
                        sil = Z[:, t * FW:(t + 1) * FW]
                        up = ps[:, t, FW:2 * FW]
                        dve.scalar_tensor_tensor(
                            Z[:, 512 + t * FW:512 + (t + 1) * FW], sil, weight(t, c), up, ALU.mult, ALU.mult).then_inc(act_ready, 1)
                        acr.up()

                def low_part():
                    dve.wait_ge(ah_ready, ahr.up())
                    dve.tensor_tensor(al[:, :, :], ps[:, 2, :].rearrange("p (k t) -> p k t", k=2),
                                                 ah[:, :, :].bitcast(F32), ALU.subtract).then_inc(a_split, 1)
                    asp.up()

                def chunk(c, j, it=None):
                    low_part()
                    split(j)
                    split(j + 1)
                    product(c)
                    split(j + 2)

                ahead(PLAN[ph])
                split()
                product(0)
                split(1)
                n[0] += 2
                loops = (chunks - 1) // 2
                per = {hsp: 6, lsp: 6, silr: 2, acr: 4, ahr: 2, asp: 2}
                if extra:
                    per.update({accd: 12, usedd: 4})
                with looped(dve, loops, per) as it:
                    for r in range(2):
                        chunk(it * 2 + (r + 1), 3 * r)
                        if extra:
                            extra(r, it)
                n[0] += 6 * loops
                for q in range(chunks - 1 - 2 * loops):
                    chunk(2 * loops + 1 + q, 0)
                    n[0] += 3
                low_part()

            def ada_in_loop(r, it):
                ada(1, r, ft_acc[:, bass.ds(it * 2 + r, 1), :].rearrange("p a n -> p (a n)"), it)

            ffn("ffn0", NFF, lambda t, c: 1.0, ada_in_loop)
            for c in (10, 11):
                ada(1, c, acc_of(1, c))
            ahead(PLAN["win"])
            add_gated(1, "win")
            mod_cols(1, 0)
            mod_cols(1, 1)
            dve.wait_ge(row_loaded, 64)
            mod_gate(0)
            mod_gate(1)
            rms_apply()
            transposed_mod(0)

            evac, ptk = Count(lin_evac), Count(lin_taken)
            evac.n = 6
            cu = FT[:, 0:8, :]
            cy = FT[:, 8:16, :]
            for c in range(6):
                ahead(PLAN["win"] + 2 * c + 1)
                dve.wait_ge(lin_evac, evac.up())
                if c in (2, 3):
                    f = cu[:, 4 * (c - 2):4 * (c - 1), :].rearrange("p k t -> p (k t)")
                    dve.tensor_tensor(f, f, Z[:, 1024 * (c % 2):1024 * (c % 2) + 1024], ALU.mult).then_inc(lin_taken, 1)
                    dve.wait_ge(lin_taken, ptk.up())
                    for k in range(4 * (c - 2), 4 * (c - 1)):
                        w = lambda j: cols[:, C_CONV + 8 * j + k:C_CONV + 8 * j + k + 1]
                        dve.tensor_scalar(cy[:, k, :], cu[:, k, :], w(2), None, ALU.mult).then_inc(dve_step, 1)
                        dve.wait_ge(dve_step, step.up())
                        dve.scalar_tensor_tensor(cy[:, k, 1:S], cu[:, k, 0:S - 1], w(1), cy[:, k, 1:S], ALU.mult, ALU.add).then_inc(dve_step, 1)
                        dve.wait_ge(dve_step, step.up())
                        dve.scalar_tensor_tensor(cy[:, k, 2:S], cu[:, k, 0:S - 2], w(0), cy[:, k, 2:S], ALU.mult, ALU.add).then_inc(dve_step, 1)
                        dve.wait_ge(dve_step, step.up())
                if c >= 4:
                    z = Z[:, 1024 * (c % 2):1024 * (c % 2) + 1024]
                    dve.tensor_tensor(z, z, cy[:, 4 * (c - 4):4 * (c - 3), :].rearrange("p k t -> p (k t)"), ALU.mult).then_inc(lin_taken, 1)
                    dve.wait_ge(lin_taken, ptk.up())
            ahead(PLAN["wout"])
            for g in range(2):
                dve.wait_ge(hh_ready, hhr.up())
                dve.tensor_tensor(hl[:, 4 * g:4 * g + 4, :], Z[:, 1024 * g:1024 * g + 1024].rearrange("p (k t) -> p k t", k=4),
                                            hh[:, 4 * g:4 * g + 4, :].bitcast(F32), ALU.subtract).then_inc(h_ready, 1)
                hr.up()
            wo("wout")
            add_gated(0, "ffn1")
            rms_apply()
            transposed_mod(1)
            ffn("ffn1", NFF, lambda t, c: 1.0)
            ahead(PLAN["mem"])
            add_gated(1, "mem")

            transposed_plain()
            for l in range(DEPTH):
                ahead(PLAN["mem"] + 2 * l + 1)
            ahead(PLAN["a_in"])
            transposed_plain()
            for c in range(7):
                ahead(PLAN["a_in"] + 2 * c + 1)
            ahead(PLAN["wo1"])
            heads(MEM[0])

            exr, dkr, dqr = Count(exp_ready), Count(qk_in), Count(dk_ready)
            levs, levt = Count(lev_scores), Count(lev_taken)
            q, f, kk, g = FT[:, 0:6, :], FT[:, 6:12, :], FT[:, 6:12, :], FT[:, 12:18, :]
            dve.scalar_tensor_tensor(kd, f, -1.0, f, ALU.mult, ALU.min).then_inc(qk_in, 1)
            dve.wait_ge(qk_in, dkr.up())
            dve.tensor_scalar(q, q, P ** -0.5, None, ALU.mult).then_inc(dve_step, 1)
            dve.wait_ge(dve_step, step.up())
            dve.tensor_copy(qd, q).then_inc(dve_step, 1)
            dve.wait_ge(dve_step, step.up())
            dve.wait_ge(exp_ready, exr.up())
            dve.scalar_tensor_tensor(pfx, f, 0.0, kd, ALU.min, ALU.subtract).then_inc(dve_step, 1)
            dve.wait_ge(dve_step, step.up())
            dve.scalar_tensor_tensor(sfx, f, 0.0, kd, ALU.max, ALU.add).then_inc(qk_in, 1)
            dve.wait_ge(qk_in, dkr.up())
            dve.memset(scD, 0.0).then_inc(dve_step, 1)
            dve.wait_ge(dve_step, step.up())
            dve.wait_ge(exp_ready, exr.up())
            dve.tensor_copy(kd, kk).then_inc(dk_ready, 1)
            dve.wait_ge(dk_ready, dqr.up())
            dve.memset(sfx, 0.0).then_inc(qk_in, 1)
            dve.wait_ge(qk_in, dkr.up())

            def take(l):
                o = 4 * (l % 2)
                if l < 8:
                    dve.copy_predicated(
                        scD.rearrange("p h (c t) -> p (h c) t", c=2), mlev[:, l:l + 1, :].to_broadcast([P, 2 * HG, P]),
                        ps[:, o:o + 3, :].rearrange("p a (b t) -> p (a b) t", t=P)).then_inc(lev_taken, 1)
                    dve.wait_ge(lev_taken, levt.up())
                else:
                    dve.tensor_copy(scX[:, 0:4, :], ps[:, o, :].rearrange("p (h t) -> p h t", t=P)).then_inc(dve_step, 1)
                    dve.wait_ge(dve_step, step.up())
                    dve.tensor_copy(scX[:, 4:6, :], ps[:, o + 1, 0:S].rearrange("p (h t) -> p h t", t=P)).then_inc(lev_taken, 1)
                    dve.wait_ge(lev_taken, levt.up())

            for l in range(1, 9):
                m = 2 ** (l - 1)
                dve.wait_ge(exp_ready, exr.up())
                dve.wait_ge(lev_scores, levs.up())
                dve.tensor_tensor(halves(qd, m)[:, :, 1, :], level_exps(m, 0), halves(q, m)[:, :, 1, :], ALU.mult).then_inc(dk_ready, 1)
                dve.wait_ge(dk_ready, dqr.up())
                take(l - 1)
            dve.wait_ge(lev_scores, levs.up())
            take(8)
            dve.wait_ge(rs_ready, rsr.up())
            exr.n += 1
            for h in range(HG):
                dve.scalar_tensor_tensor(pfx[:, h, :], pfx[:, h, :], cols[:, C_GN + h:C_GN + h + 1], kd[:, h, :],
                                            ALU.mult, ALU.mult).then_inc(dve_step, 1)
                dve.wait_ge(dve_step, step.up())
            dve.tensor_tensor(sfx, pfx, g, ALU.mult).then_inc(v_ready, 1)
            dve.wait_ge(v_ready, v.up())
            dve.wait_ge(hh_ready, hhr.up())
            dve.tensor_tensor(hl[:, 0:6, :], sfx, hh[:, 0:6, :].bitcast(F32), ALU.subtract).then_inc(ol_ready, 1)
            dve.wait_ge(ol_ready, olr.up())

            def post_norm(after, rows_need):
                dve.wait_ge(unit_used, PLAN[after])
                for t in range(TT):
                    x2 = xs[:, t, :].rearrange("p (a n) -> p a n", a=2)
                    dve.scalar_tensor_tensor(x2, x2, ALPHA, ps[:, 4 + t:8:2, :], ALU.mult, ALU.add).then_inc(dve_step, 1)
                    dve.wait_ge(dve_step, step.up())
                    for a in range(2):
                        dve.bn_stats(st[:, 32 + 12 * t + 6 * a:38 + 12 * t + 6 * a], xs[:, t, a * 512:(a + 1) * 512]).then_inc(dve_step, 1)
                        dve.wait_ge(dve_step, step.up())
                    dve.bn_aggr(st[:, 56 + 2 * t:58 + 2 * t], st[:, 32 + 12 * t:44 + 12 * t]).then_inc(stat_ready if t else dve_step, 1)
                    dve.wait_ge(stat_ready if t else dve_step, (stat if t else step).up())
                dve.wait_ge(rstd_ready, rstd.up())
                dve.wait_ge(row_loaded, rows_need)
                for t in range(TT):
                    x = xs[:, t, :]
                    dve.tensor_scalar(x, x, st[:, 56 + 2 * t:57 + 2 * t], st[:, 4 + t:5 + t], ALU.subtract, ALU.mult).then_inc(dve_step, 1)
                    dve.wait_ge(dve_step, step.up())
                    dve.tensor_tensor(x, x, lnv[:, 0, :], ALU.mult).then_inc(dve_step, 1)
                    dve.wait_ge(dve_step, step.up())
                    dve.tensor_tensor(x, x, lnv[:, 1, :], ALU.add).then_inc(x_ready if t else dve_step, 1)
                    dve.wait_ge(x_ready if t else dve_step, (xrd if t else step).up())

            rin, rsum = Count(router_ready), Count(router_sums)

            def router():
                dve.wait_ge(router_sums, rsum.up())
                N = 2 * 5
                lg = rt[:, 0:40]
                g3 = lambda a: a.rearrange("p (g e) -> p g e", e=4)
                for t in range(TT):
                    dve.tensor_tensor(lg[:, 20 * t:20 * t + 20], ps[:, 7, 20 * t:20 * t + 20], rbias, ALU.add).then_inc(dve_step, 1)
                    dve.wait_ge(dve_step, step.up())
                mx, ex = rt[:, 48:58], rt[:, 64:104]
                dve.tensor_reduce(mx, g3(lg), AX.X, ALU.max).then_inc(dve_step, 1)
                dve.wait_ge(dve_step, step.up())
                dve.tensor_tensor(g3(ex), g3(lg), mx.unsqueeze(2).to_broadcast([P, N, 4]), ALU.subtract).then_inc(router_ready, 1)
                dve.wait_ge(router_ready, rin.up())
                rank, cmp_ = rt[:, 112:152], rt[:, 160:200]
                dve.memset(rank, 0.0).then_inc(dve_step, 1)
                dve.wait_ge(dve_step, step.up())
                for j in range(4):
                    other = g3(lg)[:, :, j:j + 1].to_broadcast([P, N, 4])
                    dve.tensor_tensor(g3(cmp_), other, g3(lg), ALU.is_gt).then_inc(dve_step, 1)
                    dve.wait_ge(dve_step, step.up())
                    dve.tensor_tensor(rank, rank, cmp_, ALU.add).then_inc(dve_step, 1)
                    dve.wait_ge(dve_step, step.up())
                    if j < 3:
                        dve.tensor_tensor(g3(cmp_)[:, :, j + 1:4], other[:, :, 0:3 - j], g3(lg)[:, :, j + 1:4], ALU.is_equal).then_inc(dve_step, 1)
                        dve.wait_ge(dve_step, step.up())
                        dve.tensor_tensor(g3(rank)[:, :, j + 1:4], g3(rank)[:, :, j + 1:4], g3(cmp_)[:, :, j + 1:4], ALU.add).then_inc(dve_step, 1)
                        dve.wait_ge(dve_step, step.up())
                best, sums = rt[:, 208:248], rt[:, 256:266]
                dve.wait_ge(exp_ready, exr.up())
                dve.tensor_reduce(sums, g3(ex), AX.X, ALU.add).then_inc(dve_step, 1)
                dve.wait_ge(dve_step, step.up())
                dve.tensor_scalar(best, rank, 2.0, None, ALU.is_lt).then_inc(dve_step, 1)
                dve.wait_ge(dve_step, step.up())
                dve.tensor_tensor(best, best, ex, ALU.mult).then_inc(dve_step, 1)
                dve.wait_ge(dve_step, step.up())
                dve.tensor_reduce(mx, g3(best), AX.X, ALU.add).then_inc(dve_step, 1)
                dve.wait_ge(dve_step, step.up())
                dve.reciprocal(mx, mx).then_inc(dve_step, 1)
                dve.wait_ge(dve_step, step.up())
                dve.reciprocal(sums, sums).then_inc(dve_step, 1)
                dve.wait_ge(dve_step, step.up())
                dve.tensor_scalar(rank, rank, 1.0, None, ALU.is_lt).then_inc(dve_step, 1)
                dve.wait_ge(dve_step, step.up())
                for t in range(TT):
                    w = rt[:, 272 + 4 * t:276 + 4 * t]
                    dve.tensor_scalar(w, rank[:, 20 * t:20 * t + 4], sums[:, 5 * t:5 * t + 1], None, ALU.mult).then_inc(dve_step, 1)
                    dve.wait_ge(dve_step, step.up())
                    dve.tensor_tensor(w, w, mx[:, 5 * t + 1:5 * t + 5], ALU.mult).then_inc(dve_step, 1)
                    dve.wait_ge(dve_step, step.up())
                    dve.tensor_tensor(g3(gate[:, t, :]), g3(best[:, 20 * t + 4:20 * t + 20]),
                                         w.unsqueeze(2).to_broadcast([P, 4, 4]), ALU.mult).then_inc(dve_step, 1)
                    dve.wait_ge(dve_step, step.up())

            def expert_gate(t, e):
                if isinstance(e, int):
                    return gate[:, t, e:e + 1]
                return gate[:, t, bass.ds(e, 1)]

            wo("wo1")
            post_norm("moe0", 208)
            transposed_plain()
            router()
            ffn("moe0", NEXP, expert_gate)
            ahead(PLAN["kv"])
            post_norm("kv", 240)
            transposed_plain()
            for c in range(4):
                ahead(PLAN["kv"] + 2 * c + 1)
            for c in range(2):
                ahead(PLAN["b_in"] + 2 * c + 1)
            ahead(PLAN["wo2"])
            heads(MEM[1])
            lr, spr = Count(l_ready), Count(sp_ready)
            rr, lar = Count(rest_ready), Count(la_ready)
            both = lambda x: x.unsqueeze(1).to_broadcast([P, 2, 384])
            for i in range(SBH // 2 + 2):
                if i >= 2:
                    head_low(ps[:, 4 + i % 2, 0:S], hh[:, i - 2, :], hl[:, i - 2, :])
                if i < SBH // 2:
                    dve.wait_ge(l_ready, lr.up())
                    nb, z = sb_buf(i), ps[:, 2 * (i % 2):2 * (i % 2) + 2, 0:384]
                    dve.scalar_tensor_tensor(nb, z, 0.0, nb, ALU.max, ALU.add).then_inc(dve_step, 1)
                    dve.wait_ge(dve_step, step.up())
                    dve.tensor_tensor(nb, nb, both(mstrict), ALU.mult).then_inc(sp_ready, 1)
                    dve.wait_ge(sp_ready, spr.up())
                if 0 <= i - 1 < SBH // 2:
                    dve.wait_ge(rest_ready, rr.up())
                    dve.scalar_tensor_tensor(sb_buf(i - 1), ps[:, 2 * ((i - 1) % 2):2 * ((i - 1) % 2) + 2, 0:384],
                                                           0.0, both(nstrict), ALU.min, ALU.add).then_inc(la_ready, 1)
                    dve.wait_ge(la_ready, lar.up())
            wo("wo2")
            post_norm("moe1", 336)
            transposed_plain()
            router()
            ffn("moe1", NEXP, expert_gate)
            post_norm("end", 368)

        @block.tensor
        def _(pe):
            lsp, used = Count(l_split), Count(unit_used)
            n = [0]

            def mm3(o, h1, l1, h2, l2, start, stop):
                pe.matmul(o, h1, h2, start=start, stop=False, skip_group_check=True)
                pe.matmul(o, h1, l2, start=False, stop=False, skip_group_check=True)
                return pe.matmul(o, l1, h2, start=False, stop=stop, skip_group_check=True)

            def unit_rows(u, bank, k0, w, first, last):
                pe.wait_ge(l_split, lsp.up())
                for t in range(TT):
                    for k in range(UK):
                        tok = slice(t * P, (t + 1) * P)
                        i = mm3(bank(t)[:, 0:w], hh[:, k0 + k, tok], hl[:, k0 + k, tok],
                                wh[u % SPL][:, k, 0:w], wl[u % SPL][:, k, 0:w],
                                first and k == 0, last and k == UK - 1)
                i.then_inc(unit_used, 1)
                used.up()

            def unit_features(u, b0, nb, k0, first, last, signal=True, c0=0):
                for b in range(nb):
                    o = ps[:, b0 + b // 2, (b % 2) * S:(b % 2 + 1) * S]
                    for k in range(UK):
                        cs = slice(c0 + b * P, c0 + (b + 1) * P)
                        i = mm3(o, wh[u % SPL][:, k, cs], wl[u % SPL][:, k, cs], hh[:, k0 + k, :], hl[:, k0 + k, :],
                                first and k == 0 and b % 2 == 0, last and k == UK - 1)
                return i

            evac = Count(lin_evac)
            lin = [0]

            def chunk(kind, w=NC):
                if lin[0] >= 2:
                    pe.wait_ge(lin_evac, evac.up())
                pair = 2 * (lin[0] % 2)
                for q in range(2):
                    if kind == "rows":
                        unit_rows(n[0], lambda t: ps[:, pair + t, :], UK * q, w, q == 0, q == 1)
                    else:
                        pe.wait_ge(l_split, lsp.up())
                        unit_features(n[0], pair, w // P, UK * q, q == 0, q == 1).then_inc(unit_used, 1)
                        used.up()
                    n[0] += 1
                lin[0] += 1

            hr, xrd = Count(h_ready), Count(x_ready)
            olr = Count(ol_ready)

            def out_rows():
                for c in range(2):
                    for q in range(2):
                        unit_rows(n[0], lambda t: ps[:, 4 + 2 * c + t, :], UK * q, NC, q == 0, q == 1)
                        n[0] += 1

            xn, xt = Count(xn_ready), Count(xt_ready)

            def transposes(src):
                for g in range(4):
                    for k in range(2):
                        for t in range(TT):
                            c = (2 * g + k) * P
                            i = pe.transpose(ps[:, 4 + g, k * S + t * P:k * S + (t + 1) * P], src[:, t, c:c + P], ident[:, :])
                    i.then_inc(xt_ready, 1)
                    xt.up()

            usedd, msum, mtk = Count(ada_used), Count(mod_sums), Count(mod_taken)
            ft_acc = FT[:, :, :].rearrange("p (c a) t -> p c (a t)", a=2)

            def acc_of(layer, c):
                if layer == 0:
                    return ft_acc[:, c, :] if c < 4 else accw[:, c - 4, :]
                return ft_acc[:, c, :] if c < 10 else accw[:, c - 10, :]

            def mod_cols(layer, which):
                for c in range(4):
                    for q in range(4):
                        i = pe.matmul(ps[:, 7, 4 * c + q:4 * c + q + 1], acc_of(layer, 6 * which + c)[:, q * P:(q + 1) * P],
                                      ones[:, 0:1], start=True, stop=True)
                i.then_inc(mod_sums, 1)
                msum.up()

            def mod_gate(layer, g):
                for c in range(2):
                    i = pe.matmul(ps[:, 4 + c, :], ones[:, :], acc_of(layer, 6 * g + 4 + c), start=True, stop=True)
                i.then_inc(mod_sums, 1)
                msum.up()

            pe.wait_ge(small_loaded, 96)
            pe.wait_ge(ada_used, usedd.up(8))
            mod_cols(0, 0)
            pe.wait_ge(mod_taken, mtk.up())
            pe.wait_ge(xn_ready, xn.up())
            transposes(tv)
            pe.wait_ge(h_ready, hr.up(4))

            sqs, rsr = Count(sq_sum), Count(rs_ready)

            def square_sums():
                for a in range(2):
                    i = pe.matmul(ps[:, 4 + a, :], ones[:, :], Z[:, a * 512:(a + 1) * 512], start=True, stop=True)
                i.then_inc(sq_sum, 1)
                sqs.up()

            for c in range(6):
                chunk("features" if c < 4 else "rows")
                if 1 <= c <= 4:
                    pe.wait_ge(lin_evac, c)
                    if c >= 2:
                        pe.wait_ge(rs_ready, rsr.up())
                    square_sums()
            pe.wait_ge(lin_evac, 6)

            nrm = Count(normed)
            pe.wait_ge(ada_used, usedd.up(16))
            pe.wait_ge(rs_ready, rsr.up())
            mod_cols(0, 1)
            mod_gate(0, 0)
            pe.wait_ge(mod_taken, mtk.up(2))
            mod_gate(0, 1)
            pe.wait_ge(mod_taken, mtk.up())

            sr, er, pr = Count(s_ready), Count(e_ready), Count(p_ready)
            ptr, pte, orr = Count(pt_ready), Count(pt_evac), Count(o_ready)

            def heads(waves):
                def scores(w):
                    if w >= 2:
                        pe.wait_ge(e_ready, er.up())
                    for a, m in enumerate(waves[w]["heads"]):
                        bank = ps[:, 2 * (w % 2) + a, :]
                        for c0, c1, x, y in m["scores"]:
                            i = pe.matmul(bank[:, c0:c1], x, y, start=True, stop=not m["masked"], skip_group_check=True)
                            if m["masked"]:
                                i = pe.matmul(bank[:, c1 - P:c1], ident[:, :], mcausal[:, :], start=False, stop=True,
                                              skip_group_check=True)
                    i.then_inc(s_ready, 1)
                    sr.up()

                def turn(w):
                    pe.wait_ge(p_ready, pr.up())
                    if w:
                        pe.wait_ge(pt_evac, pte.value(1))
                    for a in range(2):
                        for x, y in waves[w]["turns"]:
                            i = pe.transpose(ps[:, 4 + a, y:y + P], prob(w)[:, a, x:x + P], ident[:, :])
                    i.then_inc(pt_ready, 1)
                    ptr.up()

                def outs(w):
                    pe.wait_ge(pt_evac, pte.up())
                    if w >= 2:
                        pe.wait_ge(ol_ready, olr.up())
                    rows = waves[w]["rows"]
                    for a, m in enumerate(waves[w]["heads"]):
                        r = slice(0, P) if rows == P else slice(64 * a, 64 * a + 64)
                        base = S * a if rows == P else 0
                        for q, (t0, t1, val, c0) in enumerate(m["outs"]):
                            i = pe.matmul(ps[r, 6 + w % 2, base + t0:base + t1], val, turned(w)[:, a, c0:c0 + t1 - t0],
                                          start=q == 0, stop=q == 1, skip_group_check=True)
                    i.then_inc(o_ready, 1)
                    orr.up()

                for i in range(len(waves) + 2):
                    if i < len(waves):
                        scores(i)
                    if 0 <= i - 1 < len(waves):
                        turn(i - 1)
                    if i >= 2:
                        outs(i - 2)
                er.n += 2
                pe.wait_ge(ol_ready, olr.up(2))

            pe.wait_ge(normed, nrm.up(4))
            heads(MOBA)
            out_rows()
            pe.wait_ge(xn_ready, xn.up())
            transposes(tv)
            pe.wait_ge(h_ready, hr.up(4))

            acr, atr, asp = Count(act_ready), Count(at_ready), Count(a_split)

            def ffn(ph, chunks):
                def gate_up(j):
                    for q in range(2):
                        pe.wait_ge(l_split, lsp.up())
                        u = n[0] + j + q
                        for t in range(TT):
                            for k in range(UK):
                                tok = slice(t * P, (t + 1) * P)
                                i = mm3(ps[:, t, :], hh[:, UK * q + k, tok], hl[:, UK * q + k, tok],
                                        wh[u % SPL][:, k, :], wl[u % SPL][:, k, :], q == 0 and k == 0, q == 1 and k == UK - 1)
                        i.then_inc(unit_used, 1)
                        used.up()

                def turn():
                    pe.wait_ge(act_ready, acr.up(2))
                    for k in range(2):
                        for t in range(TT):
                            i = pe.transpose(ps[:, 2, k * S + t * P:k * S + (t + 1) * P],
                                             Z[:, 512 + t * FW + k * P:512 + t * FW + (k + 1) * P], ident[:, :])
                    i.then_inc(at_ready, 1)
                    atr.up()

                def down(j, first, last):
                    pe.wait_ge(a_split, asp.up())
                    pe.wait_ge(l_split, lsp.up())
                    u = n[0] + j
                    for t in range(TT):
                        for k in range(2):
                            tok = slice(t * P, (t + 1) * P)
                            for h in range(2):
                                i = mm3(ps[:, 4 + 2 * h + t, :], ah[:, k, tok], al[:, k, tok],
                                        wh[u % SPL][:, 2 * k + h, :], wl[u % SPL][:, 2 * k + h, :],
                                        first and k == 0, last and k == 1)
                    i.then_inc(unit_used, 1)
                    used.up()

                gate_up(0)
                n[0] += 2
                turn()
                gate_up(0)
                down(2, True, False)
                n[0] += 3
                turn()
                gate_up(0)
                down(2, False, False)
                n[0] += 3
                loops, rest = divmod(chunks - 3, 2)
                with looped(pe, loops, {lsp: 6, used: 6, acr: 4, atr: 2, asp: 2}):
                    for r in range(2):
                        turn()
                        gate_up(3 * r)
                        down(3 * r + 2, False, False)
                n[0] += 6 * loops
                for _ in range(rest):
                    turn()
                    gate_up(0)
                    down(2, False, False)
                    n[0] += 3
                turn()
                down(0, False, True)
                n[0] += 1


            ffn("ffn0", NFF)
            pe.wait_ge(ada_used, usedd.up(24))
            pe.wait_ge(x_ready, 2)
            mod_cols(1, 0)
            pe.wait_ge(mod_taken, mtk.up())
            mod_cols(1, 1)
            mod_gate(1, 0)
            pe.wait_ge(mod_taken, mtk.up(2))
            mod_gate(1, 1)
            pe.wait_ge(mod_taken, mtk.up())
            pe.wait_ge(xn_ready, xn.up())
            transposes(tv)
            pe.wait_ge(h_ready, hr.up(4))
            for c in range(6):
                chunk("features")
            pe.wait_ge(h_ready, hr.up(2))
            out_rows()
            pe.wait_ge(xn_ready, xn.up())
            transposes(tv)
            pe.wait_ge(h_ready, hr.up(4))
            ffn("ffn1", NFF)

            pe.wait_ge(x_ready, 4)
            pe.wait_ge(mem_loaded, 16)
            transposes(tv)
            pe.wait_ge(h_ready, hr.up(4))
            for l in range(DEPTH):
                if True:
                    pe.wait_ge(lin_evac, evac.up())
                pair = 2 * (lin[0] % 2)
                for q in range(2):
                    pe.wait_ge(l_split, lsp.up())
                    unit_features(n[0], pair, 2, UK * q, q == 0, q == 1)
                    for t in range(TT):
                        for k in range(UK):
                            tok = slice(t * P, (t + 1) * P)
                            u = n[0]
                            i = mm3(ps[:, pair + 1, t * S:(t + 1) * S], hh[:, UK * q + k, tok], hl[:, UK * q + k, tok],
                                    wh[u % SPL][:, k, 256:512], wl[u % SPL][:, k, 256:512],
                                    q == 0 and k == 0 and t == 0, q == 1 and k == UK - 1)
                    i.then_inc(unit_used, 1)
                    used.up()
                    n[0] += 1
                lin[0] += 1
            transposes(xs)
            pe.wait_ge(h_ready, hr.up(4))
            for kind, w in (("features", 512), ("features", 512), ("features", 512), ("rows", 512), ("rows", 256),
                            ("features", 512), ("features", 512)):
                chunk(kind, w)
            pe.wait_ge(lin_evac, lin[0])
            heads(MEM[0])

            dqr, kdr, exr = Count(dk_ready), Count(kd_ready), Count(exp_ready)
            levs, levt = Count(lev_scores), Count(lev_taken)
            for l in range(9):
                pe.wait_ge(dk_ready, dqr.up())
                if l:
                    pe.wait_ge(kd_ready, kdr.up())
                if l >= 2:
                    pe.wait_ge(lev_taken, levt.up())
                o = 4 * (l % 2)
                for h in range(HG):
                    if l < 8:
                        for t in range(TT):
                            tok = slice(t * P, (t + 1) * P)
                            c = (h % 2) * S + t * P
                            i = pe.matmul(ps[:, o + h // 2, c:c + P], kd[:, h, tok], qd[:, h, tok], start=True, stop=True)
                    else:
                        i = pe.matmul(ps[:, o + h // 4, (h % 4) * P:(h % 4 + 1) * P], kd[:, h, 0:P], qd[:, h, P:S],
                                      start=True, stop=True)
                i.then_inc(lev_scores, 1)
                levs.up()
            pe.wait_ge(lev_taken, levt.up(2))
            for h in range(HG):
                o = ps[:, 4 + h // 2, (h % 2) * S:(h % 2 + 1) * S]
                v0, v1 = (tv[:, t, h * P:(h + 1) * P] for t in range(TT))
                pe.matmul(o[:, 0:P], v0, scD[:, h, 0:P], start=True, stop=True, skip_group_check=True)
                pe.matmul(o[:, P:S], v0, scX[:, h, :], start=True, stop=False, skip_group_check=True)
                i = pe.matmul(o[:, P:S], v1, scD[:, h, P:S], start=False, stop=True, skip_group_check=True)
            i.then_inc(o_ready, 1)
            orr.up()
            exr.n = 10
            pe.wait_ge(exp_ready, exr.up())
            for a in range(3):
                i = pe.matmul(ps[:, 4 + a, :], ones[:, :], qd[:, 2 * a:2 * a + 2, :].rearrange("p a t -> p (a t)"), start=True, stop=True)
            i.then_inc(sq_sum, 1)
            sqs.up()
            pe.wait_ge(ol_ready, olr.up())
            out_rows()

            def after_norm(count):
                pe.wait_ge(x_ready, count)
                transposes(xs)
                pe.wait_ge(h_ready, hr.up(4))

            def router(rows_need):
                pe.wait_ge(row_loaded, rows_need)
                for t in range(TT):
                    tok = slice(t * P, (t + 1) * P)
                    for k in range(KT):
                        for half in (hh, hl):
                            i = pe.matmul(ps[:, 7, 20 * t:20 * t + 20], half[:, k, tok].bitcast(F32), rw[:, k, :],
                                          start=k == 0 and half is hh, stop=k == KT - 1 and half is hl,
                                          skip_group_check=True)
                i.then_inc(router_sums, 1)
                rsum.up()

            rsum = Count(router_sums)
            after_norm(5)
            router(208)
            ffn("moe0", NEXP)
            after_norm(6)
            for kind, w in (("features", 512), ("features", 256), ("rows", 512), ("rows", 256)):
                chunk(kind, w)
            for c in range(2):
                chunk("features")
            pe.wait_ge(lin_evac, lin[0])
            heads(MEM[1])

            rr, spr, ar = Count(rest_ready), Count(sp_ready), Count(a_ready)
            for i in range(SBH // 2 + 2):
                if i >= 2:
                    w = i - 2
                    pe.wait_ge(a_ready, ar.up())
                    if w >= 2:
                        pe.wait_ge(ol_ready, olr.up())
                    for a in range(2):
                        h, nb = 2 * w + a, sb_buf(w)[:, a, :]
                        o = ps[64 * a:64 * a + 64, 4 + w % 2, 0:S]
                        pe.matmul(o, tv[:, 0, 64 * h:64 * h + 64], nb[:, 0:S], start=True, stop=False, skip_group_check=True)
                        j = pe.matmul(o[:, P:S], tv[:, 1, 64 * h:64 * h + 64], nb[:, S:S + P], start=False, stop=True,
                                      skip_group_check=True)
                    j.then_inc(o_ready, 1)
                    orr.up()
                if i < SBH // 2:
                    for a in range(2):
                        r, bank = slice(64 * a, 64 * a + 64), ps[:, 2 * (i % 2) + a, :]
                        q, k = FT[r, i, :], FT[r, 6 + i, :]
                        pe.matmul(bank[:, 0:S], k[:, 0:P], q[:, :], start=True, stop=False, skip_group_check=True)
                        j = pe.matmul(bank[:, S:S + P], k[:, P:S], q[:, P:S], start=False, stop=False, skip_group_check=True)
                    j.then_inc(s_ready, 1)
                    sr.up()
                if 0 <= i - 1 < SBH // 2:
                    pe.wait_ge(sp_ready, spr.up())
                    for a in range(2):
                        bank, nb = ps[:, 2 * ((i - 1) % 2) + a, :], sb_buf(i - 1)[:, a, :]
                        pe.matmul(bank[:, 0:S], ntri[:, :], nb[:, 0:S], start=False, stop=False, skip_group_check=True)
                        pe.matmul(bank[:, P:S], nones, nb[:, S:S + P], start=False, stop=False, skip_group_check=True)
                        j = pe.matmul(bank[:, S:S + P], ntri[:, :], nb[:, S:S + P], start=False, stop=True, skip_group_check=True)
                    j.then_inc(rest_ready, 1)
                    rr.up()
            pe.wait_ge(ol_ready, olr.up(2))
            out_rows()
            after_norm(7)
            router(336)
            ffn("moe1", NEXP)


_INS = ["x", "w_ada", "b_ada", "w_qkv", "w_o", "w_in", "w_out", "w_gate_up", "w_down", "mem_2", "a_w_in_2", "b_w_in_2",
        "w_kv_shared_2", "w_mem_kv_2", "w_o_2", "ln_mix_g_2", "ln_mix_b_2", "ln_ffn_g_2", "ln_ffn_b_2", "w_group_2",
        "b_group_2", "w_router_2", "b_router_2", "w_gate_2", "w_up_2", "w_down_2"]


def kernel(**inputs):
    import numpy as _np
    import concourse.bacc as _bacc
    from concourse import mybir as _mybir
    from concourse.bass_utils import run_bass_kernel_spmd as _run

    give = {name: _np.ascontiguousarray(inputs[name]) for name in _INS}
    give["cols"] = _np.ascontiguousarray(_np.concatenate(
        [_np.asarray(inputs[name]).reshape(-1, 128) for name in
         ("c", "norm_mix", "norm_ffn", "conv_w", "q_gain", "k_gain", "a_gnorm_2", "b_ada")]).T)
    i = _np.arange(128)
    give["k_ident"] = _np.eye(128, dtype=_np.float32)
    give["k_ones"] = _np.ones((128, 128), _np.float32)
    give["k_ntri"] = -(i[:, None] >= i[None, :]).astype(_np.float32)
    causal = _np.where(i[:, None] >= i[None, :], 0.0, -1e30).astype(_np.float32)
    give["k_causal"] = causal
    strict = (i[:, None] < i[None, :]).astype(_np.float32)
    give["k_strict"] = _np.concatenate([strict, _np.ones_like(strict), strict], axis=1)
    give["k_nstrict"] = ((give["k_strict"] - 1) * 1e30).astype(_np.float32)
    give["k_nones"] = -give["k_ones"]
    levels = [i[:, None] == i[None, :]]
    for m in (1, 2, 4, 8, 16, 32, 64):
        same = (i[:, None] // (2 * m)) == (i[None, :] // (2 * m))
        levels.append(same & ((i[:, None] // m) % 2 == 0) & ((i[None, :] // m) % 2 == 1))
    give["k_levels"] = _np.stack(levels, axis=1).reshape(128, 8 * 128).astype(_np.float32)

    nc = _bacc.Bacc("TRN2", target_bir_lowering=False, num_devices=1)
    arrays = {f"in_{name}": a for name, a in give.items()}
    A = {name: nc.dram_tensor(f"in_{name}", a.shape, _mybir.dt.from_np(a.dtype), kind="ExternalInput").ap()
         for name, a in give.items()}
    out = nc.dram_tensor("out_0", (1, S, D), _mybir.dt.float32, kind="ExternalOutput").ap()
    build(nc, A, out)
    r = _run(nc, [arrays], core_ids=[0])
    return r.results[0]["out_0"]
```

```python
from contextlib import ExitStack, contextmanager

import concourse.bass as bass
from concourse import mybir

F32 = mybir.dt.float32
F32R = mybir.dt.float32r
U8 = mybir.dt.uint8
ALU = mybir.AluOpType
ACT = mybir.ActivationFunctionType
AX = mybir.AxisListType

P = 128
S = 256
TT = S // P
D = 1024
KT = D // P
NC = 512
UK = 4
RAW = 6
SPL = 3
DEPTH = 2
HEADS = 8
FF = 2816
FW = 256
NFF = FF // FW
NEXP = 16
MIX = 768
HG = MIX // P
SBH = MIX // 64
EPS = 1e-6
LN_EPS = 1e-5
ALPHA = (2 * DEPTH) ** 0.25


class Count:

    def __init__(self, sem):
        self.sem, self.n, self.per, self.it = sem, 0, 0, None

    def value(self, ahead=0):
        return self.n + ahead if self.it is None else self.it * self.per + (self.n + ahead)

    def up(self, by=1):
        self.n += by
        return self.value()


@contextmanager
def looped(eng, times, counts):
    base = {c: c.n for c in counts}
    with eng.Fori(0, times, 1) as it:
        for c, per in counts.items():
            c.per, c.it = per, it
        yield it
    for c, per in counts.items():
        assert c.n == base[c] + per, (c.sem, c.n, base[c], per)
        c.n, c.per, c.it = base[c] + per * times, 0, None


def narrow_units():
    out = {}
    for name, ws in (("a_in", (512, 512, 512, 512, 256, 512, 512)), ("kv", (512, 256, 512, 256))):
        for i, w in enumerate(ws):
            if w < NC:
                out[PLAN[name] + 2 * i] = out[PLAN[name] + 2 * i + 1] = w
    return out


def stream_plan():
    at, plan = 0, {}
    for name, units in (("qkv", 12), ("wo0", 4), ("ffn0", 3 * NFF), ("win", 12), ("wout", 4), ("ffn1", 3 * NFF),
                        ("mem", 4), ("a_in", 14), ("wo1", 4), ("moe0", 3 * NEXP), ("kv", 8), ("b_in", 4),
                        ("wo2", 4), ("moe1", 3 * NEXP)):
        plan[name] = at
        at += units
    plan["end"] = at
    return plan


PLAN = stream_plan()

C_C, C_NMIX, C_NFFN, C_CONV, C_QG, C_KG, C_GN, C_BADA, C_LN = 0, 8, 24, 40, 64, 65, 66, 72, 168
NCOL = 232


def build(nc, A, out):
    ctx = ExitStack()
    with ctx:
        def sb(name, shape, dt=F32):
            return ctx.enter_context(nc.sbuf_tensor(name, shape, dt))

        def sem(name):
            return ctx.enter_context(nc.semaphore(name))

        raw = [sb(f"raw{i}", [P, UK, NC]) for i in range(RAW)]
        wh = [sb(f"w_high{i}", [P, UK, NC], F32R) for i in range(SPL)]
        wl = [sb(f"w_low{i}", [P, UK, NC], F32R) for i in range(SPL)]
        xs = sb("x_rows", [P, TT, D])
        hh = sb("h_high", [P, KT, S], F32R)
        hl = sb("h_low", [P, KT, S], F32R)
        FT = sb("features", [P, 20, S])
        tv = sb("rows", [P, TT, D])
        W = sb("scratch", [P, 41 * 256])
        Z = sb("small", [P, 8 * 256])
        ah = sb("act_high", [P, 2, S], F32R)
        al = sb("act_low", [P, 2, S], F32R)
        ident = sb("ident", [P, P])
        ones = sb("ones", [P, P])
        ntri = sb("minus_tri", [P, P])
        mcausal = sb("mask_causal", [P, P])
        mlev = sb("mask_levels", [P, 8, P], U8)
        cols = sb("cols", [P, NCOL])
        scol = sb("silu_c", [P, 8])
        modA = sb("mod_scale", [P, 16])
        modB = sb("mod_shift", [P, 16])
        st = sb("stats", [P, 64])
        gate = sb("gates", [P, TT, NEXP])
        rwh = sb("router_high", [P, KT, 20], F32R)
        rwl = sb("router_low", [P, KT, 20], F32R)

        cring = W[:, 0:16 * 256].rearrange("p (s k n) -> p s k n", s=2, k=UK)
        accw = W[:, 16 * 256:32 * 256].rearrange("p (c n) -> p c n", n=NC)
        gb = W[:, 32 * 256:40 * 256].rearrange("p (g n) -> p g n", g=2)
        pfx = W[:, 0:6 * 256].rearrange("p (h t) -> p h t", h=HG)
        sfx = W[:, 6 * 256:12 * 256].rearrange("p (h t) -> p h t", h=HG)
        qd = W[:, 12 * 256:18 * 256].rearrange("p (h t) -> p h t", h=HG)
        kd = W[:, 18 * 256:24 * 256].rearrange("p (h t) -> p h t", h=HG)
        scD = W[:, 24 * 256:30 * 256].rearrange("p (h t) -> p h t", h=HG)
        scX = W[:, 30 * 256:33 * 256].rearrange("p (h t) -> p h t", h=HG)
        nstrict = W[:, 24 * 256:24 * 256 + 384]
        nones = W[:, 26 * 256:26 * 256 + P]
        mk = W[:, 33 * 256:37 * 256].rearrange("p (l b m) -> p l b m", l=2, b=2)
        mv = W[:, 37 * 256:41 * 256].rearrange("p (l t n) -> p l t n", l=2, t=2)
        lnv = W[:, 0:8 * 256].rearrange("p (g n) -> p g n", g=2)
        mstrict = W[:, 8 * 256:8 * 256 + 384]
        rw = W[:, 10 * 256:10 * 256 + 160].rearrange("p (k n) -> p k n", k=KT)
        rbias = W[:, 11 * 256:11 * 256 + 20]
        rt = W[:, 12 * 256:20 * 256]

        ps = ctx.enter_context(nc.psum_tensor("ps", [P, 8, 512], F32))

        raw_loaded = [sem(f"raw_loaded{i}") for i in range(RAW)]
        small_loaded = sem("small_loaded")
        x_loaded = sem("x_loaded")
        ada_loaded = [sem(f"ada_loaded{i}") for i in range(2)]
        row_loaded = sem("row_loaded")
        mem_loaded = sem("mem_loaded")
        h_split = sem("h_split")
        l_split = sem("l_split")
        unit_used = sem("unit_used")
        act_step = sem("act_step")
        dve_step = sem("dve_step")
        ada_used = sem("ada_used")
        ada_acc = sem("ada_acc")
        sc_ready = sem("sc_ready")
        mod_sums = sem("mod_sums")
        mod_taken = sem("mod_taken")
        root_ready = sem("root_ready")
        stat_ready = sem("stat_ready")
        x0_ready = sem("x0_ready")
        row0_ready = sem("row0_ready")
        xn_ready = sem("xn_ready")
        xt_ready = sem("xt_ready")
        v_ready = sem("v_ready")
        hh_ready = sem("hh_ready")
        h_ready = sem("h_ready")
        lin_evac = sem("lin_evac")
        lin_taken = sem("lin_taken")
        sq_sum = sem("sq_sum")
        rs_ready = sem("rs_ready")
        normed = sem("normed")
        x_ready = sem("x_ready")
        s_ready = sem("s_ready")
        nmax_ready = sem("nmax_ready")
        e_ready = sem("e_ready")
        p_ready = sem("p_ready")
        pt_ready = sem("pt_ready")
        pt_evac = sem("pt_evac")
        o_ready = sem("o_ready")
        oh_ready = sem("oh_ready")
        ol_ready = sem("ol_ready")
        l_ready = sem("l_ready")
        sp_ready = sem("sp_ready")
        rest_ready = sem("rest_ready")
        la_ready = sem("la_ready")
        a_ready = sem("a_ready")
        sil_ready = sem("sil_ready")
        act_ready = sem("act_ready")
        at_ready = sem("at_ready")
        ah_ready = sem("ah_ready")
        a_split = sem("a_split")
        qk_in = sem("qk_in")
        dk_ready = sem("dk_ready")
        lev_scores = sem("lev_scores")
        lev_taken = sem("lev_taken")
        exp_ready = sem("exp_ready")
        router_ready = sem("router_ready")
        rw_high = sem("rw_high")
        rw_low = sem("rw_low")
        router_sums = sem("router_sums")
        kd_ready = sem("kd_ready")
        sums_ready = sem("sums_ready")
        ln_applied = sem("ln_applied")
        pool_step = sem("pool_step")
        out_done = sem("out_done")

        block = ctx.enter_context(nc.Block())

        used_until = PLAN["end"]

        def layer0_acc(c):
            if c >= 10:
                return FT[:, 2 * c - 4:2 * c - 2, :].rearrange("p a t -> p (a t)")
            return accw[:, c - 4 if c < 6 else c - 2, :]

        def mod(which):
            return modA[:, 8 * which:8 * which + 8], modB[:, 8 * which:8 * which + 8]

        def ln_cols(kind, layer):
            o = C_LN + 32 * kind + 8 * layer
            return cols[:, o:o + 8], cols[:, o + 16:o + 24]

        def moba_wave(w):
            heads = []
            for h in (2 * w, 2 * w + 1):
                q, k, v = FT[:, h, :], FT[:, 8 + h, :], tv[:, :, h * P:(h + 1) * P]
                heads.append(dict(
                    scores=((0, P, q[:, 0:P], k[:, 0:P]), (P, 3 * P, q[:, P:S], k[:, 0:S])),
                    masked=(0, 2 * P), outs=((0, S, v[:, 0, :], 0), (P, S, v[:, 1, :], 2 * P))))
            return dict(heads=heads, w=3 * P, spans=((0, P), (P, 3 * P)), turns=((0, 0), (P, P), (2 * P, 2 * P)),
                        blk=2 * w, nb=2, rows=P, turned=16 * 256)

        def mem_wave(l, w):
            heads = []
            for a in range(2):
                r = slice(64 * a, 64 * a + 64)
                q, k = FT[r, 18 + w, :], mk[r, l, w, :]
                v = mv[:, l, :, 128 * w + 64 * a:128 * w + 64 * a + 64]
                heads.append(dict(
                    scores=((0, S, q[:, 0:P], k), (S, 2 * S, q[:, P:S], k)), masked=(),
                    outs=((0, S, v[:, 0, :], 0), (0, S, v[:, 1, :], 2 * P))))
            return dict(heads=heads, w=4 * P, spans=((0, S), (S, 2 * S)),
                        turns=((0, 0), (P, 2 * P), (2 * P, P), (3 * P, 3 * P)), blk=HG + w, nb=1, rows=64,
                        turned=(16 if l else 24) * 256)

        MOBA = [moba_wave(w) for w in range(HEADS // 2)]
        MEM = [[mem_wave(l, w) for w in range(2)] for l in range(2)]

        def prob(w):
            return Z[:, (w % 2) * 1024:(w % 2 + 1) * 1024].rearrange("p (a c) -> p a c", a=2)

        def turned(w, m):
            o = m["turned"] + (w % 2) * 1024
            return W[:, o:o + 1024].rearrange("p (a c) -> p a c", a=2)

        def out_of(w, m):
            return ps[:, 6 + w % 2, 0:S * m["nb"]].rearrange("p (b t) -> p b t", t=S)

        def sb_buf(w):
            o = 16 * 256 if w % 3 == 2 else (w % 3) * 1024
            return (W if w % 3 == 2 else Z)[:, o:o + 768].rearrange("p (a c) -> p a c", a=2)

        def halves(x, m):
            return x.rearrange("p h (b c m) -> p (h b) c m", c=2, m=m)

        def level_exps(m, kind):
            return Z[:, 768 * kind:768 * kind + 768].rearrange("p (b m) -> p b m", m=m)

        @block.sync
        def _(sp):
            xr = A["x"].rearrange("b (t p) d -> p (b t) d", p=P)
            for dst, src in ((cols[:, :], A["cols"]), (ident[:, :], A["k_ident"]), (ones[:, :], A["k_ones"]),
                             (ntri[:, :], A["k_ntri"]), (mcausal[:, :], A["k_causal"]),
                             (Z[:, 0:8 * P], A["k_levels"])):
                sp.dma_start(dst, src).then_inc(small_loaded, 16)
            sp.dma_start(xs[:, :, :], xr).then_inc(x_loaded, 16)

            hsp, lsp = Count(h_split), Count(l_split)
            n = [0]

            def load(src_a, src_b, dst_a, dst_b, j=0):
                u = n[0] + j
                slot = u % RAW
                if u >= RAW or hsp.it is not None:
                    sp.wait_ge(h_split, hsp.up())
                    sp.wait_ge(l_split, lsp.up())
                elif u < 4:
                    sp.wait_ge(ada_loaded[0], 16 * (u + 1))
                sp.dma_start(dst_a(raw[slot]), src_a).then_inc(raw_loaded[slot], 16)
                sp.dma_start(dst_b(raw[slot]), src_b).then_inc(raw_loaded[slot], 16)

            def columns(w, c0, width):
                v = w.rearrange("(k p) n -> p k n", p=P)
                for k in (0, UK):
                    load(v[:, k:k + 2, c0:c0 + width], v[:, k + 2:k + 4, c0:c0 + width],
                         lambda r: r[:, 0:2, 0:width], lambda r: r[:, 2:4, 0:width])
                    n[0] += 1

            def gate_up(wg, wu, c0, j):
                g, u = (w.rearrange("(k p) n -> p k n", p=P) for w in (wg, wu))
                for q, k in enumerate((0, UK)):
                    load(g[:, k:k + UK, c0], u[:, k:k + UK, c0],
                         lambda r: r[:, :, 0:FW], lambda r: r[:, :, FW:2 * FW], j + q)

            def down(wd, c0, j):
                d = wd[c0, :].rearrange("(k p) (h n) -> p k h n", p=P, h=2)
                load(d[:, 0, :, :], d[:, 1, :, :], lambda r: r[:, 0:2, :], lambda r: r[:, 2:4, :], j)

            def ffn(chunks, gu, dn):
                gu(0, 0)
                n[0] += 2
                loops, rest = divmod(chunks - 1, 2)
                with looped(sp, loops, {hsp: 6, lsp: 6}) as it:
                    for r in range(2):
                        gu(it * 2 + (r + 1), 3 * r)
                        dn(it * 2 + r, 3 * r + 2)
                n[0] += 6 * loops
                for c in range(2 * loops + 1, chunks):
                    gu(c, 0)
                    dn(c - 1, 2)
                    n[0] += 3
                dn(chunks - 1, 0)
                n[0] += 1

            def dense_ffn(layer):
                w, wd = A["w_gate_up"][layer], A["w_down"][layer]
                ffn(NFF, lambda c, j: gate_up(w[:, 0:FF], w[:, FF:2 * FF], bass.ds(c * FW, FW), j),
                    lambda c, j: down(wd, bass.ds(c * FW, FW), j))

            def moe(layer):
                wg, wu = (A[name][layer].rearrange("e d f -> (e d) f") for name in ("w_gate_2", "w_up_2"))
                wd = A["w_down_2"][layer].rearrange("e f d -> (e f) d")

                def gu(e, j):
                    g, u = (w[bass.ds(e * D, D), :].rearrange("(k p) n -> p k n", p=P) for w in (wg, wu))
                    for q, k in enumerate((0, UK)):
                        load(g[:, k:k + UK, :], u[:, k:k + UK, :],
                             lambda r: r[:, :, 0:FW], lambda r: r[:, :, FW:2 * FW], j + q)
                ffn(NEXP, gu, lambda e, j: down(wd, bass.ds(e * FW, FW), j))

            for c in range(6):
                columns(A["w_qkv"][0], c * NC, NC)
            for c in range(2):
                columns(A["w_o"][0], c * NC, NC)
            dense_ffn(0)
            for c in (2, 3, 4, 5, 0, 1):
                columns(A["w_in"][0], c * NC, NC)
            for c in range(2):
                columns(A["w_out"][0], c * NC, NC)
            dense_ffn(1)
            for l in range(DEPTH):
                columns(A["w_mem_kv_2"][l], 0, NC)
            for c0, w in ((0, 512), (512, 512), (1024, 512), (1536, 512), (2048, 256), (2304, 512), (2816, 512)):
                columns(A["a_w_in_2"][0], c0, w)
            for c in range(2):
                columns(A["w_o_2"][0], c * NC, NC)
            moe(0)
            for c0, w in ((0, 512), (512, 256), (768, 512), (1280, 256)):
                columns(A["w_kv_shared_2"], c0, w)
            for c in range(2):
                columns(A["b_w_in_2"][0], c * NC, NC)
            for c in range(2):
                columns(A["w_o_2"][1], c * NC, NC)
            moe(1)
            xrd = Count(x_ready)
            sp.wait_ge(x_ready, xrd.up(8))
            sp.dma_start(out.rearrange("b (t p) d -> p (b t) d", p=P), xs[:, :, :]).then_inc(out_done, 16)
            sp.wait_ge(out_done, 16)

        @block.gpsimd
        def _(pool):
            used = Count(ada_used)

            def ada(layer):
                v = A["w_ada"][layer].rearrange("(k p) n -> p k n", p=P)

                def chunk(c, first):
                    for q in range(2):
                        if not first:
                            pool.wait_ge(ada_used, used.up())
                        pool.dma_start(cring[:, q, :, :], v[:, q * UK:(q + 1) * UK, bass.ds(c * NC, NC)]) \
                            .then_inc(ada_loaded[q], 16)
                if layer == 0:
                    chunk(0, True)
                    with looped(pool, 11, {used: 2}) as it:
                        chunk(it + 1, False)
                else:
                    with looped(pool, 12, {used: 2}) as it:
                        chunk(it, False)

            def gate_rows(layer):
                for g, c0 in enumerate((2 * D, 5 * D)):
                    pool.dma_start(gb[:, g, :], A["b_ada"][layer:layer + 1, c0:c0 + D].to_broadcast([P, D])) \
                        .then_inc(row_loaded, 16)

            xrd = Count(x_ready)
            gate_rows(0)
            ada(0)
            ada(1)
            pool.wait_ge(x_ready, xrd.up(2))
            gate_rows(1)
            pool.wait_ge(x_ready, xrd.up(2))
            olr = Count(ol_ready)

            def ln_rows(kind, layer):
                pool.dma_start(lnv[:, 0, :], A[f"ln_{kind}_g_2"][layer:layer + 1, :].to_broadcast([P, D])) \
                    .then_inc(row_loaded, 16)
                pool.dma_start(lnv[:, 1, :], A[f"ln_{kind}_b_2"][layer:layer + 1, :].to_broadcast([P, D])) \
                    .then_inc(row_loaded, 16)

            def router_rows(layer):
                pool.dma_start(rw[:, :, 0:4], A["w_group_2"][layer].rearrange("(k p) n -> p k n", p=P)) \
                    .then_inc(row_loaded, 16)
                pool.dma_start(rw[:, :, 4:20], A["w_router_2"][layer].rearrange("(k p) n -> p k n", p=P)) \
                    .then_inc(row_loaded, 16)
                pool.dma_start(rbias[:, 0:4], A["b_group_2"][layer:layer + 1, :].to_broadcast([P, 4])) \
                    .then_inc(row_loaded, 16)
                pool.dma_start(rbias[:, 4:20], A["b_router_2"][layer:layer + 1, :].to_broadcast([P, 16])) \
                    .then_inc(row_loaded, 16)

            pool.dma_start(tv[:, :, :], A["mem_2"].rearrange("b (t p) d -> p (b t) d", p=P)).then_inc(mem_loaded, 16)
            exr, levs, kdr = Count(exp_ready), Count(lev_scores), Count(kd_ready)
            kk = FT[:, 6:12, :]
            exr.n = 2
            for l in range(1, 9):
                m = 2 ** (l - 1)
                pool.wait_ge(exp_ready, exr.up())
                pool.wait_ge(lev_scores, levs.up())
                pool.tensor_tensor(halves(kd, m)[:, :, 0, :], level_exps(m, 1), halves(kk, m)[:, :, 0, :], ALU.mult).then_inc(kd_ready, 1)
                kdr.up()
            pool.wait_ge(ol_ready, olr.up(len(MOBA) + len(MEM[0]) + 1))
            ln_rows("mix", 0)
            router_rows(0)
            for dst, src in ((mstrict, "k_strict"), (nstrict, "k_nstrict"), (nones, "k_nones")):
                pool.dma_start(dst, A[src]).then_inc(row_loaded, 16)
            pst, lnd = Count(pool_step), Count(ln_applied)

            def apply_rows(turns):
                pool.wait_ge(x_ready, xrd.up())
                pool.wait_ge(xt_ready, 4 * turns)
                pool.wait_ge(row_loaded, ROWS[turns])
                for t in range(TT):
                    pool.tensor_tensor(xs[:, t, :], xs[:, t, :], lnv[:, 0, :], ALU.mult).then_inc(pool_step, 1)
                    pool.wait_ge(pool_step, pst.up())
                    pool.tensor_tensor(xs[:, t, :], xs[:, t, :], lnv[:, 1, :], ALU.add).then_inc(ln_applied if t else pool_step, 1)
                    pool.wait_ge(ln_applied if t else pool_step, (lnd if t else pst).up())

            ROWS = {7: 208, 8: 240, 9: 336}
            apply_rows(7)
            ln_rows("ffn", 0)
            apply_rows(8)
            ln_rows("mix", 1)
            router_rows(1)
            apply_rows(9)
            ln_rows("ffn", 1)

        @block.scalar
        def _(act):
            step = Count(act_step)
            hsp, used = Count(h_split), Count(unit_used)
            n = [0]
            LIMIT = PLAN["end"]
            widths = narrow_units()

            def split(j=0, waited=False):
                u = n[0] + j
                if u >= LIMIT:
                    return
                w = widths.get(u, NC)
                loaded = 32 * (u // RAW + 1)
                act.wait_ge(raw_loaded[u % RAW], loaded if hsp.it is None else hsp.it * 32 + loaded)
                if u >= SPL and not waited:
                    act.wait_ge(unit_used, used.up())
                act.activation(wh[u % SPL][:, :, 0:w], raw[u % RAW][:, :, 0:w], ACT.Copy).then_inc(h_split, 1)
                hsp.up()

            def ahead(upto):
                while n[0] < upto + SPL:
                    split()
                    n[0] += 1

            xt, v, hhr = Count(xt_ready), Count(v_ready), Count(hh_ready)
            rtr, xrd, x0r = Count(root_ready), Count(x_ready), Count(x0_ready)
            evac = Count(lin_evac)
            eps_col = {EPS: st[:, 60:61], LN_EPS: st[:, 61:62]}

            stat = Count(stat_ready)

            def root_of(src, width, eps):
                act.activation(st[:, 2:4], src, ACT.Sqrt, bias=eps_col[eps], scale=1.0 / width).then_inc(root_ready, 1)
                act.wait_ge(root_ready, rtr.up())

            def root_table():
                act.activation(st[:, 63:64], st[:, 60:61], ACT.Sqrt).then_inc(act_step, 1)
                act.wait_ge(act_step, step.up())

            def ln_stats():
                root_table()
                act.wait_ge(stat_ready, stat.up())
                root_of(st[:, 57:60:2], 1, LN_EPS)

            def rms_stats(first=False):
                root_table()
                for t in range(TT):
                    if not first:
                        act.wait_ge(x_ready if t else x0_ready, (xrd if t else x0r).up())
                    act.activation(tv[:, t, :], xs[:, t, :], ACT.Square, accum_out=st[:, t:t + 1]).then_inc(act_step, 1)
                    act.wait_ge(act_step, step.up())
                root_of(st[:, 0:2], D, EPS)

            def bank_k(g):
                return ps[:, 4 + g, :].rearrange("p (k t) -> p k t", k=2)

            def transposed_mod(scale, shift, taken):
                if taken:
                    act.wait_ge(mod_taken, taken)
                for g in range(0, 4, 2):
                    act.wait_ge(xt_ready, xt.up(2))
                    for q in range(2):
                        k, b = 2 * g + 2 + q, ps[:, 5 + g, q * S:(q + 1) * S]
                        act.activation(b, b, ACT.Identity, bias=shift[:, k:k + 1], scale=scale[:, k:k + 1]).then_inc(act_step, 1)
                        act.wait_ge(act_step, step.up())
                    act.wait_ge(v_ready, v.up())
                    for j in (g, g + 1):
                        act.activation(hh[:, 2 * j:2 * j + 2, :], bank_k(j), ACT.Copy).then_inc(hh_ready, 1)
                        hhr.up()

            def transposed():
                for g in range(4):
                    act.wait_ge(xt_ready, xt.up())
                    act.activation(hh[:, 2 * g:2 * g + 2, :], bank_k(g), ACT.Copy).then_inc(hh_ready, 1)
                    hhr.up()

            act.wait_ge(small_loaded, 96)
            scr = Count(sc_ready)
            act.activation(scol[:, :], cols[:, C_C:C_C + 8], ACT.Exp, scale=-1.0).then_inc(sc_ready, 1)
            scr.up()
            act.wait_ge(x_loaded, 16)
            act.wait_ge(dve_step, 2)
            rms_stats(True)
            ahead(0)
            transposed_mod(*mod(0), 1)

            lin = [0]

            def pair(b=0, e=2):
                return ps[:, 2 * (lin[0] % 2) + b:2 * (lin[0] % 2) + e, :]

            def chunk_ready(ph, c):
                ahead(PLAN[ph] + 2 * c + 1)
                act.wait_ge(unit_used, PLAN[ph] + 2 * c + 2)

            sqs, rsr, nrm = Count(sq_sum), Count(rs_ready), Count(normed)
            sq, rs = Z[:, 0:1024], Z[:, 1024:2048]

            def qk_rs():
                act.wait_ge(sq_sum, sqs.up())
                if rsr.n:
                    act.wait_ge(normed, nrm.up())
                act.activation(rs, ps[:, 4:6, :].rearrange("p a b -> p (a b)"), ACT.Ln, bias=eps_col[EPS], scale=1.0 / P).then_inc(act_step, 1)
                act.wait_ge(act_step, step.up())
                act.activation(rs, rs, ACT.Exp, scale=-0.5).then_inc(rs_ready, 1)
                act.wait_ge(rs_ready, rsr.up())

            for c in range(6):
                chunk_ready("qkv", c)
                if c < 4:
                    act.activation(FT[:, 4 * c:4 * c + 4, :].rearrange("p k t -> p (k t)"),
                                                  pair().rearrange("p a b -> p (a b)"), ACT.Copy).then_inc(act_step, 1)
                    act.wait_ge(act_step, step.up())
                    if c:
                        qk_rs()
                    act.activation(sq, pair().rearrange("p a b -> p (a b)"), ACT.Square).then_inc(lin_evac, 1)
                    act.wait_ge(lin_evac, evac.up())
                else:
                    if c == 4:
                        qk_rs()
                    act.activation(tv[:, :, (c - 4) * NC:(c - 3) * NC], pair(), ACT.Copy).then_inc(lin_evac, 1)
                    act.wait_ge(lin_evac, evac.up())
                lin[0] += 1
            ahead(PLAN["wo0"])

            nmx, er = Count(nmax_ready), Count(e_ready)
            ptr, pte = Count(pt_ready), Count(pt_evac)
            orr, ohr = Count(o_ready), Count(oh_ready)

            def head_out(src, dst):
                act.wait_ge(o_ready, orr.up())
                act.activation(dst, src, ACT.Copy).then_inc(oh_ready, 1)
                act.wait_ge(oh_ready, ohr.up())

            def heads(waves):
                def exps(w):
                    act.wait_ge(nmax_ready, nmx.up())
                    for a in range(2):
                        for t, (c0, c1) in enumerate(waves[w]["spans"]):
                            c = 4 * (w % 2) + 2 * a + t
                            i = act.activation(prob(w)[:, a, c0:c1], ps[:, 2 * (w % 2) + a, c0:c1], ACT.Exp,
                                               bias=st[:, 8 + c:9 + c], accum_out=st[:, 16 + c:17 + c])
                            if a == t == 1:
                                i.then_inc(e_ready, 1)
                                act.wait_ge(e_ready, er.up())
                            else:
                                i.then_inc(act_step, 1)
                                act.wait_ge(act_step, step.up())

                def turn_out(w):
                    act.wait_ge(pt_ready, ptr.up())
                    c = waves[w]["w"]
                    act.activation(turned(w, waves[w])[:, :, 0:c], ps[:, 4:6, 0:c], ACT.Copy).then_inc(pt_evac, 1)
                    act.wait_ge(pt_evac, pte.up())

                for i in range(len(waves) + 2):
                    if i < len(waves):
                        exps(i)
                    if 0 <= i - 1 < len(waves):
                        turn_out(i - 1)
                    if i >= 2:
                        m = waves[i - 2]
                        head_out(out_of(i - 2, m), hh[:, m["blk"]:m["blk"] + m["nb"], :])

            heads(MOBA)

            def wo(ph):
                ahead(PLAN[ph] + 1)
                ahead(PLAN[ph] + 4)

            def norm_first(which, taken):
                rms_stats()
                transposed_mod(*mod(which), taken)

            wo("wo0")
            norm_first(1, 3)

            silr, atr, ahr = Count(sil_ready), Count(at_ready), Count(ah_ready)

            def ffn(ph, chunks):
                def silu():
                    act.wait_ge(unit_used, used.up())
                    act.activation(Z[:, 0:512].rearrange("p (t n) -> p t n", t=2), ps[:, 0:2, 0:FW], ACT.Silu).then_inc(sil_ready, 1)
                    silr.up()

                def high():
                    act.wait_ge(at_ready, atr.up())
                    act.activation(ah[:, :, :], ps[:, 2, :].rearrange("p (k t) -> p k t", k=2), ACT.Copy).then_inc(ah_ready, 1)
                    ahr.up()

                def chunk(j):
                    high()
                    split(j)
                    silu()
                    split(j + 1, True)
                    split(j + 2)

                ahead(PLAN[ph])
                assert n[0] == PLAN[ph] + SPL
                split()
                silu()
                split(1, True)
                n[0] += 2
                loops = (chunks - 1) // 2
                with looped(act, loops, {hsp: 6, used: 6, silr: 2, atr: 2, ahr: 2}):
                    chunk(0)
                    chunk(3)
                n[0] += 6 * loops
                for _ in range(chunks - 1 - 2 * loops):
                    chunk(0)
                    n[0] += 3
                high()

            ffn("ffn0", NFF)
            ahead(PLAN["win"])
            norm_first(0, 5)

            ptk = Count(lin_taken)
            for c in range(6):
                chunk_ready("win", c)
                if c < 2:
                    i = act.activation(FT[:, 4 * c:4 * c + 4, :].rearrange("p k t -> p (k t)"),
                                       pair().rearrange("p a b -> p (a b)"), ACT.Copy)
                else:
                    i = act.activation(Z[:, 0:1024] if c % 2 == 0 else Z[:, 1024:2048],
                                       pair().rearrange("p a b -> p (a b)"), ACT.Copy)
                i.then_inc(lin_evac, 1)
                act.wait_ge(lin_evac, evac.up())
                lin[0] += 1
                if c in (2, 3, 4, 5):
                    act.wait_ge(lin_taken, ptk.up())
            ahead(PLAN["wout"])
            for g in range(2):
                act.activation(hh[:, 4 * g:4 * g + 4, :], Z[:, 1024 * g:1024 * g + 1024].rearrange("p (k t) -> p k t", k=4), ACT.Copy).then_inc(hh_ready, 1)
                hhr.up()
            wo("wout")
            norm_first(1, 7)
            ffn("ffn1", NFF)
            ahead(PLAN["mem"])
            act.wait_ge(x_ready, xrd.up())

            transposed()
            for l in range(DEPTH):
                chunk_ready("mem", l)
                act.activation(mk[:, l, :, :].rearrange("p b m -> p (b m)"), pair(0, 1).rearrange("p a b -> p (a b)"), ACT.Copy).then_inc(act_step, 1)
                act.wait_ge(act_step, step.up())
                act.activation(mv[:, l, :, :].rearrange("p b m -> p (b m)"), pair(1, 2).rearrange("p a b -> p (a b)"), ACT.Copy).then_inc(lin_evac, 1)
                act.wait_ge(lin_evac, evac.up())
                lin[0] += 1
            ahead(PLAN["a_in"])
            transposed()

            def features(b0, nb, func, last=True, skip=0, scale=1.0):
                src = pair().rearrange("p a (b t) -> p (a b) t", t=S)[:, skip:skip + nb, :]
                act.activation(FT[:, b0:b0 + nb, :], src, func, scale=scale).then_inc(lin_evac if last else act_step, 1)
                act.wait_ge(lin_evac if last else act_step, (evac if last else step).up())

            def rows(c0, w):
                act.activation(tv[:, :, c0:c0 + w], pair()[:, :, 0:w], ACT.Copy).then_inc(lin_evac, 1)
                act.wait_ge(lin_evac, evac.up())

            exr, dkr, upd = Count(exp_ready), Count(qk_in), Count(sums_ready)
            dqr, kdr = Count(dk_ready), Count(kd_ready)
            for c in range(7):
                chunk_ready("a_in", c)
                if c == 0:
                    features(0, 4, ACT.Silu)
                elif c == 1:
                    features(4, 2, ACT.Silu, last=False)
                    features(6, 2, ACT.Copy, skip=2)
                elif c == 2:
                    features(8, 4, ACT.Copy)
                elif c == 3:
                    rows(0, 512)
                elif c == 4:
                    rows(512, 256)
                elif c == 5:
                    features(12, 4, ACT.Silu)
                else:
                    features(16, 2, ACT.Silu, last=False)
                    features(18, 2, ACT.Copy, skip=2, scale=64 ** -0.5)
                lin[0] += 1
                if c == 3:
                    act.wait_ge(qk_in, dkr.up())
                    act.activation(kd, kd, ACT.Exp).then_inc(act_step, 1)
                    act.wait_ge(act_step, step.up())
                    act.activation(kd, kd, ACT.Ln, bias=1.0).then_inc(exp_ready, 1)
                    act.wait_ge(exp_ready, exr.up())
                if c == 4:
                    act.wait_ge(qk_in, dkr.up())
                    act.activation(FT[:, 6:12, :], sfx, ACT.Exp, scale=-1.0).then_inc(exp_ready, 1)
                    act.wait_ge(exp_ready, exr.up())
            ahead(PLAN["wo1"])
            heads(MEM[0])

            rwr = Count(rw_high)

            def router_high(rows_need):
                act.wait_ge(row_loaded, rows_need)
                act.activation(rwh[:, :, :], rw, ACT.Copy).then_inc(rw_high, 1)
                rwr.up()

            act.wait_ge(qk_in, dkr.up())
            dqr.n = 1
            for l in range(1, 9):
                m = 2 ** (l - 1)
                if l > 1:
                    act.wait_ge(sums_ready, upd.up())
                    act.wait_ge(dk_ready, dqr.up())
                    act.wait_ge(kd_ready, kdr.up())
                act.activation(level_exps(m, 0), halves(pfx, m)[:, :, 1, :], ACT.Exp).then_inc(act_step, 1)
                act.wait_ge(act_step, step.up())
                act.activation(level_exps(m, 1), halves(sfx, m)[:, :, 0, :], ACT.Exp).then_inc(exp_ready, 1)
                act.wait_ge(exp_ready, exr.up())
            act.wait_ge(o_ready, orr.up())
            o3 = ps[:, 4:7, :].rearrange("p a (b t) -> p (a b) t", t=S)
            act.activation(pfx, o3, ACT.Copy).then_inc(act_step, 1)
            act.wait_ge(act_step, step.up())
            act.activation(qd, o3, ACT.Square).then_inc(exp_ready, 1)
            act.wait_ge(exp_ready, exr.up())
            act.wait_ge(sq_sum, sqs.up())
            act.activation(kd, o3, ACT.Ln, bias=eps_col[EPS], scale=1.0 / P).then_inc(act_step, 1)
            act.wait_ge(act_step, step.up())
            act.activation(kd, kd, ACT.Exp, scale=-0.5).then_inc(rs_ready, 1)
            act.wait_ge(rs_ready, rsr.up())
            act.wait_ge(v_ready, v.up())
            act.activation(hh[:, 0:6, :], sfx, ACT.Copy).then_inc(hh_ready, 1)
            hhr.up()
            wo("wo1")
            router_high(208)
            ln_stats()
            act.wait_ge(x_ready, xrd.up())
            transposed_mod(*ln_cols(0, 0), 0)
            def router():
                act.wait_ge(router_ready, sp_in.up())
                act.activation(rt[:, 64:104], rt[:, 64:104], ACT.Exp).then_inc(exp_ready, 1)
                act.wait_ge(exp_ready, exr.up())

            sp_in = Count(router_ready)
            router()
            ffn("moe0", NEXP)
            ahead(PLAN["kv"])
            ln_stats()
            act.wait_ge(x_ready, xrd.up())
            transposed_mod(*ln_cols(1, 0), 0)

            for c in range(4):
                chunk_ready("kv", c)
                if c == 0:
                    features(6, 4, ACT.Copy)
                elif c == 1:
                    features(10, 2, ACT.Copy)
                elif c == 2:
                    rows(0, 512)
                else:
                    rows(512, 256)
                lin[0] += 1
            for c in range(2):
                chunk_ready("b_in", c)
                if c == 0:
                    features(0, 4, ACT.Copy, scale=64 ** -0.5)
                else:
                    features(4, 2, ACT.Copy, last=False, scale=64 ** -0.5)
                    features(18, 2, ACT.Copy, skip=2, scale=64 ** -0.5)
                lin[0] += 1
            ahead(PLAN["wo2"])
            heads(MEM[1])
            zr, lr, lar, ar = Count(s_ready), Count(l_ready), Count(la_ready), Count(a_ready)
            zr.n = len(MOBA) + len(MEM[0]) + len(MEM[1])
            for i in range(SBH // 2 + 2):
                if i < SBH // 2:
                    act.wait_ge(s_ready, zr.up())
                    nb, z = sb_buf(i), ps[:, 2 * (i % 2):2 * (i % 2) + 2, 0:384]
                    act.activation(nb, z, ACT.Abs).then_inc(act_step, 1)
                    act.wait_ge(act_step, step.up())
                    act.activation(nb, nb, ACT.Exp, scale=-1.0).then_inc(act_step, 1)
                    act.wait_ge(act_step, step.up())
                if 0 <= i - 1 < SBH // 2:
                    act.wait_ge(la_ready, lar.up())
                    act.activation(sb_buf(i - 1), sb_buf(i - 1), ACT.Exp).then_inc(a_ready, 1)
                    act.wait_ge(a_ready, ar.up())
                if i < SBH // 2:
                    act.activation(nb, nb, ACT.Ln, bias=1.0).then_inc(l_ready, 1)
                    act.wait_ge(l_ready, lr.up())
                if i >= 2:
                    head_out(ps[:, 4 + i % 2, 0:S], hh[:, i - 2, :])
            wo("wo2")
            router_high(336)
            ln_stats()
            act.wait_ge(x_ready, xrd.up())
            transposed_mod(*ln_cols(0, 1), 0)
            router()
            ffn("moe1", NEXP)
            ln_stats()

        @block.vector
        def _(dve):
            step = Count(dve_step)
            hsp, lsp = Count(h_split), Count(l_split)
            n = [0]
            LIMIT = PLAN["end"]
            widths = narrow_units()

            def split(j=0):
                u = n[0] + j
                if u >= LIMIT:
                    return
                w = widths.get(u, NC)
                dve.wait_ge(h_split, hsp.up())
                dve.tensor_tensor(wl[u % SPL][:, :, 0:w], raw[u % RAW][:, :, 0:w],
                                             wh[u % SPL][:, :, 0:w].bitcast(F32), ALU.subtract).then_inc(l_split, 1)
                lsp.up()

            def ahead(upto):
                while n[0] < upto + SPL:
                    split()
                    n[0] += 1

            rtr, xrd, x0r = Count(root_ready), Count(x_ready), Count(x0_ready)
            xn, xt, v, hhr, hr = Count(xn_ready), Count(xt_ready), Count(v_ready), Count(hh_ready), Count(h_ready)
            accd, usedd = Count(ada_acc), Count(ada_used)
            rows_in = [0]

            dve.memset(st[:, 60:61], EPS).then_inc(dve_step, 1)
            dve.wait_ge(dve_step, step.up())
            dve.memset(st[:, 61:62], LN_EPS).then_inc(dve_step, 1)
            dve.wait_ge(dve_step, step.up())
            dve.wait_ge(small_loaded, 96)
            dve.tensor_copy(mlev[:, :, :], Z[:, 0:8 * P].rearrange("p (l n) -> p l n", n=P)).then_inc(dve_step, 1)
            dve.wait_ge(dve_step, step.up())
            dve.tensor_scalar(st[:, 62:63], cols[:, C_QG:C_QG + 1], P ** -0.5, None, ALU.mult).then_inc(dve_step, 1)
            dve.wait_ge(dve_step, step.up())
            dve.wait_ge(sc_ready, 1)
            dve.tensor_scalar(scol[:, :], scol[:, :], 1.0, None, ALU.add).then_inc(dve_step, 1)
            dve.wait_ge(dve_step, step.up())
            dve.reciprocal(scol[:, :], scol[:, :]).then_inc(dve_step, 1)
            dve.wait_ge(dve_step, step.up())
            dve.tensor_tensor(scol[:, :], scol[:, :], cols[:, C_C:C_C + 8], ALU.mult).then_inc(dve_step, 1)
            dve.wait_ge(dve_step, step.up())

            def ada(layer, c, acc, it=None, parts=(0, 1)):
                g = 12 * layer + c
                for q in parts:
                    dve.wait_ge(ada_loaded[q], 16 * (g + 1) if it is None else it * 32 + 16 * (g + 1))
                    for k in range(UK):
                        w, s = cring[:, q, k, :], scol[:, UK * q + k:UK * q + k + 1]
                        if q == k == 0:
                            i = dve.tensor_scalar(acc, w, s, None, ALU.mult)
                        else:
                            i = dve.scalar_tensor_tensor(acc, w, s, acc, ALU.mult, ALU.add)
                        i.then_inc(ada_used if k == UK - 1 else ada_acc, 1)
                        dve.wait_ge(ada_used if k == UK - 1 else ada_acc, (usedd if k == UK - 1 else accd).up())

            ft_acc = FT[:, :, :].rearrange("p (c a) t -> p c (a t)", a=2)

            def acc_of(layer, c):
                if layer == 0:
                    return ft_acc[:, c, :] if c < 4 else layer0_acc(c)
                return ft_acc[:, c, :] if c < 10 else accw[:, c - 10, :]

            msum, mtk = Count(mod_sums), Count(mod_taken)

            def mod_cols(layer, which, bank):
                dve.wait_ge(mod_sums, msum.up())
                m = ps[:, bank, 0:16]
                b = cols[:, C_BADA + 48 * layer + 24 * which:C_BADA + 48 * layer + 24 * which + 16]
                gain = cols[:, (C_NFFN if which else C_NMIX) + 8 * layer:(C_NFFN if which else C_NMIX) + 8 * layer + 8]
                o = slice(8 * which, 8 * which + 8)
                dve.tensor_tensor(modB[:, o], m[:, 0:8], b[:, 0:8], ALU.add).then_inc(dve_step, 1)
                dve.wait_ge(dve_step, step.up())
                dve.tensor_tensor(modA[:, o], m[:, 8:16], b[:, 8:16], ALU.add).then_inc(dve_step, 1)
                dve.wait_ge(dve_step, step.up())
                dve.scalar_tensor_tensor(modA[:, o], modA[:, o], 1.0, gain, ALU.add, ALU.mult).then_inc(mod_taken, 1)
                dve.wait_ge(mod_taken, mtk.up())

            def mod_gate(g, bank):
                dve.wait_ge(mod_sums, msum.up())
                dve.tensor_tensor(gb[:, g, :], ps[:, bank:bank + 2, :].rearrange("p a b -> p (a b)"), gb[:, g, :], ALU.add).then_inc(mod_taken, 1)
                dve.wait_ge(mod_taken, mtk.up())

            def rms_apply():
                dve.wait_ge(root_ready, rtr.up())
                dve.reciprocal(st[:, 4:6], st[:, 2:4]).then_inc(dve_step, 1)
                dve.wait_ge(dve_step, step.up())
                dve.tensor_scalar(tv[:, 0, :], xs[:, 0, :], st[:, 4:5], None, ALU.mult).then_inc(dve_step, 1)
                dve.wait_ge(dve_step, step.up())
                dve.tensor_scalar(tv[:, 1, :], xs[:, 1, :], st[:, 5:6], None, ALU.mult).then_inc(xn_ready, 1)
                dve.wait_ge(xn_ready, xn.up())

            def bank_k(g):
                return ps[:, 4 + g, :].rearrange("p (k t) -> p k t", k=2)

            def low(g):
                dve.wait_ge(hh_ready, hhr.up())
                dve.tensor_tensor(hl[:, 2 * g:2 * g + 2, :], bank_k(g),
                                            hh[:, 2 * g:2 * g + 2, :].bitcast(F32), ALU.subtract).then_inc(h_ready, 1)
                hr.up()

            def transposed_mod(scale, shift):
                for g in range(0, 4, 2):
                    dve.wait_ge(xt_ready, xt.up())
                    for q in range(2):
                        k = 2 * g + q
                        b = ps[:, 4 + g, q * S:(q + 1) * S]
                        dve.tensor_scalar(
                            b, b, scale[:, k:k + 1], shift[:, k:k + 1], ALU.mult, ALU.add).then_inc(v_ready if q else dve_step, 1)
                        dve.wait_ge(v_ready if q else dve_step, (v if q else step).up())
                    xt.n += 1
                for g in range(4):
                    low(g)

            def transposed_plain():
                for g in range(4):
                    low(g)
                xt.n += 4

            for c in range(4):
                ada(0, c, acc_of(0, c))
            ahead(0)
            mod_cols(0, 0, 7)
            rms_apply()
            transposed_mod(*mod(0))

            rsr, nrm = Count(rs_ready), Count(normed)

            def qk_norm(c):
                dve.wait_ge(rs_ready, rsr.up())
                f = FT[:, 4 * c:4 * c + 4, :].rearrange("p k t -> p (k t)")
                gain = st[:, 62:63] if c < 2 else cols[:, C_KG:C_KG + 1]
                dve.scalar_tensor_tensor(f, f, gain, Z[:, 1024:2048], ALU.mult, ALU.mult).then_inc(normed, 1)
                dve.wait_ge(normed, nrm.up())

            for c in range(6):
                ahead(PLAN["qkv"] + 2 * c + 1)
                if 1 <= c <= 4:
                    qk_norm(c - 1)
                if c == 4:
                    dve.wait_ge(row_loaded, 32)
                    mod_gate(0, 6)
                if c < 5:
                    ada(0, 4 + c, acc_of(0, 4 + c))
            ahead(PLAN["wo0"])

            r0r = Count(row0_ready)
            sr, nmx = Count(s_ready), Count(nmax_ready)
            er, pr, ohr, olr = Count(e_ready), Count(p_ready), Count(oh_ready), Count(ol_ready)

            def head_low(src, h, dst):
                dve.wait_ge(oh_ready, ohr.up())
                dve.tensor_tensor(dst, src, h.bitcast(F32), ALU.subtract).then_inc(ol_ready, 1)
                dve.wait_ge(ol_ready, olr.up())

            def heads(waves, between=None):
                def maxima(w):
                    dve.wait_ge(s_ready, sr.up())
                    b, m = w % 2, waves[w]
                    s = ps[:, 2 * b:2 * b + 2, :]
                    for t, (c0, c1) in enumerate(m["spans"]):
                        dve.tensor_reduce(
                            st[:, 8 + 4 * b + t:12 + 4 * b:2], s[:, :, c0:c1], AX.X, ALU.max, negate=True).then_inc(nmax_ready if t else dve_step, 1)
                        dve.wait_ge(nmax_ready if t else dve_step, (nmx if t else step).up())

                def probs(w):
                    dve.wait_ge(e_ready, er.up())
                    b, m = w % 2, waves[w]
                    dve.reciprocal(st[:, 24 + 4 * b:28 + 4 * b], st[:, 16 + 4 * b:20 + 4 * b]).then_inc(dve_step, 1)
                    dve.wait_ge(dve_step, step.up())
                    for t, (c0, c1) in enumerate(m["spans"]):
                        z = prob(w)[:, :, c0:c1]
                        r = st[:, 24 + 4 * b + t:28 + 4 * b:2].unsqueeze(2).to_broadcast([P, 2, c1 - c0])
                        dve.tensor_tensor(z, z, r, ALU.mult).then_inc(p_ready if t else dve_step, 1)
                        dve.wait_ge(p_ready if t else dve_step, (pr if t else step).up())

                for i in range(len(waves) + 2):
                    if i < len(waves):
                        maxima(i)
                    if 0 <= i - 1 < len(waves):
                        probs(i - 1)
                    if i >= 2:
                        m = waves[i - 2]
                        b = slice(m["blk"], m["blk"] + m["nb"])
                        head_low(out_of(i - 2, m), hh[:, b, :], hl[:, b, :])
                    if between:
                        between(i)

            heads(MOBA, lambda i: ada(0, 9 + i // 2, acc_of(0, 9 + i // 2), parts=(i % 2,)))

            def wo(ph):
                ahead(PLAN[ph] + 2)

            def add_gated(g, after):
                dve.wait_ge(row0_ready, r0r.up())
                for t in range(TT):
                    if t:
                        dve.wait_ge(unit_used, PLAN[after])
                    y = ps[:, 4 + 2 * t:6 + 2 * t, :]
                    dve.tensor_tensor(tv[:, t, :].rearrange("p (a n) -> p a n", a=2), y,
                                         gb[:, g, :].rearrange("p (a n) -> p a n", a=2), ALU.mult).then_inc(dve_step, 1)
                    dve.wait_ge(dve_step, step.up())
                    dve.tensor_tensor(xs[:, t, :], xs[:, t, :], tv[:, t, :], ALU.add).then_inc(x_ready if t else x0_ready, 1)
                    dve.wait_ge(x_ready if t else x0_ready, (xrd if t else x0r).up())
                ahead(PLAN[after] - 1)

            ahead(PLAN["wo0"] + 1)
            ahead(PLAN["wo0"] + 2)
            add_gated(0, "ffn0")
            mod_cols(0, 1, 3)
            mod_gate(1, 0)
            rms_apply()
            transposed_mod(*mod(1))

            silr, acr, ahr, asp = Count(sil_ready), Count(act_ready), Count(ah_ready), Count(a_split)

            def ffn(ph, chunks, weight, extra=None):
                def product(c, r=0):
                    dve.wait_ge(sil_ready, silr.up())
                    for t in range(TT):
                        sil = Z[:, t * FW:(t + 1) * FW]
                        up = ps[:, t, FW:2 * FW]
                        dve.scalar_tensor_tensor(
                            Z[:, 512 + t * FW:512 + (t + 1) * FW], sil, weight(t, c), up, ALU.mult, ALU.mult).then_inc(act_ready, 1)
                        acr.up()

                def low_part():
                    dve.wait_ge(ah_ready, ahr.up())
                    dve.tensor_tensor(al[:, :, :], ps[:, 2, :].rearrange("p (k t) -> p k t", k=2),
                                                 ah[:, :, :].bitcast(F32), ALU.subtract).then_inc(a_split, 1)
                    asp.up()

                def chunk(c, j):
                    low_part()
                    split(j)
                    split(j + 1)
                    product(c)
                    split(j + 2)

                ahead(PLAN[ph])
                split()
                product(0)
                split(1)
                n[0] += 2
                loops = (chunks - 1) // 2
                per = {hsp: 6, lsp: 6, silr: 2, acr: 4, ahr: 2, asp: 2}
                if extra:
                    per.update({accd: 12, usedd: 4})
                with looped(dve, loops, per) as it:
                    for r in range(2):
                        chunk(it * 2 + (r + 1), 3 * r)
                        if extra:
                            extra(r, it)
                n[0] += 6 * loops
                for q in range(chunks - 1 - 2 * loops):
                    chunk(2 * loops + 1 + q, 0)
                    n[0] += 3
                low_part()

            def ada_in_loop(r, it):
                ada(1, r, ft_acc[:, bass.ds(it * 2 + r, 1), :].rearrange("p a n -> p (a n)"), it)

            ffn("ffn0", NFF, lambda t, c: 1.0, ada_in_loop)
            add_gated(1, "win")
            mod_cols(1, 0, 3)
            rms_apply()
            transposed_mod(*mod(0))

            evac, ptk = Count(lin_evac), Count(lin_taken)
            evac.n = 6
            cu = FT[:, 0:8, :]
            cy = FT[:, 8:16, :]
            for c in range(6):
                ahead(PLAN["win"] + 2 * c + 1)
                if c < 2:
                    ada(1, 10 + c, acc_of(1, 10 + c))
                if c == 1:
                    dve.wait_ge(row_loaded, 64)
                    mod_gate(0, 4)
                    mod_cols(1, 1, 7)
                dve.wait_ge(lin_evac, evac.up())
                if c == 4:
                    mod_gate(1, 6)
                if c in (2, 3):
                    f = cu[:, 4 * (c - 2):4 * (c - 1), :].rearrange("p k t -> p (k t)")
                    dve.tensor_tensor(f, f, Z[:, 1024 * (c % 2):1024 * (c % 2) + 1024], ALU.mult).then_inc(lin_taken, 1)
                    dve.wait_ge(lin_taken, ptk.up())
                    for k in range(4 * (c - 2), 4 * (c - 1)):
                        w = lambda j: cols[:, C_CONV + 8 * j + k:C_CONV + 8 * j + k + 1]
                        dve.tensor_scalar(cy[:, k, :], cu[:, k, :], w(2), None, ALU.mult).then_inc(dve_step, 1)
                        dve.wait_ge(dve_step, step.up())
                        dve.scalar_tensor_tensor(cy[:, k, 1:S], cu[:, k, 0:S - 1], w(1), cy[:, k, 1:S], ALU.mult, ALU.add).then_inc(dve_step, 1)
                        dve.wait_ge(dve_step, step.up())
                        dve.scalar_tensor_tensor(cy[:, k, 2:S], cu[:, k, 0:S - 2], w(0), cy[:, k, 2:S], ALU.mult, ALU.add).then_inc(dve_step, 1)
                        dve.wait_ge(dve_step, step.up())
                if c >= 4:
                    z = Z[:, 1024 * (c % 2):1024 * (c % 2) + 1024]
                    dve.tensor_tensor(z, z, cy[:, 4 * (c - 4):4 * (c - 3), :].rearrange("p k t -> p (k t)"), ALU.mult).then_inc(lin_taken, 1)
                    dve.wait_ge(lin_taken, ptk.up())
            ahead(PLAN["wout"])
            for g in range(2):
                dve.wait_ge(hh_ready, hhr.up())
                dve.tensor_tensor(hl[:, 4 * g:4 * g + 4, :], Z[:, 1024 * g:1024 * g + 1024].rearrange("p (k t) -> p k t", k=4),
                                            hh[:, 4 * g:4 * g + 4, :].bitcast(F32), ALU.subtract).then_inc(h_ready, 1)
                hr.up()
            wo("wout")
            add_gated(0, "ffn1")
            rms_apply()
            transposed_mod(*mod(1))
            ffn("ffn1", NFF, lambda t, c: 1.0)
            add_gated(1, "mem")

            transposed_plain()
            for l in range(DEPTH):
                ahead(PLAN["mem"] + 2 * l + 1)
            ahead(PLAN["a_in"])
            transposed_plain()
            exr, dkr, dqr = Count(exp_ready), Count(qk_in), Count(dk_ready)
            upd = Count(sums_ready)
            levs, levt = Count(lev_scores), Count(lev_taken)
            q, f, kk, g = FT[:, 0:6, :], FT[:, 6:12, :], FT[:, 6:12, :], FT[:, 12:18, :]
            for c in range(7):
                ahead(PLAN["a_in"] + 2 * c + 1)
                if c == 3:
                    dve.wait_ge(lin_evac, 17)
                    dve.scalar_tensor_tensor(kd, f, -1.0, f, ALU.mult, ALU.min).then_inc(qk_in, 1)
                    dve.wait_ge(qk_in, dkr.up())
                    dve.tensor_scalar(q, q, P ** -0.5, None, ALU.mult).then_inc(dve_step, 1)
                    dve.wait_ge(dve_step, step.up())
                    dve.tensor_copy(qd, q).then_inc(dve_step, 1)
                    dve.wait_ge(dve_step, step.up())
                if c == 4:
                    dve.wait_ge(exp_ready, exr.up())
                    dve.scalar_tensor_tensor(pfx, f, 0.0, kd, ALU.min, ALU.subtract).then_inc(dve_step, 1)
                    dve.wait_ge(dve_step, step.up())
                    dve.scalar_tensor_tensor(sfx, f, 0.0, kd, ALU.max, ALU.add).then_inc(qk_in, 1)
                    dve.wait_ge(qk_in, dkr.up())
                if c == 5:
                    dve.wait_ge(exp_ready, exr.up())
                    dve.tensor_copy(kd, kk).then_inc(dk_ready, 1)
                    dve.wait_ge(dk_ready, dqr.up())
                    dve.memset(sfx, 0.0).then_inc(qk_in, 1)
                    dve.wait_ge(qk_in, dkr.up())
            ahead(PLAN["wo1"])
            heads(MEM[0])

            dve.memset(scD, 0.0).then_inc(dve_step, 1)
            dve.wait_ge(dve_step, step.up())

            def take(l):
                o = 4 * (l % 2)
                if l < 8:
                    dve.copy_predicated(
                        scD.rearrange("p h (c t) -> p (h c) t", c=2), mlev[:, l:l + 1, :].to_broadcast([P, 2 * HG, P]),
                        ps[:, o:o + 3, :].rearrange("p a (b t) -> p (a b) t", t=P)).then_inc(lev_taken, 1)
                    dve.wait_ge(lev_taken, levt.up())
                else:
                    dve.tensor_copy(scX[:, 0:4, :], ps[:, o, :].rearrange("p (h t) -> p h t", t=P)).then_inc(dve_step, 1)
                    dve.wait_ge(dve_step, step.up())
                    dve.tensor_copy(scX[:, 4:6, :], ps[:, o + 1, 0:S].rearrange("p (h t) -> p h t", t=P)).then_inc(lev_taken, 1)
                    dve.wait_ge(lev_taken, levt.up())

            for l in range(1, 9):
                m = 2 ** (l - 1)
                dve.wait_ge(exp_ready, exr.up())
                dve.wait_ge(lev_scores, levs.up())
                dve.tensor_tensor(halves(qd, m)[:, :, 1, :], level_exps(m, 0), halves(q, m)[:, :, 1, :], ALU.mult).then_inc(dk_ready, 1)
                dve.wait_ge(dk_ready, dqr.up())
                if l < 8:
                    pv, sv, nb = halves(pfx, m), halves(sfx, m), HG * S // (2 * m)
                    dve.tensor_tensor(sv[:, :, 0, :], sv[:, :, 0, :],
                                         pv[:, :, 1, m - 1:m].to_broadcast([P, nb, m]), ALU.add).then_inc(dve_step, 1)
                    dve.wait_ge(dve_step, step.up())
                    dve.tensor_tensor(pv[:, :, 1, :], pv[:, :, 1, :],
                                                    pv[:, :, 0, m - 1:m].to_broadcast([P, nb, m]), ALU.add).then_inc(sums_ready, 1)
                    dve.wait_ge(sums_ready, upd.up())
                take(l - 1)
            dve.wait_ge(lev_scores, levs.up())
            take(8)
            dve.wait_ge(exp_ready, exr.up())
            for h in range(HG):
                dve.scalar_tensor_tensor(pfx[:, h, :], pfx[:, h, :], cols[:, C_GN + h:C_GN + h + 1], g[:, h, :],
                                            ALU.mult, ALU.mult).then_inc(dve_step, 1)
                dve.wait_ge(dve_step, step.up())
            dve.wait_ge(rs_ready, rsr.up())
            dve.tensor_tensor(sfx, pfx, kd, ALU.mult).then_inc(v_ready, 1)
            dve.wait_ge(v_ready, v.up())
            dve.wait_ge(hh_ready, hhr.up())
            dve.tensor_tensor(hl[:, 0:6, :], sfx, hh[:, 0:6, :].bitcast(F32), ALU.subtract).then_inc(ol_ready, 1)
            dve.wait_ge(ol_ready, olr.up())

            stat = Count(stat_ready)

            lnd = Count(ln_applied)

            def post_norm(after, last=False):
                dve.wait_ge(row0_ready, r0r.up())
                if after != "moe0":
                    dve.wait_ge(ln_applied, lnd.up())
                for t in range(TT):
                    if t:
                        dve.wait_ge(unit_used, PLAN[after])
                    x2 = xs[:, t, :].rearrange("p (a n) -> p a n", a=2)
                    dve.scalar_tensor_tensor(x2, x2, ALPHA, ps[:, 4 + 2 * t:6 + 2 * t, :], ALU.mult, ALU.add).then_inc(dve_step, 1)
                    dve.wait_ge(dve_step, step.up())
                    for a in range(2):
                        dve.bn_stats(st[:, 32 + 12 * t + 6 * a:38 + 12 * t + 6 * a], xs[:, t, a * 512:(a + 1) * 512]).then_inc(dve_step, 1)
                        dve.wait_ge(dve_step, step.up())
                    dve.bn_aggr(st[:, 56 + 2 * t:58 + 2 * t], st[:, 32 + 12 * t:44 + 12 * t]).then_inc(stat_ready if t else dve_step, 1)
                    dve.wait_ge(stat_ready if t else dve_step, (stat if t else step).up())
                dve.wait_ge(root_ready, rtr.up())
                dve.reciprocal(st[:, 4:6], st[:, 2:4]).then_inc(dve_step, 1)
                dve.wait_ge(dve_step, step.up())
                if last:
                    dve.wait_ge(row_loaded, 368)
                for t in range(TT):
                    x = xs[:, t, :]
                    dve.tensor_scalar(
                        x, x, st[:, 56 + 2 * t:57 + 2 * t], st[:, 4 + t:5 + t], ALU.subtract, ALU.mult).then_inc(dve_step if last or not t else x_ready, 1)
                    dve.wait_ge(dve_step if last or not t else x_ready, (step if last or not t else xrd).up())
                    if last:
                        dve.tensor_tensor(x, x, lnv[:, 0, :], ALU.mult).then_inc(dve_step, 1)
                        dve.wait_ge(dve_step, step.up())
                        dve.tensor_tensor(x, x, lnv[:, 1, :], ALU.add).then_inc(x_ready if t else dve_step, 1)
                        dve.wait_ge(x_ready if t else dve_step, (xrd if t else step).up())
                if not last:
                    ahead(PLAN[after] - 1)

            rin, rsum = Count(router_ready), Count(router_sums)
            rwr, rwlr = Count(rw_high), Count(rw_low)

            def router_low():
                dve.wait_ge(rw_high, rwr.up())
                dve.tensor_tensor(rwl[:, :, :], rw, rwh[:, :, :].bitcast(F32), ALU.subtract).then_inc(rw_low, 1)
                rwlr.up()


            def router():
                dve.wait_ge(router_sums, rsum.up())
                N = 2 * 5
                lg = rt[:, 0:40]
                g3 = lambda a: a.rearrange("p (g e) -> p g e", e=4)
                for t in range(TT):
                    dve.tensor_tensor(lg[:, 20 * t:20 * t + 20], ps[:, 7, 20 * t:20 * t + 20], rbias, ALU.add).then_inc(dve_step, 1)
                    dve.wait_ge(dve_step, step.up())
                mx, ex = rt[:, 48:58], rt[:, 64:104]
                dve.tensor_reduce(mx, g3(lg), AX.X, ALU.max).then_inc(dve_step, 1)
                dve.wait_ge(dve_step, step.up())
                dve.tensor_tensor(g3(ex), g3(lg), mx.unsqueeze(2).to_broadcast([P, N, 4]), ALU.subtract).then_inc(router_ready, 1)
                dve.wait_ge(router_ready, rin.up())
                rank, cmp_ = rt[:, 112:152], rt[:, 160:200]
                dve.memset(rank, 0.0).then_inc(dve_step, 1)
                dve.wait_ge(dve_step, step.up())
                for j in range(4):
                    other = g3(lg)[:, :, j:j + 1].to_broadcast([P, N, 4])
                    dve.tensor_tensor(g3(cmp_), other, g3(lg), ALU.is_gt).then_inc(dve_step, 1)
                    dve.wait_ge(dve_step, step.up())
                    dve.tensor_tensor(rank, rank, cmp_, ALU.add).then_inc(dve_step, 1)
                    dve.wait_ge(dve_step, step.up())
                    if j < 3:
                        dve.tensor_tensor(g3(cmp_)[:, :, j + 1:4], other[:, :, 0:3 - j], g3(lg)[:, :, j + 1:4], ALU.is_equal).then_inc(dve_step, 1)
                        dve.wait_ge(dve_step, step.up())
                        dve.tensor_tensor(g3(rank)[:, :, j + 1:4], g3(rank)[:, :, j + 1:4], g3(cmp_)[:, :, j + 1:4], ALU.add).then_inc(dve_step, 1)
                        dve.wait_ge(dve_step, step.up())
                best, sums = rt[:, 208:248], rt[:, 256:266]
                dve.wait_ge(exp_ready, exr.up())
                dve.tensor_reduce(sums, g3(ex), AX.X, ALU.add).then_inc(dve_step, 1)
                dve.wait_ge(dve_step, step.up())
                dve.tensor_scalar(best, rank, 2.0, None, ALU.is_lt).then_inc(dve_step, 1)
                dve.wait_ge(dve_step, step.up())
                dve.tensor_tensor(best, best, ex, ALU.mult).then_inc(dve_step, 1)
                dve.wait_ge(dve_step, step.up())
                dve.tensor_reduce(mx, g3(best), AX.X, ALU.add).then_inc(dve_step, 1)
                dve.wait_ge(dve_step, step.up())
                dve.reciprocal(mx, mx).then_inc(dve_step, 1)
                dve.wait_ge(dve_step, step.up())
                dve.reciprocal(sums, sums).then_inc(dve_step, 1)
                dve.wait_ge(dve_step, step.up())
                dve.tensor_scalar(rank, rank, 1.0, None, ALU.is_lt).then_inc(dve_step, 1)
                dve.wait_ge(dve_step, step.up())
                for t in range(TT):
                    w = rt[:, 272 + 4 * t:276 + 4 * t]
                    dve.tensor_scalar(w, rank[:, 20 * t:20 * t + 4], sums[:, 5 * t:5 * t + 1], None, ALU.mult).then_inc(dve_step, 1)
                    dve.wait_ge(dve_step, step.up())
                    dve.tensor_tensor(w, w, mx[:, 5 * t + 1:5 * t + 5], ALU.mult).then_inc(dve_step, 1)
                    dve.wait_ge(dve_step, step.up())
                    dve.tensor_tensor(g3(gate[:, t, :]), g3(best[:, 20 * t + 4:20 * t + 20]),
                                         w.unsqueeze(2).to_broadcast([P, 4, 4]), ALU.mult).then_inc(dve_step, 1)
                    dve.wait_ge(dve_step, step.up())

            def expert_gate(t, e):
                if isinstance(e, int):
                    return gate[:, t, e:e + 1]
                return gate[:, t, bass.ds(e, 1)]

            wo("wo1")
            router_low()
            post_norm("moe0")
            transposed_mod(*ln_cols(0, 0))
            router()
            ffn("moe0", NEXP, expert_gate)
            post_norm("kv")
            transposed_mod(*ln_cols(1, 0))
            for c in range(4):
                ahead(PLAN["kv"] + 2 * c + 1)
            for c in range(2):
                ahead(PLAN["b_in"] + 2 * c + 1)
            ahead(PLAN["wo2"])
            heads(MEM[1])
            lr, spr = Count(l_ready), Count(sp_ready)
            rr, lar = Count(rest_ready), Count(la_ready)
            both = lambda x: x.unsqueeze(1).to_broadcast([P, 2, 384])
            for i in range(SBH // 2 + 2):
                if 0 <= i - 1 < SBH // 2:
                    dve.wait_ge(rest_ready, rr.up())
                    dve.scalar_tensor_tensor(sb_buf(i - 1), ps[:, 2 * ((i - 1) % 2):2 * ((i - 1) % 2) + 2, 0:384],
                                                           0.0, both(nstrict), ALU.min, ALU.add).then_inc(la_ready, 1)
                    dve.wait_ge(la_ready, lar.up())
                if i < SBH // 2:
                    dve.wait_ge(l_ready, lr.up())
                    nb, z = sb_buf(i), ps[:, 2 * (i % 2):2 * (i % 2) + 2, 0:384]
                    dve.scalar_tensor_tensor(nb, z, 0.0, nb, ALU.max, ALU.add).then_inc(dve_step, 1)
                    dve.wait_ge(dve_step, step.up())
                    dve.tensor_tensor(nb, nb, both(mstrict), ALU.mult).then_inc(sp_ready, 1)
                    dve.wait_ge(sp_ready, spr.up())
                if i >= 2:
                    head_low(ps[:, 4 + i % 2, 0:S], hh[:, i - 2, :], hl[:, i - 2, :])
            wo("wo2")
            router_low()
            post_norm("moe1")
            transposed_mod(*ln_cols(0, 1))
            router()
            ffn("moe1", NEXP, expert_gate)
            post_norm("end", last=True)

        @block.tensor
        def _(pe):
            lsp, used = Count(l_split), Count(unit_used)
            n = [0]

            def mm3(o, h1, l1, h2, l2, start, stop):
                pe.matmul(o, h1, h2, start=start, stop=False, skip_group_check=True)
                pe.matmul(o, h1, l2, start=False, stop=False, skip_group_check=True)
                return pe.matmul(o, l1, h2, start=False, stop=stop, skip_group_check=True)

            def unit_rows(u, bank, k0, w, first, last, rows0=False):
                pe.wait_ge(l_split, lsp.up())
                for t in range(TT):
                    for k in range(UK):
                        tok = slice(t * P, (t + 1) * P)
                        i = mm3(bank(t)[:, 0:w], hh[:, k0 + k, tok], hl[:, k0 + k, tok],
                                wh[u % SPL][:, k, 0:w], wl[u % SPL][:, k, 0:w],
                                first and k == 0, last and k == UK - 1)
                    if rows0 and t == 0:
                        i.then_inc(row0_ready, 1)
                        r0r.up()
                i.then_inc(unit_used, 1)
                used.up()

            def unit_features(u, b0, nb, k0, first, last, signal=True, c0=0):
                for b in range(nb):
                    o = ps[:, b0 + b // 2, (b % 2) * S:(b % 2 + 1) * S]
                    for k in range(UK):
                        cs = slice(c0 + b * P, c0 + (b + 1) * P)
                        i = mm3(o, wh[u % SPL][:, k, cs], wl[u % SPL][:, k, cs], hh[:, k0 + k, :], hl[:, k0 + k, :],
                                first and k == 0 and b % 2 == 0, last and k == UK - 1)
                return i

            evac, r0r = Count(lin_evac), Count(row0_ready)
            lin = [0]

            def chunk(kind, w=NC):
                if lin[0] >= 2:
                    pe.wait_ge(lin_evac, evac.up())
                pair = 2 * (lin[0] % 2)
                for q in range(2):
                    if kind == "rows":
                        unit_rows(n[0], lambda t: ps[:, pair + t, :], UK * q, w, q == 0, q == 1)
                    else:
                        pe.wait_ge(l_split, lsp.up())
                        unit_features(n[0], pair, w // P, UK * q, q == 0, q == 1).then_inc(unit_used, 1)
                        used.up()
                    n[0] += 1
                lin[0] += 1

            hr, xrd = Count(h_ready), Count(x_ready)
            olr = Count(ol_ready)

            def out_rows():
                for c in range(2):
                    for q in range(2):
                        unit_rows(n[0], lambda t: ps[:, 4 + 2 * t + c, :], UK * q, NC, q == 0, q == 1, c == q == 1)
                        n[0] += 1

            xn, xt = Count(xn_ready), Count(xt_ready)

            def transposes(src):
                for g in range(4):
                    for k in range(2):
                        for t in range(TT):
                            c = (2 * g + k) * P
                            i = pe.transpose(ps[:, 4 + g, k * S + t * P:k * S + (t + 1) * P], src[:, t, c:c + P], ident[:, :])
                    i.then_inc(xt_ready, 1)
                    xt.up()

            usedd, msum, mtk = Count(ada_used), Count(mod_sums), Count(mod_taken)
            ft_acc = FT[:, :, :].rearrange("p (c a) t -> p c (a t)", a=2)

            def acc_of(layer, c):
                if layer == 0:
                    return ft_acc[:, c, :] if c < 4 else layer0_acc(c)
                return ft_acc[:, c, :] if c < 10 else accw[:, c - 10, :]

            def mod_cols(layer, which, bank):
                for c in range(4):
                    for q in range(4):
                        i = pe.matmul(ps[:, bank, 4 * c + q:4 * c + q + 1], acc_of(layer, 6 * which + c)[:, q * P:(q + 1) * P],
                                      ones[:, 0:1], start=True, stop=True)
                i.then_inc(mod_sums, 1)
                msum.up()

            def mod_gate(layer, g, bank):
                for c in range(2):
                    i = pe.matmul(ps[:, bank + c, :], ones[:, :], acc_of(layer, 6 * g + 4 + c), start=True, stop=True)
                i.then_inc(mod_sums, 1)
                msum.up()

            pe.wait_ge(small_loaded, 96)
            pe.wait_ge(ada_used, usedd.up(8))
            mod_cols(0, 0, 7)
            pe.wait_ge(mod_taken, mtk.up())
            pe.wait_ge(xn_ready, xn.up())
            transposes(tv)
            pe.wait_ge(h_ready, hr.up(4))

            sqs, rsr = Count(sq_sum), Count(rs_ready)

            def square_sums():
                for a in range(2):
                    i = pe.matmul(ps[:, 4 + a, :], ones[:, :], Z[:, a * 512:(a + 1) * 512], start=True, stop=True)
                i.then_inc(sq_sum, 1)
                sqs.up()

            for c in range(6):
                chunk("features" if c < 4 else "rows")
                if 1 <= c <= 4:
                    pe.wait_ge(lin_evac, c)
                    if c >= 2:
                        pe.wait_ge(rs_ready, rsr.up())
                    square_sums()
                if c == 3:
                    pe.wait_ge(ada_used, usedd.up(4))
                    mod_gate(0, 0, 6)
            pe.wait_ge(lin_evac, 6)

            nrm = Count(normed)
            pe.wait_ge(rs_ready, rsr.up())
            pe.wait_ge(mod_taken, mtk.up())

            sr, er, pr = Count(s_ready), Count(e_ready), Count(p_ready)
            ptr, pte, orr = Count(pt_ready), Count(pt_evac), Count(o_ready)

            def heads(waves):
                def scores(w):
                    if w >= 2:
                        pe.wait_ge(e_ready, er.up())
                    for a, m in enumerate(waves[w]["heads"]):
                        bank = ps[:, 2 * (w % 2) + a, :]
                        for c0, c1, x, y in m["scores"]:
                            i = pe.matmul(bank[:, c0:c1], x, y, start=True, stop=not m["masked"], skip_group_check=True)
                            if m["masked"]:
                                i = pe.matmul(bank[:, c1 - P:c1], ident[:, :], mcausal[:, :], start=False, stop=True,
                                              skip_group_check=True)
                    i.then_inc(s_ready, 1)
                    sr.up()

                def turn(w):
                    pe.wait_ge(p_ready, pr.up())
                    if w:
                        pe.wait_ge(pt_evac, pte.value(1))
                    for a in range(2):
                        for x, y in waves[w]["turns"]:
                            i = pe.transpose(ps[:, 4 + a, y:y + P], prob(w)[:, a, x:x + P], ident[:, :])
                    i.then_inc(pt_ready, 1)
                    ptr.up()

                def outs(w):
                    pe.wait_ge(pt_evac, pte.up())
                    if w >= 2:
                        pe.wait_ge(ol_ready, olr.up())
                    rows = waves[w]["rows"]
                    for a, m in enumerate(waves[w]["heads"]):
                        r = slice(0, P) if rows == P else slice(64 * a, 64 * a + 64)
                        base = S * a if rows == P else 0
                        for q, (t0, t1, val, c0) in enumerate(m["outs"]):
                            i = pe.matmul(ps[r, 6 + w % 2, base + t0:base + t1], val, turned(w, waves[w])[:, a, c0:c0 + t1 - t0],
                                          start=q == 0, stop=q == 1, skip_group_check=True)
                    i.then_inc(o_ready, 1)
                    orr.up()

                for i in range(len(waves) + 2):
                    if i < len(waves):
                        scores(i)
                    if 0 <= i - 1 < len(waves):
                        turn(i - 1)
                    if i >= 2:
                        outs(i - 2)
                er.n += 2
                pe.wait_ge(ol_ready, olr.up(2))

            pe.wait_ge(normed, nrm.up(4))
            heads(MOBA)
            out_rows()
            pe.wait_ge(ada_used, usedd.up(12))
            mod_cols(0, 1, 3)
            mod_gate(0, 1, 0)
            pe.wait_ge(xn_ready, xn.up())
            transposes(tv)
            pe.wait_ge(h_ready, hr.up(4))
            pe.wait_ge(mod_taken, mtk.up(2))

            acr, atr, asp = Count(act_ready), Count(at_ready), Count(a_split)

            def ffn(ph, chunks):
                def gate_up(j):
                    for q in range(2):
                        pe.wait_ge(l_split, lsp.up())
                        u = n[0] + j + q
                        for t in range(TT):
                            for k in range(UK):
                                tok = slice(t * P, (t + 1) * P)
                                i = mm3(ps[:, t, :], hh[:, UK * q + k, tok], hl[:, UK * q + k, tok],
                                        wh[u % SPL][:, k, :], wl[u % SPL][:, k, :], q == 0 and k == 0, q == 1 and k == UK - 1)
                        i.then_inc(unit_used, 1)
                        used.up()

                def turn():
                    pe.wait_ge(act_ready, acr.up(2))
                    for k in range(2):
                        for t in range(TT):
                            i = pe.transpose(ps[:, 2, k * S + t * P:k * S + (t + 1) * P],
                                             Z[:, 512 + t * FW + k * P:512 + t * FW + (k + 1) * P], ident[:, :])
                    i.then_inc(at_ready, 1)
                    atr.up()

                def down(j, first, last):
                    pe.wait_ge(a_split, asp.up())
                    pe.wait_ge(l_split, lsp.up())
                    u = n[0] + j
                    for t in range(TT):
                        for k in range(2):
                            tok = slice(t * P, (t + 1) * P)
                            for h in range(2):
                                i = mm3(ps[:, 4 + 2 * t + h, :], ah[:, k, tok], al[:, k, tok],
                                        wh[u % SPL][:, 2 * k + h, :], wl[u % SPL][:, 2 * k + h, :],
                                        first and k == 0, last and k == 1)
                        if last and t == 0:
                            i.then_inc(row0_ready, 1)
                            r0r.up()
                    i.then_inc(unit_used, 1)
                    used.up()

                gate_up(0)
                n[0] += 2
                turn()
                gate_up(0)
                down(2, True, False)
                n[0] += 3
                turn()
                gate_up(0)
                down(2, False, False)
                n[0] += 3
                loops, rest = divmod(chunks - 3, 2)
                with looped(pe, loops, {lsp: 6, used: 6, acr: 4, atr: 2, asp: 2}):
                    for r in range(2):
                        turn()
                        gate_up(3 * r)
                        down(3 * r + 2, False, False)
                n[0] += 6 * loops
                for _ in range(rest):
                    turn()
                    gate_up(0)
                    down(2, False, False)
                    n[0] += 3
                turn()
                down(0, False, True)
                n[0] += 1


            ffn("ffn0", NFF)
            pe.wait_ge(ada_used, usedd.up(8))
            mod_cols(1, 0, 3)
            pe.wait_ge(xn_ready, xn.up())
            transposes(tv)
            pe.wait_ge(h_ready, hr.up(4))
            for c in range(6):
                if c == 1:
                    pe.wait_ge(ada_used, usedd.up(12))
                    pe.wait_ge(mod_taken, mtk.up())
                    mod_gate(1, 0, 4)
                    mod_cols(1, 1, 7)
                if c == 4:
                    pe.wait_ge(ada_used, usedd.up(4))
                    pe.wait_ge(mod_taken, mtk.up(2))
                    mod_gate(1, 1, 6)
                chunk("features")
            pe.wait_ge(h_ready, hr.up(2))
            pe.wait_ge(mod_taken, mtk.up())
            out_rows()
            pe.wait_ge(xn_ready, xn.up())
            transposes(tv)
            pe.wait_ge(h_ready, hr.up(4))
            ffn("ffn1", NFF)

            pe.wait_ge(x_ready, 4)
            pe.wait_ge(mem_loaded, 16)
            transposes(tv)
            pe.wait_ge(h_ready, hr.up(4))
            for l in range(DEPTH):
                if True:
                    pe.wait_ge(lin_evac, evac.up())
                pair = 2 * (lin[0] % 2)
                for q in range(2):
                    pe.wait_ge(l_split, lsp.up())
                    unit_features(n[0], pair, 2, UK * q, q == 0, q == 1)
                    for t in range(TT):
                        for k in range(UK):
                            tok = slice(t * P, (t + 1) * P)
                            u = n[0]
                            i = mm3(ps[:, pair + 1, t * S:(t + 1) * S], hh[:, UK * q + k, tok], hl[:, UK * q + k, tok],
                                    wh[u % SPL][:, k, 256:512], wl[u % SPL][:, k, 256:512],
                                    q == 0 and k == 0 and t == 0, q == 1 and k == UK - 1)
                    i.then_inc(unit_used, 1)
                    used.up()
                    n[0] += 1
                lin[0] += 1
            transposes(xs)
            pe.wait_ge(h_ready, hr.up(4))
            for kind, w in (("features", 512), ("features", 512), ("features", 512), ("rows", 512), ("rows", 256),
                            ("features", 512), ("features", 512)):
                chunk(kind, w)
            pe.wait_ge(lin_evac, lin[0])
            heads(MEM[0])

            dqr, kdr, exr = Count(dk_ready), Count(kd_ready), Count(exp_ready)
            levs, levt = Count(lev_scores), Count(lev_taken)
            for l in range(9):
                pe.wait_ge(dk_ready, dqr.up())
                if l:
                    pe.wait_ge(kd_ready, kdr.up())
                if l >= 2:
                    pe.wait_ge(lev_taken, levt.up())
                o = 4 * (l % 2)
                for h in range(HG):
                    if l < 8:
                        for t in range(TT):
                            tok = slice(t * P, (t + 1) * P)
                            c = (h % 2) * S + t * P
                            i = pe.matmul(ps[:, o + h // 2, c:c + P], kd[:, h, tok], qd[:, h, tok], start=True, stop=True)
                    else:
                        i = pe.matmul(ps[:, o + h // 4, (h % 4) * P:(h % 4 + 1) * P], kd[:, h, 0:P], qd[:, h, P:S],
                                      start=True, stop=True)
                i.then_inc(lev_scores, 1)
                levs.up()
            pe.wait_ge(lev_taken, levt.up(2))
            for h in range(HG):
                o = ps[:, 4 + h // 2, (h % 2) * S:(h % 2 + 1) * S]
                v0, v1 = (tv[:, t, h * P:(h + 1) * P] for t in range(TT))
                pe.matmul(o[:, 0:P], v0, scD[:, h, 0:P], start=True, stop=True, skip_group_check=True)
                pe.matmul(o[:, P:S], v0, scX[:, h, :], start=True, stop=False, skip_group_check=True)
                i = pe.matmul(o[:, P:S], v1, scD[:, h, P:S], start=False, stop=True, skip_group_check=True)
            i.then_inc(o_ready, 1)
            orr.up()
            exr.n = 10
            pe.wait_ge(exp_ready, exr.up())
            for a in range(3):
                i = pe.matmul(ps[:, 4 + a, :], ones[:, :], qd[:, 2 * a:2 * a + 2, :].rearrange("p a t -> p (a t)"), start=True, stop=True)
            i.then_inc(sq_sum, 1)
            sqs.up()
            pe.wait_ge(ol_ready, olr.up())
            out_rows()

            def after_norm(count):
                pe.wait_ge(x_ready, count)
                transposes(xs)
                pe.wait_ge(h_ready, hr.up(4))

            def router():
                pe.wait_ge(rw_low, rwlr.up())
                for t in range(TT):
                    tok = slice(t * P, (t + 1) * P)
                    for k in range(KT):
                        i = mm3(ps[:, 7, 20 * t:20 * t + 20], hh[:, k, tok], hl[:, k, tok], rwh[:, k, :], rwl[:, k, :],
                                k == 0, k == KT - 1)
                i.then_inc(router_sums, 1)
                rsum.up()

            rsum, rwlr = Count(router_sums), Count(rw_low)
            after_norm(5)
            router()
            ffn("moe0", NEXP)
            after_norm(6)
            for kind, w in (("features", 512), ("features", 256), ("rows", 512), ("rows", 256)):
                chunk(kind, w)
            for c in range(2):
                chunk("features")
            pe.wait_ge(lin_evac, lin[0])
            heads(MEM[1])

            rr, spr, ar = Count(rest_ready), Count(sp_ready), Count(a_ready)
            lar = Count(la_ready)
            for i in range(SBH // 2 + 2):
                if i < SBH // 2:
                    if i >= 2:
                        pe.wait_ge(la_ready, lar.up())
                    for a in range(2):
                        r, bank = slice(64 * a, 64 * a + 64), ps[:, 2 * (i % 2) + a, :]
                        q, k = FT[r, i, :], FT[r, 6 + i, :]
                        pe.matmul(bank[:, 0:S], k[:, 0:P], q[:, :], start=True, stop=False, skip_group_check=True)
                        j = pe.matmul(bank[:, S:S + P], k[:, P:S], q[:, P:S], start=False, stop=False, skip_group_check=True)
                    j.then_inc(s_ready, 1)
                    sr.up()
                if 0 <= i - 1 < SBH // 2:
                    pe.wait_ge(sp_ready, spr.up())
                    for a in range(2):
                        bank, nb = ps[:, 2 * ((i - 1) % 2) + a, :], sb_buf(i - 1)[:, a, :]
                        pe.matmul(bank[:, 0:S], ntri[:, :], nb[:, 0:S], start=False, stop=False, skip_group_check=True)
                        pe.matmul(bank[:, P:S], nones, nb[:, S:S + P], start=False, stop=False, skip_group_check=True)
                        j = pe.matmul(bank[:, S:S + P], ntri[:, :], nb[:, S:S + P], start=False, stop=True, skip_group_check=True)
                    j.then_inc(rest_ready, 1)
                    rr.up()
                if i >= 2:
                    w = i - 2
                    pe.wait_ge(a_ready, ar.up())
                    if w >= 2:
                        pe.wait_ge(ol_ready, olr.up())
                    for a in range(2):
                        h, nb = 2 * w + a, sb_buf(w)[:, a, :]
                        o = ps[64 * a:64 * a + 64, 4 + w % 2, 0:S]
                        pe.matmul(o, tv[:, 0, 64 * h:64 * h + 64], nb[:, 0:S], start=True, stop=False, skip_group_check=True)
                        j = pe.matmul(o[:, P:S], tv[:, 1, 64 * h:64 * h + 64], nb[:, S:S + P], start=False, stop=True,
                                      skip_group_check=True)
                    j.then_inc(o_ready, 1)
                    orr.up()
            pe.wait_ge(ol_ready, olr.up(2))
            out_rows()
            after_norm(7)
            router()
            ffn("moe1", NEXP)


_INS = ["x", "w_ada", "b_ada", "w_qkv", "w_o", "w_in", "w_out", "w_gate_up", "w_down", "mem_2", "a_w_in_2", "b_w_in_2",
        "w_kv_shared_2", "w_mem_kv_2", "w_o_2", "ln_mix_g_2", "ln_mix_b_2", "ln_ffn_g_2", "ln_ffn_b_2", "w_group_2",
        "b_group_2", "w_router_2", "b_router_2", "w_gate_2", "w_up_2", "w_down_2"]


def kernel(**inputs):
    import numpy as _np
    import concourse.bacc as _bacc
    from concourse import mybir as _mybir
    from concourse.bass_utils import run_bass_kernel_spmd as _run

    give = {name: _np.ascontiguousarray(inputs[name]) for name in _INS}
    give["cols"] = _np.ascontiguousarray(_np.concatenate(
        [_np.asarray(inputs[name]).reshape(-1, 128) for name in
         ("c", "norm_mix", "norm_ffn", "conv_w", "q_gain", "k_gain", "a_gnorm_2", "b_ada",
          "ln_mix_g_2", "ln_mix_b_2", "ln_ffn_g_2", "ln_ffn_b_2")]).T)
    i = _np.arange(128)
    give["k_ident"] = _np.eye(128, dtype=_np.float32)
    give["k_ones"] = _np.ones((128, 128), _np.float32)
    give["k_ntri"] = -(i[:, None] >= i[None, :]).astype(_np.float32)
    causal = _np.where(i[:, None] >= i[None, :], 0.0, -1e30).astype(_np.float32)
    give["k_causal"] = causal
    strict = (i[:, None] < i[None, :]).astype(_np.float32)
    give["k_strict"] = _np.concatenate([strict, _np.ones_like(strict), strict], axis=1)
    give["k_nstrict"] = ((give["k_strict"] - 1) * 1e30).astype(_np.float32)
    give["k_nones"] = -give["k_ones"]
    levels = [i[:, None] == i[None, :]]
    for m in (1, 2, 4, 8, 16, 32, 64):
        same = (i[:, None] // (2 * m)) == (i[None, :] // (2 * m))
        levels.append(same & ((i[:, None] // m) % 2 == 0) & ((i[None, :] // m) % 2 == 1))
    give["k_levels"] = _np.stack(levels, axis=1).reshape(128, 8 * 128).astype(_np.float32)

    nc = _bacc.Bacc("TRN2", target_bir_lowering=False, num_devices=1)
    arrays = {f"in_{name}": a for name, a in give.items()}
    A = {name: nc.dram_tensor(f"in_{name}", a.shape, _mybir.dt.from_np(a.dtype), kind="ExternalInput").ap()
         for name, a in give.items()}
    out = nc.dram_tensor("out_0", (1, S, D), _mybir.dt.float32, kind="ExternalOutput").ap()
    build(nc, A, out)
    r = _run(nc, [arrays], core_ids=[0])
    return r.results[0]["out_0"]
```
